# Optimizing a Trainium2 kernel written in Bass

```python
import math
import jax, jax.numpy as jnp
from jax import lax
import numpy as np

D_MODEL = 1024
BATCH = 1
SEQ = 256
DEPTH = 2

GRID_W = 64
CTX_LEN = 256
N_HEADS = 16
N_KV_HEADS = 4
HEAD_DIM = 64
GROUP = N_HEADS // N_KV_HEADS
ROPE_THETA = 10000.0
Q_BLOCK = 128
CONV_WIDTH = 3
SC_WIDTH = D_MODEL
DN_HEADS = 8
DN_DIM = 128
DN_CHUNK = 64
D_FF = 2816
N_BRANCH = 3
N_SUB = 3
EPS = 1e-6
ATT_Q = N_HEADS * HEAD_DIM
ATT_KV = N_KV_HEADS * HEAD_DIM
DN_W = DN_HEADS * DN_DIM
BRANCH_W = ATT_Q
SPLIT_SIZES = (ATT_Q, ATT_KV, ATT_KV, SC_WIDTH, SC_WIDTH, SC_WIDTH, 3 * DN_W, DN_W, DN_HEADS, DN_HEADS, DN_HEADS, DN_HEADS, N_BRANCH * D_MODEL)
D_IN_PROJ = ATT_Q + 2 * ATT_KV + 3 * SC_WIDTH + 4 * DN_W + 4 * DN_HEADS + N_BRANCH * D_MODEL

kernel_name = 'hybrid_dit_gqa_shortconv_gdn_macaron'

def _rmsnorm(x, g):
    xf = x.astype(jnp.float32)
    y = xf * lax.rsqrt(jnp.mean(xf * xf, axis=-1, keepdims=True) + EPS)
    return (y * g.astype(jnp.float32)).astype(x.dtype)

def _l2norm(x):
    return x * lax.rsqrt(jnp.sum(x * x, axis=-1, keepdims=True) + EPS)

def _adaln(cond, w, b):
    return (jax.nn.silu(cond) @ w + b).reshape(cond.shape[0], 3 * N_SUB, D_MODEL)

def _modulate(x, g, mod, j):
    return _rmsnorm(x, g) * (1 + mod[:, 3 * j + 1, None]) + mod[:, 3 * j, None]

def _ffn_half(h, mod, j, g, w1, w3, w2):
    u = _modulate(h, g, mod, j)
    return h + 0.5 * mod[:, 3 * j + 2, None] * ((jax.nn.silu(u @ w1) * (u @ w3)) @ w2)

def _split_cols(z):
    return jnp.split(z, [int(s) for s in np.cumsum(SPLIT_SIZES)[:-1]], axis=-1)

def _dwconv(x, w):
    p = w.shape[0] // 2
    return lax.conv_general_dilated(x, w[:, None, :].astype(x.dtype), window_strides=(1,), padding=[(p, p)],
                                    dimension_numbers=('NWC', 'WIO', 'NWC'), feature_group_count=x.shape[-1])

def _rope_2d(rows):
    row = jnp.repeat(jnp.arange(rows, dtype=jnp.float32), GRID_W)
    col = jnp.tile(jnp.arange(GRID_W, dtype=jnp.float32), rows)
    n_freq = HEAD_DIM // 4
    inv = ROPE_THETA ** (-jnp.arange(n_freq, dtype=jnp.float32) / n_freq)
    ang = jnp.concatenate([row[:, None] * inv, col[:, None] * inv], axis=-1)
    return jnp.cos(ang), jnp.sin(ang)

def _apply_rope(x, cos, sin):
    c = cos[None, :, None, :].astype(x.dtype)
    s = sin[None, :, None, :].astype(x.dtype)
    x1, x2 = jnp.split(x, 2, axis=-1)
    return jnp.concatenate([x1 * c - x2 * s, x1 * s + x2 * c], axis=-1)

def _att_qkv(p, q_norm_g, k_norm_g):
    B, T = p[0].shape[:2]
    q = _rmsnorm(p[0].reshape(B, T, N_HEADS, HEAD_DIM), q_norm_g)
    k = _rmsnorm(p[1].reshape(B, T, N_KV_HEADS, HEAD_DIM), k_norm_g)
    v = p[2].reshape(B, T, N_KV_HEADS, HEAD_DIM)
    return q, k, v

def _group(q):
    B, T = q.shape[:2]
    return q.reshape(B, T, N_KV_HEADS, GROUP, HEAD_DIM)

def _attend(q, k, v):
    s = jnp.einsum('bqhgd,bkhd->bhgqk', q * HEAD_DIM ** -0.5, k).astype(jnp.float32)
    p = jax.nn.softmax(s, axis=-1).astype(v.dtype)
    return jnp.einsum('bhgqk,bkhd->bqhgd', p, v)

def _attention_blocked(q, k, v):
    B, T = q.shape[:2]
    nb = T // Q_BLOCK
    qb = jnp.moveaxis(_group(q).reshape(B, nb, Q_BLOCK, N_KV_HEADS, GROUP, HEAD_DIM), 1, 0)
    ob = lax.map(lambda qi: _attend(qi, k, v), qb)
    return jnp.moveaxis(ob, 0, 1).reshape(B, T, ATT_Q)

def _short_conv(p, w):
    return p[3] * _dwconv(p[4] * p[5], w)

def _gated_delta_chunked(q, k, v, g, beta, s0):
    B, T, H, Dk = q.shape
    Dv = v.shape[-1]
    nc = T // DN_CHUNK

    def chunks(t):
        t = t.reshape((B, nc, DN_CHUNK, H) + t.shape[3:])
        return jnp.moveaxis(t, (1, 3), (0, 2))

    qc = chunks(q) * Dk ** -0.5
    kc, vc, bc = chunks(k), chunks(v), chunks(beta)
    gc = jnp.cumsum(chunks(g), axis=-1)
    idx = jnp.arange(DN_CHUNK)
    incl = idx[:, None] >= idx[None, :]
    strict = idx[:, None] > idx[None, :]
    diff = gc[..., :, None] - gc[..., None, :]
    decay_mat = jnp.where(incl, jnp.exp(jnp.where(incl, diff, 0.0)), 0.0)
    kb = kc * bc[..., None]
    a_mat = jnp.where(strict, jnp.einsum('nbhid,nbhjd->nbhij', kb, kc) * decay_mat, 0.0)
    rhs = jnp.concatenate([vc * bc[..., None], kb * jnp.exp(gc)[..., None]], axis=-1)
    sol = lax.linalg.triangular_solve(a_mat, rhs, left_side=True, lower=True, unit_diagonal=True)
    u, w = sol[..., :Dv], sol[..., Dv:]
    attn_intra = jnp.einsum('nbhid,nbhjd->nbhij', qc, kc) * decay_mat

    def step(s, inp):
        q_i, k_i, u_i, w_i, g_i, a_i = inp
        v_new = u_i - jnp.einsum('bhcd,bhde->bhce', w_i, s)
        o = jnp.einsum('bhcd,bhde->bhce', q_i * jnp.exp(g_i)[..., None], s) + jnp.einsum('bhij,bhje->bhie', a_i, v_new)
        g_last = g_i[..., -1:]
        s = s * jnp.exp(g_last)[..., None] + jnp.einsum('bhcd,bhce->bhde', k_i * jnp.exp(g_last - g_i)[..., None], v_new)
        return s, o

    s_fin, o = lax.scan(step, s0, (qc, kc, u, w, gc, attn_intra))
    return jnp.moveaxis(o, (0, 2), (1, 3)).reshape(B, T, H, Dv), s_fin

def _dn_inputs(p, dn_conv):
    y = jax.nn.silu(_dwconv(p[6], dn_conv)).astype(jnp.float32)
    B, T = y.shape[:2]
    q, k, v = [t.reshape(B, T, DN_HEADS, DN_DIM) for t in jnp.split(y, 3, axis=-1)]
    return (_l2norm(q), _l2norm(k), v) + tuple(t.astype(jnp.float32) for t in p[8:12])

def _dn_bidirectional(pl, pc, dn_a_log, dn_dt_bias):
    B = pl[0].shape[0]
    o_lat, o_ctx = None, None
    for d in range(2):
        def prep(p):
            g = -jnp.exp(dn_a_log[d].astype(jnp.float32)) * jax.nn.softplus(p[3 + d] + dn_dt_bias[d].astype(jnp.float32))
            beta = jax.nn.sigmoid(p[5 + d])
            ins = (p[0], p[1], p[2], g, beta)
            return tuple(jnp.flip(t, axis=1) for t in ins) if d == 1 else ins
        s0 = jnp.zeros((B, DN_HEADS, DN_DIM, DN_DIM), jnp.float32)
        oc, sc = _gated_delta_chunked(*prep(pc), s0)
        ol, _ = _gated_delta_chunked(*prep(pl), sc)
        if d == 1:
            oc, ol = jnp.flip(oc, axis=1), jnp.flip(ol, axis=1)
        o_lat = ol if o_lat is None else o_lat + ol
        o_ctx = oc if o_ctx is None else o_ctx + oc
    return o_lat, o_ctx

def _dn_output(o, gate, g):
    B, T = o.shape[:2]
    y = _rmsnorm(o, g) * jax.nn.silu(gate.astype(jnp.float32).reshape(B, T, DN_HEADS, DN_DIM))
    return y.reshape(B, T, DN_W).astype(gate.dtype)

def _merge(att, conv, dn, gz, w_br, w_out):
    gates = jax.nn.sigmoid(gz)
    m = (gates[..., :D_MODEL] * (att @ w_br[0])
         + gates[..., D_MODEL:2 * D_MODEL] * (conv @ w_br[1])
         + gates[..., 2 * D_MODEL:] * (dn @ w_br[2]))
    return m @ w_out

def _token_mixer(u, uc, cos, sin, w_in, b_in, q_norm_g, k_norm_g, sc_conv, dn_conv, dn_a_log, dn_dt_bias,
                 dn_norm_g, w_br, w_out, with_ctx_out):
    pl = _split_cols(u @ w_in + b_in)
    pc = _split_cols(uc @ w_in + b_in)
    ql, kl, vl = _att_qkv(pl, q_norm_g, k_norm_g)
    qc, kc, vc = _att_qkv(pc, q_norm_g, k_norm_g)
    ql, kl = _apply_rope(ql, cos, sin), _apply_rope(kl, cos, sin)
    k_all = jnp.concatenate([kc, kl], axis=1)
    v_all = jnp.concatenate([vc, vl], axis=1)
    att_l = _attention_blocked(ql, k_all, v_all)
    conv_l = _short_conv(pl, sc_conv)
    dn_l, dn_c = _dn_bidirectional(_dn_inputs(pl, dn_conv), _dn_inputs(pc, dn_conv), dn_a_log, dn_dt_bias)
    out_l = _merge(att_l, conv_l, _dn_output(dn_l, pl[7], dn_norm_g), pl[12], w_br, w_out)
    if not with_ctx_out:
        return out_l, None
    B, Lc = uc.shape[:2]
    att_c = _attend(_group(qc), kc, vc).reshape(B, Lc, ATT_Q)
    conv_c = _short_conv(pc, sc_conv)
    out_c = _merge(att_c, conv_c, _dn_output(dn_c, pc[7], dn_norm_g), pc[12], w_br, w_out)
    return out_l, out_c

def setup_inputs(seed: int = 0) -> dict:
    key = jax.random.key(seed)
    ks = jax.random.split(key, 24)
    f32 = jnp.float32
    D = D_MODEL

    def nrm(k, shape, scale):
        return jax.random.normal(k, shape, f32) * scale

    dt = jnp.exp(jax.random.uniform(ks[17], (DEPTH, 2, DN_HEADS), f32, math.log(1e-3), math.log(1e-1)))
    return {
        'x': nrm(ks[0], (BATCH, SEQ, D), 1.0),
        'c': nrm(ks[1], (BATCH, D), 1.0),
        'ctx': nrm(ks[2], (BATCH, CTX_LEN, D), 1.0),
        'c_ctx': nrm(ks[3], (D,), 1.0),
        'w_ada': nrm(ks[4], (DEPTH, D, 3 * N_SUB * D), 0.5 * D ** -0.5),
        'b_ada': nrm(ks[5], (DEPTH, 3 * N_SUB * D), 0.02),
        'norm_g': 1.0 + nrm(ks[6], (DEPTH, N_SUB, D), 0.05),
        'ffn_w1': nrm(ks[7], (DEPTH, 2, D, D_FF), D ** -0.5),
        'ffn_w3': nrm(ks[8], (DEPTH, 2, D, D_FF), D ** -0.5),
        'ffn_w2': nrm(ks[9], (DEPTH, 2, D_FF, D), D_FF ** -0.5),
        'w_in': nrm(ks[10], (DEPTH, D, D_IN_PROJ), D ** -0.5),
        'b_in': nrm(ks[11], (DEPTH, D_IN_PROJ), 0.02),
        'q_norm_g': 1.0 + nrm(ks[12], (DEPTH, HEAD_DIM), 0.05),
        'k_norm_g': 1.0 + nrm(ks[13], (DEPTH, HEAD_DIM), 0.05),
        'sc_conv': nrm(ks[14], (DEPTH, CONV_WIDTH, SC_WIDTH), CONV_WIDTH ** -0.5),
        'dn_conv': nrm(ks[15], (DEPTH, CONV_WIDTH, 3 * DN_W), CONV_WIDTH ** -0.5),
        'dn_a_log': jnp.log(jax.random.uniform(ks[16], (DEPTH, 2, DN_HEADS), f32, 1.0, 16.0)),
        'dn_dt_bias': dt + jnp.log(-jnp.expm1(-dt)),
        'dn_norm_g': 1.0 + nrm(ks[18], (DEPTH, DN_DIM), 0.05),
        'w_br': nrm(ks[19], (DEPTH, N_BRANCH, BRANCH_W, D), BRANCH_W ** -0.5),
        'w_out': nrm(ks[20], (DEPTH, D, D), D ** -0.5),
        'final_norm_g': 1.0 + nrm(ks[21], (D,), 0.05),
    }

def reference(x, c, ctx, c_ctx, w_ada, b_ada, norm_g, ffn_w1, ffn_w3, ffn_w2, w_in, b_in, q_norm_g, k_norm_g,
              sc_conv, dn_conv, dn_a_log, dn_dt_bias, dn_norm_g, w_br, w_out, final_norm_g):
    n = x.shape[1]
    rows = n // GRID_W
    cos, sin = _rope_2d(rows)
    h, hc = x, ctx
    c_ctx_b = c_ctx[None]
    for l in range(DEPTH):
        last = l == DEPTH - 1
        ml = _adaln(c, w_ada[l], b_ada[l])
        mc = _adaln(c_ctx_b, w_ada[l], b_ada[l])
        h = _ffn_half(h, ml, 0, norm_g[l, 0], ffn_w1[l, 0], ffn_w3[l, 0], ffn_w2[l, 0])
        hc = _ffn_half(hc, mc, 0, norm_g[l, 0], ffn_w1[l, 0], ffn_w3[l, 0], ffn_w2[l, 0])
        u = _modulate(h, norm_g[l, 1], ml, 1)
        uc = _modulate(hc, norm_g[l, 1], mc, 1)
        o, oc = _token_mixer(u, uc, cos, sin, w_in[l], b_in[l], q_norm_g[l], k_norm_g[l], sc_conv[l], dn_conv[l],
                             dn_a_log[l], dn_dt_bias[l], dn_norm_g[l], w_br[l], w_out[l], not last)
        h = h + ml[:, 5, None] * o
        h = _ffn_half(h, ml, 2, norm_g[l, 2], ffn_w1[l, 1], ffn_w3[l, 1], ffn_w2[l, 1])
        if not last:
            hc = hc + mc[:, 5, None] * oc
            hc = _ffn_half(hc, mc, 2, norm_g[l, 2], ffn_w1[l, 1], ffn_w3[l, 1], ffn_w2[l, 1])
    return _rmsnorm(h, final_norm_g)


_drawn_inputs = setup_inputs


def setup_inputs(seed=0):
    import zlib

    import numpy as np

    out = dict(_drawn_inputs(seed))
    spreads = {}
    factors = {'ctx': 2.742, 'b_in': 4.514, 'q_norm_g': 8.0, 'k_norm_g': 8.0, 'dn_norm_g': 7.252}
    for name, (base, spread) in spreads.items():
        noise = np.random.default_rng([zlib.crc32(name.encode()), seed]).standard_normal(out[name].shape)
        drawn = base * np.exp(spread * noise) if base else spread * noise
        out[name] = __import__('jax').numpy.asarray(drawn.astype(out[name].dtype))
    for name, factor in factors.items():
        out[name] = (out[name] * factor).astype(out[name].dtype)
    return out
```

```python
from contextlib import ExitStack, contextmanager

import numpy as np
import concourse.bass as bass
from concourse import mybir

D = 1024
KT = D // 128
SEQ, CTX = 256, 256
T = CTX + SEQ
TC = T // 128
DEPTH = 2
HD = 64
NH, NKV = 16, 4
DNH = 8
DFF = 2816
FT = DFF // 128
EPS = 1e-6
NEG = -1.0e30
PIECES = (8, 8, 6)
assert sum(PIECES) == FT

OQ, OK, OV = 0, 1024, 1280
O3, O4, O5 = 1536, 2560, 3584
ODN, OG, OAB, OGZ = 4608, 7680, 8704, 8736
D_IN = 11808

V_KV = 0
V_Q = 4
V_QG, V_KG = 12, 13
V_HEAD = 14
HV = 13
V_CONV = V_HEAD + DNH * HV
CV = 6
V_GZ = V_CONV + KT * CV
V_NG = V_GZ + 24
V_DNG = V_NG + 24
V_ADA = V_DNG + 1
NVL = V_ADA + 72
V_FG = 2 * NVL
V_C = V_FG + KT
NV = V_C + 2 * KT

C_ID, C_OFF, C_ONE, C_BLK, C_PERM = 0, 128, 256, 384, 512
C_LV = 640
C_NM = C_LV + 7 * 128
C_CUM = C_NM + 256
C_COS, C_SIN = C_CUM + 256, C_CUM + 512
C_SEL = C_CUM + 768
NC = C_SEL + 2

R_AB, R_DT, R_AL = 0, 32, 48
NR = 64

HB_G, HB_GC, HB_NEG, HB_BETA, HB_KD, HB_TOT = range(6)
HBN = 48

ADA_GROUPS = 18


def plan():
    at, blk, gblk = {}, 0, 0

    def take(key, nblocks, gemm=True):
        nonlocal blk, gblk
        at[key] = (blk, gblk)
        blk += nblocks
        gblk += nblocks if gemm else 0

    groups = 0
    at["groups"] = {}

    def ada(key, n):
        nonlocal groups
        at["groups"][key] = (groups, n)
        groups += n
        take(key, n, False)

    for l in range(DEPTH):
        if l == 0:
            ada(("ada", 0), 6)
        for f in range(2):
            for p, tiles in enumerate(PIECES):
                n = tiles // 2
                rides = n if (f == 0 or (l == 0 and p == 0)) else 0
                at[("rides", l, f, p)] = (groups, rides)
                groups += rides
                at[("up", l, f, p)] = (blk, gblk)
                blk += n + rides
                gblk += n
                take(("down", l, f, p), 2)
            if f == 0:
                ada(("ada1", l), 1)
                take(("head", l), DNH)
                take(("br", l, 0), 4)
                take(("kv", l), 1)
                take(("q", l), 2)
                take(("br", l, 1), 4)
                take(("conv", l), 6)
                take(("br", l, 2), 4)
                take(("out", l), 2)
            elif l == 0:
                ada(("ada2", l), 2)
    assert groups == DEPTH * ADA_GROUPS
    at["blocks"], at["gblocks"] = blk, gblk
    return at


def build(nc, stream, h_in, vecs_in, rows_in, wab_in, consts_in, out):
    f32, f32r = mybir.dt.float32, mybir.dt.float32r
    ALU, ACT, AX = mybir.AluOpType, mybir.ActivationFunctionType, mybir.AxisListType
    ds = bass.ds
    P = plan()
    NB = P["blocks"]

    ctx = ExitStack()
    with ctx:
        def sb(name, shape, dt=f32):
            return ctx.enter_context(nc.sbuf_tensor(name, shape, dt))

        def sem(name):
            return ctx.enter_context(nc.semaphore(name))

        raw = sb("raw", [128, 4, 1024])
        whi = sb("whi", [128, 4, 1024], f32r)
        wlo = sb("wlo", [128, 4, 1024], f32r)
        h = sb("h", [128, KT, T])
        uh = sb("uh", [128, KT, T], f32r)
        ul = sb("ul", [128, KT, T], f32r)
        bh = sb("bh", [128, KT, T], f32r)
        bl = sb("bl", [128, KT, T], f32r)
        m = sb("m", [128, KT * T])
        cst = sb("cst", [128, NC])
        vec = sb("vec", [128, NV])
        rows = sb("row_vectors", [128, DEPTH, NR])
        wab = sb("wab_raw", [128, DEPTH, KT * 32])
        idr = sb("idr", [128, 128], f32r)
        nidr = sb("nidr", [128, 128], f32r)
        cstat = sb("cstat", [128, KT, 128], f32r)
        csil = sb("csil", [128, KT, 2])
        mod = sb("mod", [128, DEPTH * 72, 2])
        normA = sb("normA", [128, KT, 2])
        hgate = sb("hgate", [128, KT, 2])
        tab = sb("tab", [128, DNH, HBN])
        hv = sb("hv", [128, HV])
        hb = sb("hb", [128, HBN])
        stat = sb("stat", [128, 32])
        scr = sb("scr", [128, 6160])
        scr_r = sb("scr_r", [128, 4, 2 * 512], f32r)
        bank = [ctx.enter_context(nc.psum_tensor(f"bank{i}", [128, 512], f32)) for i in range(8)]

        m3 = m[:, :].rearrange("p (k t) -> p k t", k=KT)
        ident = cst[:, C_ID:C_ID + 128]
        ones = cst[:, C_ONE:C_ONE + 128]

        def s_(a, n):
            return scr[:, a:a + n]

        nsq = s_(0, 1024).rearrange("p (a t) -> p a t", a=2)
        nvar, nrs = s_(1024, 512), s_(1536, 512)
        nut = s_(2048, 1024).rearrange("p (a t) -> p a t", a=2)
        sil = s_(3072, 1024).rearrange("p (a t) -> p a t", a=2)
        hbuf = s_(4096, 1024).rearrange("p (a t) -> p a t", a=2)
        arow = scr[0:4, 5120:5632]
        SM = s_(5120, 1024)

        pre = s_(0, 3 * 516).rearrange("p (j s t) -> p j s t", j=3, s=2)
        eg = s_(0, 1024).rearrange("p (d t) -> p d t", d=2)
        qkv = s_(1548, 1536).rearrange("p (j t) -> p j t", j=3)
        gate = s_(3084, 512)
        ktok = s_(3596, 512)
        vtok = s_(4108, 512)
        Gs = s_(4620, 512)
        KQs = s_(5132, 512)
        St = s_(5644, 512).rearrange("p (b d e) -> p b d e", b=2, d=2)
        Rr = s_(4620, 256).rearrange("p (d e) -> p d e", d=2)
        vn = s_(4876, 256).rearrange("p (d e) -> p d e", d=2)
        vd = s_(5132, 256).rearrange("p (d e) -> p d e", d=2)
        hsq = s_(4620, 1024).rearrange("p (d t) -> p d t", d=2)
        hrs = s_(0, 1024).rearrange("p (d t) -> p d t", d=2)
        DT = m[:, 0:1024].rearrange("p (d t) -> p d t", d=2)
        Qt = m[:, 1024:2048].rearrange("p (d t) -> p d t", d=2)
        AT = m[:, 2048:3072].rearrange("p (d t) -> p d t", d=2)
        IT = m[:, 3072:4096].rearrange("p (d t) -> p d t", d=2)
        XTf = DT
        ATr, X, XT, Pm = (scr_r[:, k, :].rearrange("p (d t) -> p d t", d=2) for k in range(4))
        wabh, wabl = scr_r[:, 0, 0:256], scr_r[:, 0, 256:512]

        kT = s_(0, 1024).rearrange("p (a t) -> p a t", a=2)
        vt = s_(1024, 1024).rearrange("p (a c f) -> p a c f", a=2, c=TC)
        qx = s_(2048, 2048).rearrange("p (a t) -> p a t", a=4)
        asq, ars = s_(4096, 512), s_(4608, 512)
        asw, ax = s_(5120, 512), s_(5632, 512)
        Pb = s_(4096, 1024).rearrange("p (a t) -> p a t", a=2)
        PT = s_(5120, 1024).rearrange("p (a t) -> p a t", a=2)
        c4 = s_(0, 512)
        cpr = s_(512, 516).rearrange("p (s t) -> p s t", s=2)
        cy = s_(1028, 512)
        cz = s_(1540, 1024).rearrange("p (a t) -> p a t", a=2)
        cvec = s_(2600, 4 * CV)

        raw_in = [sem("raw_in0"), sem("raw_in1")]
        hi_ready, lo_ready, panel_done = sem("hi_ready"), sem("lo_ready"), sem("panel_done")
        pair_done = [sem("pair_done0"), sem("pair_done1")]
        consts_loaded, vecs_loaded, h_loaded, wab_loaded = (sem(n) for n in (
            "consts_loaded", "vecs_loaded", "h_loaded", "wab_loaded"))
        setup_act, setup_dve = sem("setup_act"), sem("setup_dve")
        ada_row, ada_turned, mod_ready = (sem(n) for n in ("ada_row", "ada_turned", "mod_ready"))
        sq_ready, sq_used, var_ready, rstd_ready, ut_ready, uh_ready, u_ready = (sem(n) for n in (
            "sq_ready", "sq_used", "var_ready", "rstd_ready", "ut_ready", "uh_ready", "u_ready"))
        sil_ready, hid_hi, hid_ready = sem("sil_ready"), sem("hid_hi"), sem("hid_ready")
        wab_hi, wab_lo = sem("wab_hi"), sem("wab_lo")
        ab_sum, ab_z, ab_exp, g_ready, gc_sum, gc_exp, tab_ready = (sem(n) for n in (
            "ab_sum", "ab_z", "ab_exp", "g_ready", "gc_sum", "gc_exp", "tab_ready"))
        E = {n: sem(n) for n in (
            "hv_ready", "pre_ready", "conv_ready", "silu_ready", "hsq_ready", "l2_sum", "l2_var", "l2_rstd",
            "kn_ready", "qn_ready", "kv_turned", "ktok_ready", "vtok_ready", "gram", "kq_ready",
            "gs_ready", "gc_row", "dm_ready", "dt_ready", "eg_ready", "qt_ready", "at_ready", "atr_ready", "it_ready",
            "xt0_ready", "xt0_turned", "x0_ready", "p_sum", "pm_ready", "x_sum", "x_ready", "xt_ready",
            "ks_sum", "r_ready", "y_sum", "vn_ready", "vd_ready", "ds_sum", "s_ready", "o_sum", "osq_ready",
            "on_sum", "on_var", "on_rstd", "on_ready", "bh_ready", "head_ready")}
        dve_step, act_step = sem("dve_step"), sem("act_step")
        A = {n: sem(n) for n in (
            "a_x", "a_sq", "a_sum", "a_var", "a_rstd", "a_norm", "a_swap", "a_done", "a_vx", "a_vturn", "a_vtok",
            "s_sum", "s_max", "s_exp", "s_scaled", "s_turned", "s_pt", "s_pv", "att_hi", "att_ready")}
        C = {n: sem(n) for n in ("c_vec", "c_p4", "c_out", "c_hi", "c_ready", "br_gate", "mh_ready", "mx_ready")}
        out_ready, out_stored = sem("out_ready"), sem("out_stored")

        block = ctx.enter_context(nc.Block())

        class Steps:

            def __init__(self, eng, s):
                self.eng, self.s, self.base, self.k = eng, s, 0, 0

            def do(self, ins):
                ins.then_inc(self.s, 1)
                self.k += 1

            def sync(self):
                self.eng.wait_ge(self.s, self.base + self.k)

            @contextmanager
            def loop(self, start, stop, per):
                base, self.k = self.base + self.k, 0
                with self.eng.Fori(start, stop) as i:
                    self.base = base + (i - start) * per
                    yield i
                    assert self.k == per, (self.k, per)
                self.base, self.k = base + (stop - start) * per, 0

        def wait(eng, s, n):
            if not (isinstance(n, int) and n <= 0):
                eng.wait_ge(s, n)

        def have(eng, s, n):
            eng.wait_ge(s, n + 1)

        def conds(c0):
            return [(k, a, b) for k, a, b in ((0, 0, CTX), (1, CTX, T)) if a >= c0]

        def bc(ap, n, w):
            return ap.rearrange("p (a w) -> p a w", a=1).broadcast_to([128, n, w])

        def c4d(ap):
            return ap.rearrange("p (c t) -> p c t", c=TC)

        def modc(l, jj):
            return l * 72 + jj * 8

        def chunk(d, s):
            return (0, 1, 2, 3)[s] if d == 0 else (1, 0, 3, 2)[s]

        def hcol(kind, d, c):
            n = (kind * 2 + d) * 4 + c
            return slice(n, n + 1)

        def att_units(l):
            kinds = ((2, 3) if l == DEPTH - 1 else (0, 2, 3))
            return [(j, a, k) for j in range(4) for a in range(2) for k in kinds]

        def att_units_before(l, p):
            return sum(2 * len(att_units(k)) for k in range(l)) + p * len(att_units(l))

        @block.sync
        def _(sp):
            sp.dma_start(cst[:, :], consts_in).then_inc(consts_loaded, 16)
            sp.dma_start(vec[:, :], vecs_in).then_inc(vecs_loaded, 16)

            def load(b, r):
                sp.dma_start(raw[:, 2 * r:2 * r + 2, :],
                             stream[ds(4 * b + 2 * r, 2), :, :].rearrange("g p n -> p g n")).then_inc(raw_in[r], 16)

            load(0, 0)
            load(0, 1)
            sp.dma_start(h[:, :, :], h_in.rearrange("(k p) t -> p k t", p=128)).then_inc(h_loaded, 16)
            sp.dma_start(wab[:, :, :].rearrange("p l n -> p (l n)"), wab_in).then_inc(wab_loaded, 16)
            sp.dma_start(rows[:, :, :].rearrange("p l n -> p (l n)"), rows_in).then_inc(wab_loaded, 16)
            with sp.Fori(1, NB) as b:
                for r in range(2):
                    sp.wait_ge(lo_ready, 4 * (b - 1) + 2 * r + 2)
                    load(b, r)
            for t in range(KT):
                sp.wait_ge(out_ready, t + 1)
                sp.dma_start(out.rearrange("(k p) t -> p k t", p=128)[:, t, :], m3[:, t, 0:SEQ]).then_inc(out_stored, 16)
            sp.wait_ge(out_stored, 16 * KT)

        @block.scalar
        def _(act):
            steps = Steps(act, act_step)

            def split(B, j):
                if isinstance(B, int) and B >= NB:
                    return
                if j % 2 == 0:
                    act.wait_ge(raw_in[j // 2], 16 * (B + 1))
                if not (isinstance(B, int) and B == 0):
                    act.wait_ge(panel_done, 4 * (B - 1) + j + 1)
                act.activation(whi[:, j, :], raw[:, j, :], ACT.Copy).then_inc(hi_ready, 1)

            def log_exp():
                act.preload_act_table_set("natural_log_exp_and_others")

            def rsqrt(out_, in_, ready):
                steps.do(act.activation(out_, in_, ACT.Ln))
                steps.sync()
                act.activation(out_, out_, ACT.Exp, scale=-0.5).then_inc(ready, 1)

            act.sem_inc(ada_row, 1)
            act.wait_ge(consts_loaded, 16)
            act.activation(idr[:, :], ident, ACT.Copy)
            act.activation(nidr[:, :], ident, ACT.Copy, scale=-1.0).then_inc(setup_act, 1)
            act.wait_ge(vecs_loaded, 16)
            steps.do(act.activation(csil[:, :, :], vec[:, V_C:V_C + 16].rearrange("p (k c) -> p k c", c=2), ACT.Silu))
            steps.sync()
            act.wait_ge(setup_dve, 1)
            act.activation(cstat[:, :, 0:2], csil[:, :, :], ACT.Copy).then_inc(setup_act, 1)
            for j in range(4):
                split(0, j)

            def ada_panels(B):
                for j in range(4):
                    split(B + 1, j)

            def ada_evac(n, B):
                act.wait_ge(panel_done, 4 * B + 4)
                have(act, ada_turned, n)
                act.activation(arow[:, :], bank[4][0:4, :], ACT.Copy).then_inc(ada_row, 1)

            def ada_only(key):
                B0, _ = P[key]
                g0, n = P["groups"][key]
                with act.Fori(0, n) as i:
                    ada_panels(B0 + i)
                    ada_evac(g0 + i, B0 + i)

            def norm(n, l, j, c0, hcount):
                hcount(act)
                for t in range(KT):
                    wait(act, sq_used, 8 * n + t - 1)
                    act.activation(nsq[:, t % 2, c0:T], h[:, t, c0:T], ACT.Square).then_inc(sq_ready, 1)
                log_exp()
                act.wait_ge(var_ready, n + 1)
                rsqrt(nrs[:, c0:T], nvar[:, c0:T], rstd_ready)
                if j is None:
                    return
                sh = modc(l, 3 * j)
                for t in range(KT):
                    act.wait_ge(ut_ready, 8 * n + t + 1)
                    for k, a, b in conds(c0):
                        last = act.activation(uh[:, t, a:b], nut[:, t % 2, a:b], ACT.Identity,
                                              bias=mod[:, sh + t, k:k + 1])
                    last.then_inc(uh_ready, 1)

            def ffn(l, f):
                c0 = CTX if l == DEPTH - 1 and f == 1 else 0
                occ = 2 * l + f
                tile0 = occ * FT
                for p, tiles in enumerate(PIECES):
                    B0, G0 = P[("up", l, f, p)]
                    g0, rides = P[("rides", l, f, p)]
                    per = 2 if rides else 1
                    act.wait_ge(panel_done, 4 * B0)
                    with act.Fori(0, tiles // 2) as i:
                        B, G, n0 = B0 + per * i, G0 + i, tile0 + 2 * i
                        if rides:
                            ada_panels(B)
                            ada_evac(g0 + i, B)
                            B = B + 1
                        for k in range(2):
                            split(B + 1, 2 * k)
                            act.wait_ge(panel_done, 4 * B + 2 * k + 1)
                            have(act, pair_done[k], G)
                            act.activation(sil[:, k, c0:T], bank[2 * k][:, c0:T], ACT.Silu).then_inc(sil_ready, 1)
                            split(B + 1, 2 * k + 1)
                            have(act, pair_done[k], G + 1)
                            act.activation(bh[:, ds(2 * i + k, 1), c0:T].rearrange("p a t -> p (a t)"), hbuf[:, k, c0:T],
                                           ACT.Copy).then_inc(hid_hi, 1)
                    tile0 += tiles
                    B0, _ = P[("down", l, f, p)]
                    if B0 + 2 < NB:
                        with act.Fori(0, 2) as i:
                            for j in range(4):
                                split(B0 + i + 1, j)
                    else:
                        for j in range(4):
                            split(B0 + 1, j)

            def ab(l):
                act.wait_ge(wab_loaded, 32)
                act.activation(wabh, wab[:, l, :], ACT.Copy).then_inc(wab_hi, 1)
                act.wait_ge(ab_z, 2 * l + 1)
                act.activation(SM[:, 128:192], SM[:, 64:128], ACT.Exp)
                act.activation(SM[:, 192:256], SM[:, 960:1024], ACT.Exp, scale=-1.0)
                steps.do(act.activation(SM[:, 256:272], rows[:, l, R_AL:R_AL + 16], ACT.Exp))
                steps.sync()
                act.activation(SM[:, 320:384], SM[:, 128:192], ACT.Ln, bias=1.0).then_inc(ab_exp, 1)
                act.wait_ge(ab_z, 2 * l + 2)
                act.activation(SM[:, 640:704], SM[:, 448:512], ACT.Exp)
                act.activation(SM[:, 704:768], SM[:, 512:576], ACT.Exp)
                act.activation(SM[:, 768:832], SM[:, 576:640], ACT.Exp).then_inc(ab_exp, 1)

            def head(l, b, gemm, gdn):
                B0, G0 = P[("head", l)]
                c0 = CTX if l == DEPTH - 1 else 0
                s0 = c0 // CTX
                B = B0 + b

                def sp(j):
                    if gemm:
                        split(B + 1, j)

                if not gdn:
                    for j in range(4):
                        sp(j)
                    return
                o = l * DNH + b - 1
                act.wait_ge(E["hv_ready"], o + 1)
                act.wait_ge(panel_done, 4 * B)
                seg = lambda ap: ap.rearrange("p (s t) -> p s t", s=2)
                for j in (1, 0, 2):
                    a = s0 if j == 0 else 0
                    act.activation(pre[:, j, a:2, 1:257], seg(bank[j][:, :])[:, a:2, :], ACT.Identity,
                                   bias=hv[:, j:j + 1]).then_inc(pair_done[0] if j == 0 else E["pre_ready"], 1)
                act.activation(gate[:, c0:T], bank[3][:, c0:T], ACT.Silu, bias=hv[:, 3:4]).then_inc(pair_done[1], 1)
                for n, j in enumerate((1, 0, 2)):
                    a = c0 if j == 0 else 0
                    act.wait_ge(E["conv_ready"], 3 * o + n + 1)
                    act.activation(qkv[:, j, a:T], qkv[:, j, a:T], ACT.Silu).then_inc(E["silu_ready"], 1)
                    if j != 2:
                        act.wait_ge(E["silu_ready"], 3 * o + n + 1)
                        act.activation(hsq[:, n, a:T], qkv[:, j, a:T], ACT.Square).then_inc(E["hsq_ready"], 1)
                sp(0)
                for n, j in enumerate((1, 0)):
                    a = c0 if j == 0 else 0
                    log_exp()
                    act.wait_ge(E["l2_var"], 2 * o + n + 1)
                    rsqrt(hrs[:, n, a:T], hrs[:, n, a:T], E["l2_rstd"])
                act.wait_ge(E["kv_turned"], 2 * o + 2)
                act.activation(ktok, bank[6][:, :], ACT.Copy).then_inc(E["ktok_ready"], 1)
                act.wait_ge(E["gram"], 2 * o + 2)
                act.activation(KQs[:, c0:T], bank[5][:, c0:T], ACT.Copy).then_inc(E["kq_ready"], 1)
                for d in range(2):
                    act.wait_ge(E["dm_ready"], 2 * o + d + 1)
                    act.activation(eg[:, d, c0:T], bank[6 + d][:, c0:T], ACT.Exp).then_inc(E["eg_ready"], 1)
                    act.activation(DT[:, d, :], DT[:, d, :], ACT.Exp).then_inc(E["dt_ready"], 1)
                for d in range(2):
                    act.wait_ge(E["at_ready"], 2 * o + d + 1)
                    act.activation(ATr[:, d, :], AT[:, d, :], ACT.Copy).then_inc(E["atr_ready"], 1)
                for d in range(2):
                    act.wait_ge(E["xt0_turned"], 2 * o + d + 1)
                    act.activation(X[:, d, :], bank[4 + d][:, :], ACT.Copy).then_inc(E["x_ready"], 1)
                sp(1)
                for v in range(1, 7):
                    for d in range(2):
                        n = 12 * o + 2 * (v - 1) + d + 1
                        act.wait_ge(E["x_sum"], n)
                        act.activation(X[:, d, :], bank[6 + d][:, :], ACT.Copy).then_inc(E["x_ready"], 1)
                        if v < 6:
                            act.activation(XT[:, d, :], bank[4 + d][:, :], ACT.Copy).then_inc(E["xt_ready"], 1)
                sp(2)
                for d in range(2):
                    act.wait_ge(E["p_sum"], 18 * o + 12 + d + 1)
                    act.activation(XT[:, d, :], bank[4 + d][:, :], ACT.Copy).then_inc(E["xt_ready"], 1)
                for d in range(2):
                    act.wait_ge(E["p_sum"], 18 * o + 14 + d + 1)
                    act.activation(Pm[:, d, :], bank[6 + d][:, :], ACT.Copy).then_inc(E["pm_ready"], 1)
                for s in range(TC - 1):
                    for d in range(2):
                        c = chunk(d, s)
                        act.wait_ge(E["vn_ready"], 8 * o + 2 * s + d + 1)
                        act.activation(vd[:, d, :], vn[:, d, :], ACT.Copy,
                                       scale=hb[:, hcol(HB_KD, d, c)]).then_inc(E["vd_ready"], 1)
                act.wait_ge(E["o_sum"], o + 1)
                act.activation(eg[:, 0, c0:T], bank[6][:, c0:T], ACT.Square).then_inc(E["osq_ready"], 1)
                log_exp()
                act.wait_ge(E["on_var"], o + 1)
                rsqrt(eg[:, 1, c0:T], eg[:, 1, c0:T], E["on_rstd"])
                sp(3)
                act.wait_ge(E["on_ready"], o + 1)
                act.activation(bh[:, ds(b - 1, 1), c0:T].rearrange("p a t -> p (a t)"), gate[:, c0:T],
                               ACT.Copy).then_inc(E["bh_ready"], 1)

            def heads(l):
                act.wait_ge(panel_done, 4 * P[("head", l)][0])
                act.wait_ge(tab_ready, l + 1)
                head(l, 0, True, False)
                with steps.loop(1, DNH, 3) as b:
                    head(l, b, True, True)
                head(l, DNH, False, True)

            def branch(l, r):
                B0, G0 = P[("br", l, r)]
                c0 = CTX if l == DEPTH - 1 else 0
                n0 = (3 * l + r) * 8
                with act.Fori(0, 4) as i:
                    for k in range(2):
                        split(B0 + i + 1, 2 * k)
                        act.wait_ge(panel_done, 4 * (B0 + i) + 2 * k + 1)
                        have(act, pair_done[k], G0 + i)
                        act.activation(sil[:, k, c0:T], bank[2 * k][:, c0:T], ACT.Sigmoid,
                                       bias=vec[:, ds(l * NVL + V_GZ + 8 * r + 2 * i + k, 1)]).then_inc(C["br_gate"], 1)
                        split(B0 + i + 1, 2 * k + 1)

            def qk_norm(na, j, bcol, c0):
                act.activation(ax[:, c0:T], bank[j][:, c0:T], ACT.Identity, bias=vec[:, bcol:bcol + 1]).then_inc(A["a_x"], 1)
                act.wait_ge(A["a_x"], na + 1)
                act.activation(asq[:, c0:T], ax[:, c0:T], ACT.Square).then_inc(A["a_sq"], 1)
                log_exp()
                act.wait_ge(A["a_var"], na + 1)
                rsqrt(ars[:, c0:T], ars[:, c0:T], A["a_rstd"])

            def attention(l):
                c0 = CTX if l == DEPTH - 1 else 0
                B0, G0 = P[("kv", l)]
                L = l * NVL
                na = 10 * l
                for j in range(4):
                    split(B0 + 1, j)
                act.wait_ge(panel_done, 4 * B0 + 4)
                for j in range(2):
                    wait(act, A["a_done"], na)
                    qk_norm(na, j, L + V_KV + j, 0)
                    na += 1
                for j in range(2):
                    n = 2 * l + j
                    if j:
                        act.wait_ge(A["a_vturn"], n)
                    else:
                        act.wait_ge(A["a_done"], na)
                    act.activation(ax, bank[2 + j][:, :], ACT.Identity, bias=vec[:, L + V_KV + 2 + j:L + V_KV + 3 + j]).then_inc(A["a_vx"], 1)
                act.wait_ge(A["a_vturn"], 2 * l + 2)
                nu = att_units_before(l, 0)
                for p in range(2):
                    B, G = P[("q", l)][0] + p, P[("q", l)][1] + p
                    for j in range(4):
                        split(B + 1, j)
                        wait(act, A["a_done"], na)
                        qk_norm(na, j, L + V_Q + 4 * p + j, c0)
                        na += 1
                    act.wait_ge(A["a_done"], na)
                    units = att_units(l)

                    def evac_pt(u):
                        act.wait_ge(A["s_turned"], nu + u + 1)
                        act.activation(PT[:, u % 2, :], bank[6 + u % 2][:, :], ACT.Copy).then_inc(A["s_pt"], 1)

                    for u, (j, a, lat) in enumerate(units):
                        act.wait_ge(A["s_max"], nu + u + 1)
                        if u >= 2:
                            act.wait_ge(A["s_turned"], nu + u - 1)
                        for q in range(1 if lat else 2):
                            w = 512 if lat else 256
                            st = 8 * (u % 2) + q
                            last = act.activation(Pb[:, u % 2, q * w:(q + 1) * w], bank[4 + u % 2][:, q * w:(q + 1) * w], ACT.Exp,
                                                  scale=HD ** -0.5, bias=stat[:, st + 2:st + 3], accum_out=stat[:, st + 4:st + 5])
                        last.then_inc(A["s_exp"], 1)
                        if u:
                            evac_pt(u - 1)
                    evac_pt(len(units) - 1)
                    nu += len(units)
                    for j in range(4):
                        act.wait_ge(A["s_pv"], nu)
                        act.activation(bh[:, 4 * p + j, c0:T], bank[j][:, c0:T], ACT.Copy).then_inc(A["att_hi"], 1)

            def conv(l):
                B0, G0 = P[("conv", l)]
                c0 = CTX if l == DEPTH - 1 else 0
                with steps.loop(0, 2, 0) as i:
                    B = B0 + 3 * i
                    n0 = 8 * l + 4 * i
                    for t in range(4):
                        q = 3 * t
                        split(B + q // 4 + 1, q % 4)
                        act.wait_ge(panel_done, 4 * B + q + 1)
                        act.wait_ge(C["c_vec"], 2 * l + i + 1)
                        have(act, C["c_out"], n0 + t)
                        act.activation(c4[:, c0:T], bank[q % 4][:, c0:T], ACT.Identity,
                                       bias=cvec[:, t * CV:t * CV + 1]).then_inc(C["c_p4"], 1)
                        split(B + (q + 1) // 4 + 1, (q + 1) % 4)
                        split(B + (q + 2) // 4 + 1, (q + 2) % 4)
                        have(act, C["c_out"], n0 + t + 1)
                        act.activation(bh[:, ds(4 * i + t, 1), c0:T].rearrange("p a t -> p (a t)"), cz[:, t % 2, c0:T],
                                       ACT.Copy).then_inc(C["c_hi"], 1)

            def project_out(l):
                B0, G0 = P[("out", l)]
                c0 = CTX if l == DEPTH - 1 else 0
                act.wait_ge(panel_done, 4 * B0)
                have(act, pair_done[1], G0)
                for t in range(KT):
                    act.activation(uh[:, t, c0:T], m3[:, t, c0:T], ACT.Copy).then_inc(C["mh_ready"], 1)
                with act.Fori(0, 2) as i:
                    for j in range(4):
                        split(B0 + i + 1, j)

            ada_only(("ada", 0))
            n = 0
            for l in range(DEPTH):
                c_last = CTX if l == DEPTH - 1 else 0
                norm(n, l, 0, 0, (lambda e: e.wait_ge(h_loaded, 16)) if l == 0 else (lambda e: have(e, pair_done[1], P[("down", 0, 1, 2)][1] + 2)))
                ffn(l, 0)
                ada_only(("ada1", l))
                norm(n + 1, l, 1, 0, lambda e: have(e, pair_done[1], P[("down", l, 0, 2)][1] + 2))
                ab(l)
                heads(l)
                branch(l, 0)
                attention(l)
                branch(l, 1)
                conv(l)
                branch(l, 2)
                project_out(l)
                norm(n + 2, l, 2, c_last, lambda e: have(e, pair_done[1], P[("out", l)][1] + 2))
                ffn(l, 1)
                if l == 0:
                    ada_only(("ada2", 0))
                n += 3
            norm(n, None, None, CTX, lambda e: have(e, pair_done[1], P["gblocks"]))

        @block.vector
        def _(dve):
            steps = Steps(dve, dve_step)
            stt = dve.scalar_tensor_tensor

            def split(B, j):
                if isinstance(B, int) and B >= NB:
                    return
                dve.wait_ge(hi_ready, 4 * B + j + 1)
                dve.tensor_tensor(wlo[:, j, :], raw[:, j, :], whi[:, j, :].bitcast(f32), ALU.subtract).then_inc(lo_ready, 1)

            for s in (*pair_done, mod_ready, E["head_ready"], C["c_out"]):
                dve.sem_inc(s, 1)
            dve.memset(cstat[:, :, :].bitcast(f32), 0.0).then_inc(setup_dve, 1)
            dve.wait_ge(setup_act, 2)
            dve.wait_ge(setup_dve, 1)
            dve.tensor_tensor(cstat[:, :, 2:4], csil[:, :, :], cstat[:, :, 0:2].bitcast(f32), ALU.subtract).then_inc(setup_dve, 1)
            for j in range(4):
                split(0, j)

            def ada_panels(B):
                for j in range(4):
                    split(B + 1, j)

            def ada_mod(g, l, local):
                have(dve, ada_turned, g + 1)
                b0 = l * NVL + V_ADA + 4 * local
                bias = vec[:, ds(b0, 4)].rearrange("p (a b) -> p a b", b=1).broadcast_to([128, 4, 2])
                dve.tensor_tensor(mod[:, ds(4 * g, 4), :], bank[5][:, 0:8].rearrange("p (a b) -> p a b", b=2), bias,
                                  ALU.add).then_inc(mod_ready, 1)

            def ada_only(key):
                B0, _ = P[key]
                g0, n = P["groups"][key]
                with dve.Fori(0, n) as i:
                    ada_panels(B0 + i)
                    ada_mod(g0 + i, g0 // ADA_GROUPS, (g0 % ADA_GROUPS) + i)

            def norm(n, l, j, c0):
                if j is not None:
                    have(dve, mod_ready, ADA_GROUPS * l + 6 * (j + 1))
                    sc = modc(l, 3 * j + 1)
                    g = vec[:, l * NVL + V_NG + 8 * j:l * NVL + V_NG + 8 * j + 8]
                    g = g.rearrange("p (a b) -> p a b", b=1).broadcast_to([128, KT, 2])
                    stt(out=normA[:, :, :], in0=mod[:, sc:sc + 8, :], scalar=1.0, in1=g, op0=ALU.add, op1=ALU.mult)
                    gt = modc(l, 3 * j + 2)
                    steps.do(dve.tensor_scalar(hgate[:, :, :], mod[:, gt:gt + 8, :], 1.0 if j == 1 else 0.5, None, ALU.mult))
                    sh = modc(l, 3 * j)
                dve.wait_ge(sq_used, 8 * n + 8)
                dve.tensor_scalar(nvar[:, c0:T], bank[6][:, c0:T], 1.0 / D, EPS, ALU.mult, ALU.add).then_inc(var_ready, 1)
                dve.wait_ge(rstd_ready, n + 1)
                steps.sync()

                def low(t):
                    dve.wait_ge(uh_ready, 8 * n + t + 1)
                    for k, a, b in conds(c0):
                        last = stt(out=ul[:, t, a:b], in0=nut[:, t % 2, a:b], scalar=mod[:, sh + t, k:k + 1],
                                   in1=uh[:, t, a:b].bitcast(f32), op0=ALU.add, op1=ALU.subtract)
                    last.then_inc(u_ready, 1)

                for t in range(KT):
                    if j is None:
                        f = vec[:, V_FG + t:V_FG + t + 1]
                        stt(out=m3[:, t, 0:SEQ], in0=h[:, t, CTX:T], scalar=f, in1=nrs[:, CTX:T],
                            op0=ALU.mult, op1=ALU.mult).then_inc(out_ready, 1)
                        continue
                    wait(dve, u_ready, 8 * n + t - 1)
                    for k, a, b in conds(c0):
                        last = stt(out=nut[:, t % 2, a:b], in0=h[:, t, a:b], scalar=normA[:, t, k:k + 1],
                                   in1=nrs[:, a:b], op0=ALU.mult, op1=ALU.mult)
                    last.then_inc(ut_ready, 1)
                    if t:
                        low(t - 1)
                if j is not None:
                    low(KT - 1)

            def residual(B, G, t0, c0):
                for j in range(4):
                    split(B + 1, j)
                    dve.wait_ge(panel_done, 4 * B + j + 1)
                    for k, a, b in conds(c0):
                        t = t0 + j
                        hh = h[:, ds(t, 1), a:b].rearrange("p a t -> p (a t)")
                        last = stt(out=hh, in0=bank[j][:, a:b], scalar=hgate[:, ds(t, 1), k:k + 1].rearrange("p a t -> p (a t)"),
                                   in1=hh, op0=ALU.mult, op1=ALU.add)
                    if j % 2:
                        last.then_inc(pair_done[j // 2], 1)

            def ffn(l, f):
                c0 = CTX if l == DEPTH - 1 and f == 1 else 0
                tile0 = (2 * l + f) * FT
                for p, tiles in enumerate(PIECES):
                    B0, G0 = P[("up", l, f, p)]
                    g0, rides = P[("rides", l, f, p)]
                    per = 2 if rides else 1
                    dve.wait_ge(panel_done, 4 * B0)
                    with dve.Fori(0, tiles // 2) as i:
                        B, G, n0 = B0 + per * i, G0 + i, tile0 + 2 * i
                        if rides:
                            ada_panels(B)
                            B = B + 1
                        for k in range(2):
                            split(B + 1, 2 * k)
                            if rides and k == 0:
                                ada_mod(g0 + i, g0 // ADA_GROUPS, (g0 % ADA_GROUPS) + i)
                            dve.wait_ge(sil_ready, n0 + k + 1)
                            dve.wait_ge(panel_done, 4 * B + 2 * k + 2)
                            dve.tensor_tensor(hbuf[:, k, c0:T], sil[:, k, c0:T], bank[2 * k + 1][:, c0:T],
                                              ALU.mult).then_inc(pair_done[k], 1)
                            split(B + 1, 2 * k + 1)
                            dve.wait_ge(hid_hi, n0 + k + 1)
                            dve.tensor_tensor(bl[:, ds(2 * i + k, 1), c0:T].rearrange("p a t -> p (a t)"), hbuf[:, k, c0:T],
                                              bh[:, ds(2 * i + k, 1), c0:T].rearrange("p a t -> p (a t)").bitcast(f32),
                                              ALU.subtract).then_inc(hid_ready, 1)
                    tile0 += tiles
                    B0, G0 = P[("down", l, f, p)]
                    have(dve, pair_done[1], G0)
                    if B0 + 2 < NB:
                        with dve.Fori(0, 2) as i:
                            residual(B0 + i, G0 + i, 4 * i, c0)
                    else:
                        residual(B0, G0, 0, c0)
                        residual(B0 + 1, G0 + 1, 4, c0)
                    have(dve, pair_done[0], G0 + 2)
                    have(dve, pair_done[1], G0 + 2)

            def ab(l):
                q = lambda a: SM[:, a:a + 64]
                q3 = lambda a: q(a).rearrange("p (c n) -> p c n", c=TC)
                row = lambda a, n: rows[:, l, a:a + n].rearrange("p (c n) -> p c n", c=1).broadcast_to([128, TC, n])
                dve.wait_ge(wab_hi, l + 1)
                dve.tensor_tensor(wabl, wab[:, l, :], wabh.bitcast(f32), ALU.subtract).then_inc(wab_lo, 1)
                dve.wait_ge(ab_sum, l + 1)
                ps = bank[7][:, 0:128].rearrange("p (c n) -> p c n", c=TC)
                dve.tensor_tensor(q3(0), ps[:, :, 0:16], row(R_AB, 16), ALU.add)
                steps.do(dve.tensor_tensor(q3(960), ps[:, :, 16:32], row(R_AB + 16, 16), ALU.add))
                steps.sync()
                steps.do(dve.tensor_tensor(q3(0), q3(0), row(R_DT, 16), ALU.add))
                steps.sync()
                stt(out=q(64), in0=q(0), scalar=-1.0, in1=q(0), op0=ALU.mult, op1=ALU.min).then_inc(ab_z, 1)
                dve.wait_ge(ab_exp, 2 * l + 1)
                steps.do(stt(out=q(384), in0=q(0), scalar=0.0, in1=q(320), op0=ALU.max, op1=ALU.add))
                steps.do(dve.tensor_scalar(q(832), q(192), 1.0, None, ALU.add))
                steps.sync()
                al = SM[:, 256:272].rearrange("p (c n) -> p c n", c=1).broadcast_to([128, TC, 16])
                stt(out=q3(384), in0=q3(384), scalar=-1.0, in1=al, op0=ALU.mult, op1=ALU.mult).then_inc(g_ready, 1)
                steps.do(dve.reciprocal(q(832), q(832)))
                dve.wait_ge(gc_sum, l + 1)
                dve.tensor_copy(q(448), bank[7][:, 128:192])
                steps.do(dve.tensor_copy(q(512), bank[7][:, 192:256]))
                steps.sync()
                dve.tensor_tensor(q(576), q(512), q(448), ALU.subtract).then_inc(ab_z, 1)
                dve.wait_ge(ab_exp, 2 * l + 2)
                dve.wait_ge(ab_z, 2 * l + 2)
                steps.do(dve.tensor_scalar(q(640), q(640), -1.0, None, ALU.mult))
                steps.sync()
                for kind, src in ((HB_G, 384), (HB_GC, 448), (HB_NEG, 640), (HB_BETA, 832), (HB_KD, 768), (HB_TOT, 704)):
                    for d in range(2):
                        dst = tab[:, :, (kind * 2 + d) * 4:(kind * 2 + d) * 4 + 4]
                        s = q(src).rearrange("p (c d h) -> p h d c", c=TC, d=2)[:, :, d, :]
                        last = dve.tensor_copy(dst, s)
                last.then_inc(tab_ready, 1)

            def head(l, b, gemm, gdn):
                B0, G0 = P[("head", l)]
                c0 = CTX if l == DEPTH - 1 else 0
                B = B0 + b
                cs = [c for c in range(TC) if 128 * c >= c0]
                s0 = c0 // CTX

                def sp(j):
                    if gemm:
                        split(B + 1, j)

                if not gdn:
                    for j in range(4):
                        sp(j)
                    return
                o = l * DNH + b - 1
                v0 = V_HEAD + l * NVL + HV * (b - 1)
                dve.tensor_copy(hv[:, :], vec[:, ds(v0, HV)])
                dve.tensor_copy(hb[:, :], tab[:, ds(b - 1, 1), :].rearrange("p a n -> p (a n)")).then_inc(E["hv_ready"], 1)
                dve.wait_ge(E["hv_ready"], o + 1)
                for n, j in enumerate((1, 0, 2)):
                    if j == 1:
                        dve.wait_ge(E["pre_ready"], 2 * o + 1)
                    elif j == 0:
                        have(dve, pair_done[0], G0 + b)
                    else:
                        dve.wait_ge(E["pre_ready"], 2 * o + 2)
                    a = s0 if j == 0 else 0
                    y = qkv[:, j, :].rearrange("p (s t) -> p s t", s=2)[:, a:2, :]
                    tap = lambda i: hv[:, 4 + 3 * j + i:5 + 3 * j + i]
                    steps.do(dve.tensor_scalar(y, pre[:, j, a:2, 0:256], tap(0), None, ALU.mult))
                    steps.sync()
                    steps.do(stt(out=y, in0=pre[:, j, a:2, 1:257], scalar=tap(1), in1=y, op0=ALU.mult, op1=ALU.add))
                    steps.sync()
                    stt(out=y, in0=pre[:, j, a:2, 2:258], scalar=tap(2), in1=y, op0=ALU.mult, op1=ALU.add).then_inc(E["conv_ready"], 1)
                sp(0)
                dve.wait_ge(E["conv_ready"], 3 * o + 3)
                for n, j in enumerate((1, 0)):
                    a = c0 if j == 0 else 0
                    dve.wait_ge(E["l2_sum"], 2 * o + n + 1)
                    dve.tensor_scalar(hrs[:, n, a:T], bank[4 + n][:, a:T], EPS, None, ALU.add).then_inc(E["l2_var"], 1)
                dve.wait_ge(E["l2_rstd"], 2 * o + 1)
                dve.tensor_tensor(qkv[:, 1, :], qkv[:, 1, :], hrs[:, 0, :], ALU.mult).then_inc(E["kn_ready"], 1)
                dve.wait_ge(E["kv_turned"], 2 * o + 1)
                dve.tensor_copy(vtok, bank[7][:, :]).then_inc(E["vtok_ready"], 1)
                dve.wait_ge(E["l2_rstd"], 2 * o + 2)
                stt(out=qkv[:, 0, c0:T], in0=qkv[:, 0, c0:T], scalar=128 ** -0.5, in1=hrs[:, 1, c0:T],
                    op0=ALU.mult, op1=ALU.mult).then_inc(E["qn_ready"], 1)
                dve.wait_ge(E["gram"], 2 * o + 1)
                dve.tensor_tensor(c4d(Gs), c4d(bank[4][:, :]), bc(cst[:, C_OFF:C_OFF + 128], TC, 128), ALU.mult).then_inc(E["gs_ready"], 1)
                for d in range(2):
                    dve.wait_ge(E["gc_row"], 2 * o + d + 1)
                    for c in range(TC):
                        last = stt(out=DT[:, d, 128 * c:128 * c + 128], in0=bank[6 + d][:, 128 * c:128 * c + 128],
                                   scalar=hb[:, hcol(HB_GC, d, c)], in1=cst[:, C_NM + 128 * d:C_NM + 128 * d + 128],
                                   op0=ALU.subtract, op1=ALU.add)
                    last.then_inc(E["dm_ready"], 1)
                    dve.wait_ge(E["eg_ready"], 2 * o + d + 1)
                    dve.wait_ge(E["qn_ready"], o + 1)
                    dve.tensor_tensor(Qt[:, d, c0:T], qkv[:, 0, c0:T], eg[:, d, c0:T], ALU.mult).then_inc(E["qt_ready"], 1)
                dve.wait_ge(E["gs_ready"], o + 1)
                for d in range(2):
                    dve.wait_ge(E["dt_ready"], 2 * o + d + 1)
                    for c in range(TC):
                        s = slice(128 * c, 128 * c + 128)
                        last = stt(out=AT[:, d, s], in0=Gs[:, s], scalar=hb[:, hcol(HB_BETA, d, c)], in1=DT[:, d, s],
                                   op0=ALU.mult, op1=ALU.mult)
                    last.then_inc(E["at_ready"], 1)
                    dve.wait_ge(E["at_ready"], 2 * o + d + 1)
                    steps.do(dve.tensor_tensor(c4d(eg[:, d, :]), c4d(AT[:, d, :]), bc(cst[:, C_LV:C_LV + 128], TC, 128), ALU.mult))
                    steps.sync()
                    dve.tensor_tensor(c4d(XT[:, d, :]), c4d(eg[:, d, :]), bc(ident, TC, 128), ALU.add).then_inc(E["xt0_ready"], 1)
                for d in range(2):
                    dve.wait_ge(E["kq_ready"], o + 1)
                    dve.tensor_tensor(IT[:, d, c0:T], KQs[:, c0:T], DT[:, d, c0:T], ALU.mult).then_inc(E["it_ready"], 1)
                sp(1)
                for v in range(1, 7):
                    mask = bc(cst[:, C_LV + 128 * v:C_LV + 128 * v + 128], TC, 128)
                    for d in range(2):
                        dve.wait_ge(E["p_sum"], 18 * o + 2 * (v - 1) + d + 1)
                        dve.tensor_tensor(c4d(Pm[:, d, :]), c4d(bank[4 + d][:, :]), mask, ALU.mult).then_inc(E["pm_ready"], 1)
                sp(2)
                for d in range(2):
                    dve.wait_ge(E["p_sum"], 18 * o + 16 + d + 1)
                    last = dve.tensor_tensor(XTf[:, d, :], XT[:, d, :].bitcast(f32), bank[4 + d][:, :], ALU.subtract)
                    last.then_inc(E["xt0_ready"], 1)
                for s in range(TC):
                    for d in range(2):
                        c = chunk(d, s)
                        if s:
                            dve.wait_ge(E["ks_sum"], 6 * o + 2 * (s - 1) + d + 1)
                            stt(out=Rr[:, d, :], in0=bank[4 + d][:, 0:128], scalar=hb[:, hcol(HB_NEG, d, c)],
                                in1=vtok[:, 128 * c:128 * c + 128], op0=ALU.mult, op1=ALU.add).then_inc(E["r_ready"], 1)
                    for d in range(2):
                        c = chunk(d, s)
                        dve.wait_ge(E["y_sum"], 8 * o + 2 * s + d + 1)
                        dve.tensor_scalar(vn[:, d, :], bank[4 + d][:, 128:256], hb[:, hcol(HB_BETA, d, c)], None,
                                          ALU.mult).then_inc(E["vn_ready"], 1)
                    if s < TC - 1:
                        for d in range(2):
                            c = chunk(d, s)
                            dve.wait_ge(E["ds_sum"], 6 * o + 2 * s + d + 1)
                            if s == 0:
                                dve.tensor_copy(St[:, 0, d, :], bank[4 + d][:, 256:384]).then_inc(E["s_ready"], 1)
                            else:
                                dve.wait_ge(E["s_ready"], 6 * o + 2 * (s - 1) + d + 1)
                                stt(out=St[:, s % 2, d, :], in0=St[:, (s - 1) % 2, d, :], scalar=hb[:, hcol(HB_TOT, d, c)],
                                    in1=bank[4 + d][:, 256:384], op0=ALU.mult, op1=ALU.add).then_inc(E["s_ready"], 1)
                dve.wait_ge(E["on_sum"], o + 1)
                dve.tensor_scalar(eg[:, 1, c0:T], bank[7][:, c0:T], 1.0 / 128, EPS, ALU.mult, ALU.add).then_inc(E["on_var"], 1)
                dve.wait_ge(E["on_rstd"], o + 1)
                steps.do(stt(out=eg[:, 0, c0:T], in0=bank[6][:, c0:T], scalar=vec[:, l * NVL + V_DNG:l * NVL + V_DNG + 1],
                             in1=eg[:, 1, c0:T], op0=ALU.mult, op1=ALU.mult))
                steps.sync()
                dve.tensor_tensor(gate[:, c0:T], gate[:, c0:T], eg[:, 0, c0:T], ALU.mult).then_inc(E["on_ready"], 1)
                sp(3)
                dve.wait_ge(E["bh_ready"], o + 1)
                dve.tensor_tensor(bl[:, ds(b - 1, 1), c0:T].rearrange("p a t -> p (a t)"), gate[:, c0:T],
                                  bh[:, ds(b - 1, 1), c0:T].rearrange("p a t -> p (a t)").bitcast(f32),
                                  ALU.subtract).then_inc(E["head_ready"], 1)
                zero_pads()

            def zero_pads():
                for j in range(3):
                    steps.do(dve.memset(pre[:, j, :, 0:1], 0.0))
                    steps.do(dve.memset(pre[:, j, :, 257:258], 0.0))
                steps.sync()

            HSTEPS = 6 + 2 + 1 + 6
            def heads(l):
                dve.wait_ge(panel_done, 4 * P[("head", l)][0])
                zero_pads()
                head(l, 0, True, False)
                with steps.loop(1, DNH, HSTEPS) as b:
                    head(l, b, True, True)
                head(l, DNH, False, True)

            def branch(l, r):
                B0, G0 = P[("br", l, r)]
                c0 = CTX if l == DEPTH - 1 else 0
                n0 = (3 * l + r) * 8
                with steps.loop(0, 4, 0 if r == 0 else 2) as i:
                    for k in range(2):
                        split(B0 + i + 1, 2 * k)
                        dve.wait_ge(panel_done, 4 * (B0 + i) + 2 * k + 2)
                        dve.wait_ge(C["br_gate"], n0 + 2 * i + k + 1)
                        mt = m3[:, ds(2 * i + k, 1), c0:T].rearrange("p a t -> p (a t)")
                        if r == 0:
                            dve.tensor_tensor(mt, sil[:, k, c0:T], bank[2 * k + 1][:, c0:T], ALU.mult).then_inc(pair_done[k], 1)
                        else:
                            steps.do(dve.tensor_tensor(hbuf[:, k, c0:T], sil[:, k, c0:T], bank[2 * k + 1][:, c0:T], ALU.mult))
                            steps.sync()
                            dve.tensor_tensor(mt, mt, hbuf[:, k, c0:T], ALU.add).then_inc(pair_done[k], 1)
                        split(B0 + i + 1, 2 * k + 1)
                for k in range(2):
                    have(dve, pair_done[k], G0 + 4)

            def qk_norm(na, gcol, dst, c0):
                dve.wait_ge(A["a_sum"], na + 1)
                dve.tensor_scalar(ars[:, c0:T], bank[4][:, c0:T], 1.0 / HD, EPS, ALU.mult, ALU.add).then_inc(A["a_var"], 1)
                dve.wait_ge(A["a_rstd"], na + 1)
                stt(out=dst[:, c0:T], in0=ax[:, c0:T], scalar=vec[:, gcol:gcol + 1], in1=ars[:, c0:T],
                    op0=ALU.mult, op1=ALU.mult).then_inc(A["a_norm"], 1)
                dve.wait_ge(A["a_swap"], na + 1)
                steps.do(dve.tensor_tensor(asw[:, 0:256], bank[5][:, 0:256], cst[:, C_SIN:C_SIN + 256], ALU.mult))
                steps.do(dve.tensor_tensor(asw[:, 256:512], dst[:, CTX:T], cst[:, C_COS:C_COS + 256], ALU.mult))
                steps.sync()
                dve.tensor_tensor(dst[:, CTX:T], asw[:, 0:256], asw[:, 256:512], ALU.add).then_inc(A["a_done"], 1)

            def attention(l):
                c0 = CTX if l == DEPTH - 1 else 0
                B0, G0 = P[("kv", l)]
                L = l * NVL
                na = 10 * l
                for j in range(4):
                    split(B0 + 1, j)
                dve.wait_ge(panel_done, 4 * B0 + 4)
                for j in range(2):
                    qk_norm(na, L + V_KG, kT[:, j, :], 0)
                    na += 1
                for j in range(2):
                    dve.wait_ge(A["a_vturn"], 2 * l + j + 1)
                    dve.tensor_copy(vt[:, j, :, :].rearrange("p c f -> p (c f)"), bank[4 + j][:, :]).then_inc(A["a_vtok"], 1)
                dve.wait_ge(A["a_vtok"], 2 * l + 2)
                dve.sem_inc(pair_done[0], 1)
                dve.sem_inc(pair_done[1], 1)
                nu = att_units_before(l, 0)
                for p in range(2):
                    B, G = P[("q", l)][0] + p, P[("q", l)][1] + p
                    for j in range(4):
                        split(B + 1, j)
                        qk_norm(na, L + V_QG, qx[:, j, :], c0)
                        na += 1
                    dve.wait_ge(A["a_done"], na)
                    units = att_units(l)

                    def scale_p(u):
                        lat = units[u][2]
                        n = 1 if lat else 2
                        dve.wait_ge(A["s_exp"], nu + u + 1)
                        st = 8 * (u % 2)
                        steps.do(dve.reciprocal(stat[:, st + 6:st + 6 + n], stat[:, st + 4:st + 4 + n]))
                        steps.sync()
                        for q in range(n):
                            w = 512 // n
                            last = dve.tensor_scalar(Pb[:, u % 2, q * w:(q + 1) * w], Pb[:, u % 2, q * w:(q + 1) * w],
                                                     stat[:, st + 6 + q:st + 7 + q], None, ALU.mult)
                        last.then_inc(A["s_scaled"], 1)

                    for u, (j, a, lat) in enumerate(units):
                        n = 1 if lat else 2
                        st = 8 * (u % 2)
                        dve.wait_ge(A["s_sum"], nu + u + 1)
                        steps.do(dve.reduce_max(stat[:, st:st + n], bank[4 + u % 2][:, :].rearrange("p (n k) -> p n k", n=n), AX.X))
                        steps.sync()
                        dve.tensor_scalar(stat[:, st + 2:st + 2 + n], stat[:, st:st + n], -HD ** -0.5, None,
                                          ALU.mult).then_inc(A["s_max"], 1)
                        if u:
                            scale_p(u - 1)
                    scale_p(len(units) - 1)
                    nu += len(units)
                    for j in range(4):
                        dve.wait_ge(A["att_hi"], 8 * l + 4 * p + j + 1)
                        last = dve.tensor_tensor(bl[:, 4 * p + j, c0:T], bank[j][:, c0:T], bh[:, 4 * p + j, c0:T].bitcast(f32), ALU.subtract)
                        if j % 2:
                            last.then_inc(pair_done[j // 2], 1)
                        else:
                            last.then_inc(A["att_ready"], 1)

            def conv(l):
                B0, G0 = P[("conv", l)]
                c0 = CTX if l == DEPTH - 1 else 0
                s0 = c0 // CTX
                two = lambda ap: ap.rearrange("p (s t) -> p s t", s=2)[:, s0:2, :]
                for k in (0, 257):
                    steps.do(dve.memset(cpr[:, :, k:k + 1], 0.0))
                steps.sync()
                with steps.loop(0, 2, 4 * 4 - 2) as i:
                    B = B0 + 3 * i
                    n0 = 8 * l + 4 * i
                    dve.tensor_copy(cvec, vec[:, ds(l * NVL + V_CONV + 4 * CV * i, 4 * CV)]).then_inc(C["c_vec"], 1)
                    dve.wait_ge(C["c_vec"], 2 * l + i + 1)
                    for t in range(4):
                        q = 3 * t
                        v = lambda n: cvec[:, t * CV + n:t * CV + n + 1]
                        split(B + q // 4 + 1, q % 4)
                        split(B + (q + 1) // 4 + 1, (q + 1) % 4)
                        dve.wait_ge(C["c_p4"], n0 + t + 1)
                        dve.wait_ge(panel_done, 4 * B + q + 2)
                        ins = stt(out=cpr[:, s0:2, 1:257], in0=two(bank[(q + 1) % 4][:, :]), scalar=v(1), in1=two(c4[:, :]),
                                  op0=ALU.add, op1=ALU.mult)
                        if t in (0, 2):
                            ins.then_inc(pair_done[0 if t == 0 else 1], 1)
                            have(dve, pair_done[0 if t == 0 else 1], (G0 + 3 * i + (0 if t == 0 else 1)) + 1)
                        else:
                            steps.do(ins)
                            steps.sync()
                        y = two(cy[:, :])
                        ins = dve.tensor_scalar(y, cpr[:, s0:2, 0:256], v(3), None, ALU.mult)
                        if t in (1, 3):
                            k = 1 if t == 1 else 0
                            ins.then_inc(pair_done[k], 1)
                            have(dve, pair_done[k], G0 + 3 * i + (1 if t == 1 else 3))
                        else:
                            steps.do(ins)
                            steps.sync()
                        steps.do(stt(out=y, in0=cpr[:, s0:2, 1:257], scalar=v(4), in1=y, op0=ALU.mult, op1=ALU.add))
                        steps.sync()
                        steps.do(stt(out=y, in0=cpr[:, s0:2, 2:258], scalar=v(5), in1=y, op0=ALU.mult, op1=ALU.add))
                        steps.sync()
                        split(B + (q + 2) // 4 + 1, (q + 2) % 4)
                        dve.wait_ge(panel_done, 4 * B + q + 3)
                        z = cz[:, t % 2, :]
                        stt(out=z[:, c0:T], in0=bank[(q + 2) % 4][:, c0:T], scalar=v(2), in1=cy[:, c0:T],
                            op0=ALU.add, op1=ALU.mult).then_inc(C["c_out"], 1)
                        dve.wait_ge(C["c_hi"], n0 + t + 1)
                        ins = dve.tensor_tensor(bl[:, ds(4 * i + t, 1), c0:T].rearrange("p a t -> p (a t)"), z[:, c0:T],
                                                bh[:, ds(4 * i + t, 1), c0:T].rearrange("p a t -> p (a t)").bitcast(f32), ALU.subtract)
                        if t == 1:
                            ins.then_inc(pair_done[0], 1)
                        elif t == 3:
                            ins.then_inc(pair_done[1], 1)
                        else:
                            steps.do(ins)

            def project_out(l):
                B0, G0 = P[("out", l)]
                c0 = CTX if l == DEPTH - 1 else 0
                for t in range(KT):
                    dve.wait_ge(C["mh_ready"], 8 * l + t + 1)
                    dve.tensor_tensor(ul[:, t, c0:T], m3[:, t, c0:T], uh[:, t, c0:T].bitcast(f32), ALU.subtract).then_inc(C["mx_ready"], 1)
                with dve.Fori(0, 2) as i:
                    residual(B0 + i, G0 + i, 4 * i, c0)
                have(dve, pair_done[0], G0 + 2)
                have(dve, pair_done[1], G0 + 2)

            ada_only(("ada", 0))
            n = 0
            for l in range(DEPTH):
                c_last = CTX if l == DEPTH - 1 else 0
                norm(n, l, 0, 0)
                ffn(l, 0)
                ada_only(("ada1", l))
                norm(n + 1, l, 1, 0)
                ab(l)
                heads(l)
                branch(l, 0)
                attention(l)
                branch(l, 1)
                conv(l)
                branch(l, 2)
                project_out(l)
                norm(n + 2, l, 2, c_last)
                ffn(l, 1)
                if l == 0:
                    ada_only(("ada2", 0))
                n += 3
            norm(n, None, None, CTX)

        @block.tensor
        def _(pe):
            mm = pe.matmul

            def panel(B, j, xh, xl, c0, kts=KT, ready=None, lo=0, hi=None):
                hi = 3 * kts if hi is None else hi
                if lo == 0:
                    pe.wait_ge(lo_ready, 4 * B + j + 1)
                w = lambda t, a: a[:, j, 128 * t:128 * t + 128]
                for n in range(lo, hi):
                    t, r = n // 3, n % 3
                    if ready is not None and r == 0:
                        pe.wait_ge(ready[0], ready[1] + t + 1)
                    a, x = ((whi, xh), (whi, xl), (wlo, xh))[r]
                    last = mm(bank[j][:, c0:T], w(t, a), x[:, t, c0:T], start=n == 0, stop=n == 3 * kts - 1)
                if hi == 3 * kts:
                    last.then_inc(panel_done, 1)

            def pair_free(G, j):
                if j % 2 == 0:
                    have(pe, pair_done[j // 2], G)

            def ada_panels(B, g):
                have(pe, ada_row, g)
                for j in range(4):
                    pe.wait_ge(lo_ready, 4 * B + j + 1)
                    for t in range(2):
                        for w in (whi, wlo):
                            last = mm(bank[4][:, :], cstat[:, 2 * j + t, :], w[:, j, 512 * t:512 * t + 512],
                                      start=(j, t) == (0, 0) and w is whi, stop=(j, t) == (3, 1) and w is wlo)
                    last.then_inc(panel_done, 1)

            def ada_turn(g):
                have(pe, ada_row, g + 1)
                have(pe, mod_ready, g)
                for t in range(4):
                    last = mm(bank[5][:, 2 * t:2 * t + 2], arow[:, 128 * t:128 * t + 128], cst[0:4, C_SEL:C_SEL + 2],
                              start=True, stop=True)
                last.then_inc(ada_turned, 1)

            def ada_only(key):
                B0, _ = P[key]
                g0, n = P["groups"][key]
                with pe.Fori(0, n) as i:
                    ada_panels(B0 + i, g0 + i)
                    ada_turn(g0 + i)

            def norm(n, c0):
                for t in range(KT):
                    pe.wait_ge(sq_ready, 8 * n + t + 1)
                    if t == 0:
                        wait(pe, var_ready, n)
                    mm(bank[6][:, c0:T], ones, nsq[:, t % 2, c0:T], start=t == 0, stop=t == KT - 1).then_inc(sq_used, 1)

            def ffn(l, f, n):
                c0 = CTX if l == DEPTH - 1 and f == 1 else 0
                tile0 = (2 * l + f) * FT
                for p, tiles in enumerate(PIECES):
                    B0, G0 = P[("up", l, f, p)]
                    g0, rides = P[("rides", l, f, p)]
                    per = 2 if rides else 1
                    with pe.Fori(0, tiles // 2) as i:
                        B, G = B0 + per * i, G0 + i
                        if rides:
                            ada_panels(B, g0 + i)
                            B = B + 1
                        for j in range(4):
                            pair_free(G, j)
                            panel(B, j, uh, ul, c0, ready=(u_ready, 8 * n) if j == 0 and p == 0 else None)
                            if rides and j == 0:
                                ada_turn(g0 + i)
                    tile0 += tiles
                    B0, G0 = P[("down", l, f, p)]
                    pe.wait_ge(hid_ready, tile0)
                    with pe.Fori(0, 2) as i:
                        for j in range(4):
                            pair_free(G0 + i, j)
                            panel(B0 + i, j, bh, bl, c0, kts=tiles)

            def ab(l, n):
                pe.wait_ge(u_ready, 8 * n + 8)
                pe.wait_ge(wab_lo, l + 1)
                for c in range(TC):
                    s = slice(128 * c, 128 * c + 128)
                    for t in range(KT):
                        for r, (x, w) in enumerate(((uh, wabh), (ul, wabh), (uh, wabl))):
                            last = mm(bank[7][:, 32 * c:32 * c + 32], x[:, t, s], w[:, 32 * t:32 * t + 32],
                                      start=t == 0 and r == 0, stop=t == KT - 1 and r == 2)
                last.then_inc(ab_sum, 1)
                pe.wait_ge(g_ready, l + 1)
                g = SM[:, 384:448].rearrange("p (c n) -> p c n", c=TC)
                for c in range(TC):
                    for d in range(2):
                        mm(bank[7][:, 128 + 16 * c + 8 * d:136 + 16 * c + 8 * d], cst[:, C_CUM + 128 * d:C_CUM + 128 * d + 128],
                           g[:, c, 8 * d:8 * d + 8], start=True, stop=True)
                    last = mm(bank[7][:, 192 + 16 * c:208 + 16 * c], ones, g[:, c, :], start=True, stop=True)
                last.then_inc(gc_sum, 1)

            def head(l, b, gemm, gdn):
                B0, G0 = P[("head", l)]
                c0 = CTX if l == DEPTH - 1 else 0
                B, G = B0 + b, G0 + b
                issued = [0]

                def project(n):
                    if not gemm:
                        return
                    while n:
                        j, at = issued[0] // 24, issued[0] % 24
                        k = min(n, 24 - at)
                        if at == 0:
                            pair_free(G, j)
                        panel(B, j, uh, ul, c0 if j in (0, 3) else 0, lo=at, hi=at + k)
                        issued[0] += k
                        n -= k

                if not gdn:
                    project(96)
                    return
                o = l * DNH + b - 1
                cs = [c for c in range(TC) if 128 * c >= c0]
                sl = lambda c: slice(128 * c, 128 * c + 128)
                project(24)
                for n, j in enumerate((1, 0)):
                    a = c0 if j == 0 else 0
                    pe.wait_ge(E["hsq_ready"], 2 * o + n + 1)
                    mm(bank[4 + n][:, a:T], ones, hsq[:, n, a:T], start=True, stop=True).then_inc(E["l2_sum"], 1)
                    project(4)
                pe.wait_ge(E["silu_ready"], 3 * o + 3)
                have(pe, E["head_ready"], o)
                for c in range(TC):
                    last = pe.transpose(bank[7][:, sl(c)], qkv[:, 2, sl(c)], ident)
                last.then_inc(E["kv_turned"], 1)
                project(4)
                pe.wait_ge(E["kn_ready"], o + 1)
                for c in range(TC):
                    last = pe.transpose(bank[6][:, sl(c)], qkv[:, 1, sl(c)], ident)
                last.then_inc(E["kv_turned"], 1)
                pe.wait_ge(E["l2_var"], 2 * o + 2)
                for c in range(TC):
                    last = mm(bank[4][:, sl(c)], qkv[:, 1, sl(c)], qkv[:, 1, sl(c)], start=True, stop=True)
                last.then_inc(E["gram"], 1)
                project(2)
                pe.wait_ge(E["qn_ready"], o + 1)
                for c in cs:
                    last = mm(bank[5][:, sl(c)], qkv[:, 1, sl(c)], qkv[:, 0, sl(c)], start=True, stop=True)
                last.then_inc(E["gram"], 1)
                project(2)
                pe.wait_ge(E["ktok_ready"], o + 1)
                pe.wait_ge(E["vtok_ready"], o + 1)
                for d in range(2):
                    for c in range(TC):
                        last = mm(bank[6 + d][:, sl(c)], hb[:, hcol(HB_G, d, c)].broadcast_to([128, 128]),
                                  cst[:, C_CUM + 128 * d:C_CUM + 128 * d + 128], start=True, stop=True)
                    last.then_inc(E["gc_row"], 1)
                    project(2)
                for d in range(2):
                    pe.wait_ge(E["xt0_ready"], 4 * o + d + 1)
                    if d == 0:
                        pe.wait_ge(E["gs_ready"], o + 1)
                    else:
                        pe.wait_ge(E["kq_ready"], o + 1)
                    for c in range(TC):
                        last = pe.transpose(bank[4 + d][:, sl(c)], XT[:, d, sl(c)].bitcast(f32), ident)
                    last.then_inc(E["xt0_turned"], 1)
                    project(4)
                for v in range(1, 7):
                    for d in range(2):
                        if v == 1:
                            pe.wait_ge(E["atr_ready"], 2 * o + d + 1)
                        else:
                            pe.wait_ge(E["xt_ready"], 12 * o + 2 * (v - 2) + d + 1)
                        pe.wait_ge(E["x_ready"], 14 * o + 2 * (v - 1) + d + 1)
                        for c in range(TC):
                            last = mm(bank[4 + d][:, sl(c)], ATr[:, d, sl(c)], X[:, d, sl(c)], start=True, stop=True)
                        last.then_inc(E["p_sum"], 1)
                    project(2)
                    for d in range(2):
                        pe.wait_ge(E["pm_ready"], 14 * o + 2 * (v - 1) + d + 1)
                        if v == 1:
                            pe.wait_ge(E["eg_ready"], 2 * o + d + 1)
                            pe.wait_ge(E["dm_ready"], 2 * o + d + 1)
                        for c in range(TC):
                            mm(bank[6 + d][:, sl(c)], XT[:, d, sl(c)], Pm[:, d, sl(c)], start=True, stop=False)
                            last = mm(bank[6 + d][:, sl(c)], XT[:, d, sl(c)], idr[:, :], start=False, stop=True)
                            if v < 6:
                                mm(bank[4 + d][:, sl(c)], Pm[:, d, sl(c)], XT[:, d, sl(c)], start=True, stop=False)
                                last = mm(bank[4 + d][:, sl(c)], idr[:, :], XT[:, d, sl(c)], start=False, stop=True)
                        last.then_inc(E["x_sum"], 1)
                    project(2)
                for d in range(2):
                    pe.wait_ge(E["x_ready"], 14 * o + 12 + d + 1)
                    for c in range(TC):
                        last = pe.transpose(bank[4 + d][:, sl(c)], X[:, d, sl(c)].bitcast(f32), ident)
                    last.then_inc(E["p_sum"], 1)
                for d in range(2):
                    for c in range(TC):
                        mm(bank[6 + d][:, sl(c)], AT[:, d, sl(c)], X[:, d, sl(c)].bitcast(f32), start=True, stop=False)
                        mm(bank[6 + d][:, sl(c)], idr[:, :], X[:, d, sl(c)], start=False, stop=False)
                        last = mm(bank[6 + d][:, sl(c)], nidr[:, :], idr[:, :], start=False, stop=True)
                    last.then_inc(E["p_sum"], 1)
                project(2)
                for d in range(2):
                    pe.wait_ge(E["xt_ready"], 12 * o + 10 + d + 1)
                    pe.wait_ge(E["pm_ready"], 14 * o + 12 + d + 1)
                    for c in range(TC):
                        last = mm(bank[4 + d][:, sl(c)], Pm[:, d, sl(c)], XT[:, d, sl(c)], start=True, stop=True)
                    last.then_inc(E["p_sum"], 1)
                project(2)
                first = [True]
                for s in range(TC):
                    if s:
                        for d in range(2):
                            c = chunk(d, s)
                            pe.wait_ge(E["s_ready"], 6 * o + 2 * (s - 1) + d + 1)
                            mm(bank[4 + d][:, 0:128], qkv[:, 1, sl(c)], St[:, (s - 1) % 2, d, :], start=True, stop=True).then_inc(E["ks_sum"], 1)
                        project(1)
                    for d in range(2):
                        c = chunk(d, s)
                        if s == 0:
                            pe.wait_ge(E["xt0_ready"], 4 * o + 2 + d + 1)
                            r = vtok[:, sl(c)]
                        else:
                            pe.wait_ge(E["r_ready"], 6 * o + 2 * (s - 1) + d + 1)
                            r = Rr[:, d, :]
                        mm(bank[4 + d][:, 128:256], XTf[:, d, sl(c)], r, start=True, stop=True).then_inc(E["y_sum"], 1)
                    project(1)
                    for d in range(2):
                        c = chunk(d, s)
                        if s < TC - 1:
                            pe.wait_ge(E["vd_ready"], 6 * o + 2 * s + d + 1)
                            mm(bank[4 + d][:, 256:384], ktok[:, sl(c)], vd[:, d, :], start=True, stop=True).then_inc(E["ds_sum"], 1)
                    for d in range(2):
                        c = chunk(d, s)
                        pe.wait_ge(E["vn_ready"], 8 * o + 2 * s + d + 1)
                        if first[0]:
                            pe.wait_ge(E["qt_ready"], 2 * o + 2)
                            pe.wait_ge(E["it_ready"], 2 * o + 2)
                        if c not in cs:
                            continue
                        if s:
                            mm(bank[6][:, sl(c)], St[:, (s - 1) % 2, d, :], Qt[:, d, sl(c)], start=first[0], stop=False, skip_group_check=True)
                            first[0] = False
                        last = mm(bank[6][:, sl(c)], vn[:, d, :], IT[:, d, sl(c)], start=first[0],
                                  stop=False, skip_group_check=True)
                        first[0] = False
                    project(1)
                last.then_inc(E["o_sum"], 1)
                project(3)
                pe.wait_ge(E["osq_ready"], o + 1)
                mm(bank[7][:, c0:T], ones, eg[:, 0, c0:T], start=True, stop=True).then_inc(E["on_sum"], 1)
                if gemm:
                    project(96 - issued[0])

            def heads(l):
                head(l, 0, True, False)
                with pe.Fori(1, DNH) as b:
                    head(l, b, True, True)
                head(l, DNH, False, True)

            def branch(l, r, ready):
                B0, G0 = P[("br", l, r)]
                c0 = CTX if l == DEPTH - 1 else 0
                for s, n in ready:
                    have(pe, s, n)
                with pe.Fori(0, 4) as i:
                    for j in range(4):
                        pair_free(G0 + i, j)
                        panel(B0 + i, j, *((uh, ul) if j % 2 == 0 else (bh, bl)), c0)

            def qk_sum(na, c0):
                pe.wait_ge(A["a_sq"], na + 1)
                mm(bank[4][:, c0:T], cst[:, C_BLK:C_BLK + 128], asq[:, c0:T], start=True, stop=True).then_inc(A["a_sum"], 1)

            def qk_swap(na, dst):
                pe.wait_ge(A["a_norm"], na + 1)
                mm(bank[5][:, 0:256], cst[:, C_PERM:C_PERM + 128], dst[:, CTX:T], start=True, stop=True).then_inc(A["a_swap"], 1)

            def attention(l):
                c0 = CTX if l == DEPTH - 1 else 0
                B0, G0 = P[("kv", l)]
                na = 10 * l
                for j in range(4):
                    pair_free(G0, j)
                    panel(B0, j, uh, ul, 0)
                for j in range(2):
                    qk_sum(na, 0)
                    qk_swap(na, kT[:, j, :])
                    na += 1
                pe.wait_ge(A["a_done"], na)
                for j in range(2):
                    pe.wait_ge(A["a_vx"], 2 * l + j + 1)
                    for c in range(TC):
                        last = pe.transpose(bank[4 + j][:, 128 * c:128 * c + 128], ax[:, 128 * c:128 * c + 128], ident)
                    last.then_inc(A["a_vturn"], 1)
                pe.wait_ge(A["a_vtok"], 2 * l + 2)
                nu = att_units_before(l, 0)
                for p in range(2):
                    B, G = P[("q", l)][0] + p, P[("q", l)][1] + p
                    for j in range(5):
                        if j < 4:
                            pair_free(G, j)
                            panel(B, j, uh, ul, c0, hi=12)
                        if j:
                            qk_sum(na, c0)
                        if j < 4:
                            panel(B, j, uh, ul, c0, lo=12)
                        if j:
                            qk_swap(na, qx[:, j - 1, :])
                            na += 1
                    pe.wait_ge(A["a_done"], na)
                    units = att_units(l)

                    def turn(u):
                        pe.wait_ge(A["s_scaled"], nu + u + 1)
                        for k in range(4):
                            last = pe.transpose(bank[6 + u % 2][:, 128 * k:128 * k + 128], Pb[:, u % 2, 128 * k:128 * k + 128], ident)
                        last.then_inc(A["s_turned"], 1)

                    def pv(u):
                        j, a, kind = units[u]
                        pe.wait_ge(A["s_pt"], nu + u + 1)
                        rows_ = slice(64 * a, 64 * a + 64)
                        v = lambda kt: vt[:, p, kt, 64 * a:64 * a + 64]
                        pt = lambda k: PT[:, u % 2, 128 * k:128 * k + 128]
                        if kind:
                            for kt in range(4):
                                last = mm(bank[j][rows_, 128 * kind:128 * kind + 128], v(kt), pt(kt), start=kt == 0, stop=kt == 3)
                        else:
                            for q in range(2):
                                for kt in range(2):
                                    last = mm(bank[j][rows_, 128 * q:128 * q + 128], v(kt), pt(2 * q + kt), start=kt == 0, stop=kt == 1)
                        last.then_inc(A["s_pv"], 1)

                    def scores(u):
                        j, a, kind = units[u]
                        if u >= 2:
                            pe.wait_ge(A["s_exp"], nu + u - 1)
                        r = slice(64 * a, 64 * a + 64)
                        if kind:
                            last = mm(bank[4 + u % 2][:, :], qx[r, j, 128 * kind:128 * kind + 128], kT[r, p, :], start=True, stop=True)
                        else:
                            for q in range(2):
                                last = mm(bank[4 + u % 2][:, 256 * q:256 * q + 256], qx[r, j, 128 * q:128 * q + 128], kT[r, p, 0:CTX],
                                          start=True, stop=True)
                        last.then_inc(A["s_sum"], 1)

                    n = len(units)
                    scores(0)
                    for u in range(n + 2):
                        if u + 1 < n:
                            scores(u + 1)
                        if u >= 2:
                            pv(u - 2)
                        if 1 <= u <= n:
                            turn(u - 1)
                    nu += n

            def conv(l):
                B0, G0 = P[("conv", l)]
                c0 = CTX if l == DEPTH - 1 else 0
                with pe.Fori(0, 2) as i:
                    for q in range(12):
                        pair_free(G0 + 3 * i + q // 4, q % 4)
                        panel(B0 + 3 * i + q // 4, q % 4, uh, ul, c0)

            def project_out(l):
                B0, G0 = P[("out", l)]
                c0 = CTX if l == DEPTH - 1 else 0
                with pe.Fori(0, 2) as i:
                    for j in range(4):
                        pair_free(G0 + i, j)
                        panel(B0 + i, j, uh, ul, c0, ready=(C["mx_ready"], 8 * l) if j == 0 else None)

            pe.sem_inc(ada_turned, 1)
            pe.wait_ge(setup_act, 2)
            pe.wait_ge(setup_dve, 2)
            pe.wait_ge(consts_loaded, 16)
            ada_only(("ada", 0))
            n = 0
            for l in range(DEPTH):
                c_last = CTX if l == DEPTH - 1 else 0
                norm(n, 0)
                ffn(l, 0, n)
                ada_only(("ada1", l))
                norm(n + 1, 0)
                ab(l, n + 1)
                heads(l)
                branch(l, 0, [(E["head_ready"], DNH * (l + 1))])
                attention(l)
                branch(l, 1, [(pair_done[0], P[("q", l)][1] + 2), (pair_done[1], P[("q", l)][1] + 2)])
                conv(l)
                branch(l, 2, [(pair_done[1], P[("conv", l)][1] + 6)])
                project_out(l)
                norm(n + 2, c_last)
                ffn(l, 1, n + 2)
                if l == 0:
                    ada_only(("ada2", 0))
                n += 3
            norm(n, CTX)


def _tables():
    c = np.zeros((128, NC), np.float32)
    i = np.arange(128)
    c[:, C_ID:C_ID + 128] = np.eye(128)
    c[:, C_OFF:C_OFF + 128] = 1 - np.eye(128)
    c[:, C_ONE:C_ONE + 128] = 1
    c[:, C_BLK:C_BLK + 128] = (i[:, None] // 64) == (i[None, :] // 64)
    c[:, C_PERM:C_PERM + 128] = (i[:, None] ^ 32) == i[None, :]
    for v in range(7):
        s = 1 << v
        c[:, C_LV + 128 * v:C_LV + 128 * v + 128] = -1.0 * (
            (i[:, None] // (2 * s) == i[None, :] // (2 * s)) & (i[:, None] // s != i[None, :] // s))
    for d in range(2):
        ok = (i[None, :] >= i[:, None]) if d == 0 else (i[None, :] <= i[:, None])
        c[:, C_NM + 128 * d:C_NM + 128 * d + 128] = np.where(ok, 0.0, NEG)
        c[:, C_CUM + 128 * d:C_CUM + 128 * d + 128] = ok
    GW = 64
    t = np.arange(SEQ)
    inv = (10000.0 ** (-np.arange(16, dtype=np.float32) / 16)).astype(np.float32)
    ang = np.concatenate([(t // GW).astype(np.float32)[:, None] * inv, (t % GW).astype(np.float32)[:, None] * inv], 1)
    cos, sin = np.cos(ang).T, np.sin(ang).T
    c[:, C_COS:C_COS + 256] = np.tile(cos, (4, 1))
    c[:, C_SIN:C_SIN + 256] = np.tile(np.concatenate([-sin, sin]), (2, 1))
    c[0, C_SEL] = c[2, C_SEL] = c[1, C_SEL + 1] = c[3, C_SEL + 1] = 1
    return c


def _q_order():
    heads = [(2 * p + a) * 4 + i for p in range(2) for i in range(4) for a in range(2)]
    return np.concatenate([np.arange(64 * x, 64 * x + 64) for x in heads])


def _panels(w):
    k, mm = w.shape
    p = w.reshape(k // 128, 128, mm // 128, 128).transpose(2, 1, 0, 3)
    if k < 1024:
        p = np.concatenate([p, np.zeros((p.shape[0], 128, 8 - k // 128, 128), np.float32)], 2)
    return p.reshape(-1, 128, 1024)


def _stream(w_ada, ffn_w1, ffn_w3, ffn_w2, w_in, w_br, w_out):
    P = plan()
    s = np.zeros((4 * P["blocks"], 128, 1024), np.float32)

    def put(key, panels):
        b = P[key][0]
        s[4 * b:4 * b + len(panels)] = panels

    def ada(g):
        l, n = g // ADA_GROUPS, g % ADA_GROUPS
        w = w_ada[l][:, 512 * n:512 * n + 512]
        return w.reshape(4, 2, 128, 512).transpose(0, 2, 1, 3).reshape(4, 128, 1024)

    def ada_run(key, n):
        b, (g0, _) = P[key][0], P["groups"][key]
        for i in range(n):
            s[4 * (b + i):4 * (b + i) + 4] = ada(g0 + i)

    qo = _q_order()
    for l in range(DEPTH):
        wi = w_in[l]
        if l == 0:
            ada_run(("ada", 0), 6)
        for f in range(2):
            at = 0
            for p, tiles in enumerate(PIECES):
                b = P[("up", l, f, p)][0]
                g0, rides = P[("rides", l, f, p)]
                cols = slice(128 * at, 128 * (at + tiles))
                w1, w3 = _panels(ffn_w1[l, f][:, cols]), _panels(ffn_w3[l, f][:, cols])
                for i in range(tiles // 2):
                    if rides:
                        s[4 * b:4 * b + 4] = ada(g0 + i)
                        b += 1
                    for k in range(2):
                        s[4 * b + 2 * k], s[4 * b + 2 * k + 1] = w1[2 * i + k], w3[2 * i + k]
                    b += 1
                put(("down", l, f, p), _panels(ffn_w2[l, f][cols]))
                at += tiles
            if f == 0:
                ada_run(("ada1", l), 1)
                parts = [_panels(wi[:, o:o + 1024]) for o in (ODN, ODN + 1024, ODN + 2048, OG)]
                put(("head", l), np.stack(parts, 1).reshape(-1, 128, 1024))
                for r, br in enumerate((2, 0, 1)):
                    wb = w_br[l, br]
                    if br == 0:
                        wb = wb[qo]
                    pr = np.stack([_panels(wi[:, OGZ + 1024 * br:OGZ + 1024 * br + 1024]), _panels(wb)], 1)
                    put(("br", l, r), pr.reshape(-1, 128, 1024))
                put(("kv", l), _panels(wi[:, OK:OK + 512]))
                put(("q", l), _panels(wi[:, OQ:OQ + 1024][:, qo]))
                parts = [_panels(wi[:, o:o + 1024]) for o in (O4, O5, O3)]
                put(("conv", l), np.stack(parts, 1).reshape(-1, 128, 1024))
                put(("out", l), _panels(w_out[l]))
            elif l == 0:
                ada_run(("ada2", 0), 2)
    return s


def _fm(v):
    return v.reshape(-1, 128).T


def _vectors(c, c_ctx, b_ada, norm_g, b_in, q_norm_g, k_norm_g, sc_conv, dn_conv, dn_norm_g, final_norm_g):
    v = np.zeros((128, NV), np.float32)
    for l in range(DEPTH):
        L, b = l * NVL, b_in[l]

        def put(at, x):
            v[:, L + at:L + at + x.shape[1]] = x

        put(V_KV, _fm(b[OK:OK + 512]))
        put(V_Q, _fm(b[OQ:OQ + 1024][_q_order()]))
        put(V_QG, np.concatenate([q_norm_g[l], q_norm_g[l]])[:, None])
        put(V_KG, np.concatenate([k_norm_g[l], k_norm_g[l]])[:, None])
        for n in range(DNH):
            at = V_HEAD + HV * n
            for j, o in enumerate((ODN, ODN + 1024, ODN + 2048, OG)):
                put(at + j, b[o + 128 * n:o + 128 * n + 128][:, None])
            for j in range(3):
                put(at + 4 + 3 * j, dn_conv[l][:, 1024 * j + 128 * n:1024 * j + 128 * n + 128].T)
        for n in range(KT):
            at = V_CONV + CV * n
            for j, o in enumerate((O4, O5, O3)):
                put(at + j, b[o + 128 * n:o + 128 * n + 128][:, None])
            put(at + 3, sc_conv[l][:, 128 * n:128 * n + 128].T)
        for r, br in enumerate((2, 0, 1)):
            put(V_GZ + 8 * r, _fm(b[OGZ + 1024 * br:OGZ + 1024 * br + 1024]))
        put(V_NG, _fm(norm_g[l].reshape(-1)))
        put(V_DNG, dn_norm_g[l][:, None])
        put(V_ADA, _fm(b_ada[l]))
    v[:, V_FG:V_FG + KT] = _fm(final_norm_g)
    v[:, V_C:V_C + 2 * KT:2] = _fm(c_ctx)
    v[:, V_C + 1:V_C + 2 * KT:2] = _fm(c[0])
    return v


def _rows(b_in, dn_dt_bias, dn_a_log):
    r = np.zeros((DEPTH, NR), np.float32)
    for l in range(DEPTH):
        r[l, R_AB:R_AB + 32] = b_in[l, OAB:OAB + 32]
        r[l, R_DT:R_DT + 16] = dn_dt_bias[l].reshape(-1)
        r[l, R_AL:R_AL + 16] = dn_a_log[l].reshape(-1)
    return np.ascontiguousarray(np.broadcast_to(r.reshape(1, -1), (128, DEPTH * NR)))


def kernel(**inputs):
    import concourse.bacc as bacc
    from concourse.bass_utils import run_bass_kernel_spmd

    a = {k: np.asarray(v) for k, v in inputs.items()}
    arrays = {
        "stream": _stream(*(a[k] for k in ("w_ada", "ffn_w1", "ffn_w3", "ffn_w2", "w_in", "w_br", "w_out"))),
        "h_in": np.ascontiguousarray(np.concatenate([a["ctx"][0], a["x"][0]]).T),
        "vecs": _vectors(*(a[k] for k in ("c", "c_ctx", "b_ada", "norm_g", "b_in", "q_norm_g", "k_norm_g", "sc_conv",
                                          "dn_conv", "dn_norm_g", "final_norm_g"))),
        "rows": _rows(a["b_in"], a["dn_dt_bias"], a["dn_a_log"]),
        "wab": np.ascontiguousarray(a["w_in"][:, :, OAB:OAB + 32].reshape(DEPTH, KT, 128, 32).transpose(2, 0, 1, 3)).reshape(128, -1),
        "consts": _tables(),
    }
    nc = bacc.Bacc("TRN2", target_bir_lowering=False, num_devices=1)
    aps = [nc.dram_tensor(k, v.shape, mybir.dt.float32, kind="ExternalInput").ap() for k, v in arrays.items()]
    out = nc.dram_tensor("out", (D, SEQ), mybir.dt.float32, kind="ExternalOutput").ap()
    build(nc, *aps, out)
    r = run_bass_kernel_spmd(nc, [arrays], core_ids=[0])
    return np.ascontiguousarray(np.asarray(r.results[0]["out"]).T)[None]
```

```python
from contextlib import ExitStack, contextmanager

import numpy as np
import concourse.bass as bass
from concourse import mybir

D = 1024
KT = D // 128
SEQ, CTX = 256, 256
T = CTX + SEQ
TC = T // 128
DEPTH = 2
HD = 64
NH, NKV = 16, 4
DNH = 8
DFF = 2816
FT = DFF // 128
EPS = 1e-6
NEG = -1.0e30
PIECES = (8, 8, 6)
assert sum(PIECES) == FT

OQ, OK, OV = 0, 1024, 1280
O3, O4, O5 = 1536, 2560, 3584
ODN, OG, OAB, OGZ = 4608, 7680, 8704, 8736
D_IN = 11808

V_KV = 0
V_Q = 4
V_QG, V_KG = 12, 13
V_HEAD = 14
HV = 13
V_CONV = V_HEAD + DNH * HV
CV = 6
V_GZ = V_CONV + KT * CV
V_NG = V_GZ + 24
V_DNG = V_NG + 24
V_ADA = V_DNG + 1
NVL = V_ADA + 72
V_FG = 2 * NVL
V_C = V_FG + KT
NV = V_C + 2 * KT

C_ID, C_OFF, C_ONE, C_BLK, C_PERM = 0, 128, 256, 384, 512
C_LV = 640
C_NM = C_LV + 7 * 128
C_CUM = C_NM + 256
C_COS, C_SIN = C_CUM + 256, C_CUM + 512
C_SEL = C_CUM + 768
NC = C_SEL + 2

R_AB, R_DT, R_AL = 0, 32, 48
NR = 64

HB_G, HB_GC, HB_NEG, HB_BETA, HB_KD, HB_TOT = range(6)
HBN = 48

ADA_GROUPS = 18


def plan():
    at, blk, gblk = {}, 0, 0

    def take(key, nblocks, gemm=True):
        nonlocal blk, gblk
        at[key] = (blk, gblk)
        blk += nblocks
        gblk += nblocks if gemm else 0

    groups = 0
    at["groups"] = {}

    def ada(key, n):
        nonlocal groups
        at["groups"][key] = (groups, n)
        groups += n
        take(key, n, False)

    for l in range(DEPTH):
        if l == 0:
            ada(("ada", 0), 6)
        for f in range(2):
            for p, tiles in enumerate(PIECES):
                n = tiles // 2
                rides = n if (f == 0 or (l == 0 and p == 0)) else 0
                at[("rides", l, f, p)] = (groups, rides)
                groups += rides
                at[("up", l, f, p)] = (blk, gblk)
                blk += n + rides
                gblk += n
                take(("down", l, f, p), 2)
            if f == 0:
                ada(("ada1", l), 1)
                take(("head", l), DNH)
                take(("kv", l), 1)
                take(("br", l, 0), 4)
                take(("q", l), 2)
                take(("br", l, 1), 4)
                take(("conv", l), 6)
                take(("br", l, 2), 4)
                take(("out", l), 2)
            elif l == 0:
                ada(("ada2", l), 2)
    assert groups == DEPTH * ADA_GROUPS
    at["blocks"], at["gblocks"] = blk, gblk
    return at


def build(nc, stream, h_in, vecs_in, rows_in, wab_in, consts_in, out):
    f32, f32r = mybir.dt.float32, mybir.dt.float32r
    ALU, ACT, AX = mybir.AluOpType, mybir.ActivationFunctionType, mybir.AxisListType
    ds = bass.ds
    P = plan()
    NB = P["blocks"]

    ctx = ExitStack()
    with ctx:
        def sb(name, shape, dt=f32):
            return ctx.enter_context(nc.sbuf_tensor(name, shape, dt))

        def sem(name):
            return ctx.enter_context(nc.semaphore(name))

        raw = sb("raw", [128, 4, 1024])
        whi = sb("whi", [128, 4, 1024], f32r)
        wlo = sb("wlo", [128, 4, 1024], f32r)
        h = sb("h", [128, KT, T])
        uh = sb("uh", [128, KT, T], f32r)
        ul = sb("ul", [128, KT, T], f32r)
        bh = sb("bh", [128, KT, T], f32r)
        bl = sb("bl", [128, KT, T], f32r)
        m = sb("m", [128, KT * T])
        cst = sb("cst", [128, NC])
        vec = sb("vec", [128, NV])
        rows = sb("row_vectors", [128, DEPTH, NR])
        kraw = sb("kraw", [128, T])
        idr = sb("idr", [128, 128], f32r)
        nidr = sb("nidr", [128, 128], f32r)
        cstat = sb("cstat", [128, KT, 128], f32r)
        csil = sb("csil", [128, KT, 2])
        mod = sb("mod", [128, DEPTH * 72, 2])
        normA = sb("normA", [128, KT, 2])
        hgate = sb("hgate", [128, KT, 2])
        tab = sb("tab", [128, DNH, HBN])
        hv = sb("hv", [128, HV])
        hb = sb("hb", [128, HBN])
        stat = sb("stat", [128, 32])
        scr = sb("scr", [128, 6160])
        scr_r = sb("scr_r", [128, 4, 2 * 512], f32r)
        bank = [ctx.enter_context(nc.psum_tensor(f"bank{i}", [128, 512], f32)) for i in range(8)]

        wab = m[:, 0:KT * 32]
        m3 = m[:, :].rearrange("p (k t) -> p k t", k=KT)
        ident = cst[:, C_ID:C_ID + 128]
        ones = cst[:, C_ONE:C_ONE + 128]

        def s_(a, n):
            return scr[:, a:a + n]

        nsq = s_(0, 1024).rearrange("p (a t) -> p a t", a=2)
        nvar, nrs = s_(1024, 512), s_(1536, 512)
        nut = s_(2048, 1024).rearrange("p (a t) -> p a t", a=2)
        sil = s_(3072, 1024).rearrange("p (a t) -> p a t", a=2)
        hbuf = s_(4096, 1024).rearrange("p (a t) -> p a t", a=2)
        arow = scr[0:4, 5120:5632]
        SM = s_(5120, 1024)

        pre = s_(0, 3 * 516).rearrange("p (j s t) -> p j s t", j=3, s=2)
        eg = s_(0, 1024).rearrange("p (d t) -> p d t", d=2)
        qkv = s_(1548, 1536).rearrange("p (j t) -> p j t", j=3)
        gate = s_(3084, 512)
        ktok = s_(3596, 512)
        vtok = s_(4108, 512)
        Gs = s_(4620, 512)
        KQs = s_(5132, 512)
        St = s_(5644, 512).rearrange("p (b d e) -> p b d e", b=2, d=2)
        Rr = s_(4620, 256).rearrange("p (d e) -> p d e", d=2)
        vn = s_(4876, 256).rearrange("p (d e) -> p d e", d=2)
        vd = s_(5132, 256).rearrange("p (d e) -> p d e", d=2)
        hsq = s_(4620, 1024).rearrange("p (d t) -> p d t", d=2)
        gated = s_(0, 512)
        eo = hsq
        hrs = s_(0, 1024).rearrange("p (d t) -> p d t", d=2)
        DT = m[:, 0:1024].rearrange("p (d t) -> p d t", d=2)
        Qt = m[:, 1024:2048].rearrange("p (d t) -> p d t", d=2)
        AT = m[:, 2048:3072].rearrange("p (d t) -> p d t", d=2)
        IT = m[:, 3072:4096].rearrange("p (d t) -> p d t", d=2)
        XTf = DT
        ATr, X, XT, Pm = (scr_r[:, k, :].rearrange("p (d t) -> p d t", d=2) for k in range(4))
        wabh, wabl = scr_r[:, 0, 0:256], scr_r[:, 0, 256:512]

        kT = s_(0, 1024).rearrange("p (a t) -> p a t", a=2)
        vt = s_(1024, 1024).rearrange("p (a c f) -> p a c f", a=2, c=TC)
        qx = s_(2048, 2048).rearrange("p (a t) -> p a t", a=4)
        asq, ars = s_(4096, 512), s_(4608, 512)
        asw, ax = s_(5120, 512), s_(5632, 512)
        Pb = s_(4096, 1024).rearrange("p (a t) -> p a t", a=2)
        PT = s_(5120, 1024).rearrange("p (a t) -> p a t", a=2)
        c4 = s_(0, 512)
        cpr = s_(512, 516).rearrange("p (s t) -> p s t", s=2)
        cy = s_(1028, 512)
        cz = s_(1540, 1024).rearrange("p (a t) -> p a t", a=2)
        cvec = s_(2600, 4 * CV)

        raw_in = [sem("raw_in0"), sem("raw_in1")]
        hi_ready, lo_ready, panel_done = sem("hi_ready"), sem("lo_ready"), sem("panel_done")
        pair_done = [sem("pair_done0"), sem("pair_done1")]
        consts_loaded, vecs_loaded, h_loaded, wab_loaded = (sem(n) for n in (
            "consts_loaded", "vecs_loaded", "h_loaded", "wab_loaded"))
        setup_act, setup_dve = sem("setup_act"), sem("setup_dve")
        ada_row, ada_turned, mod_ready = (sem(n) for n in ("ada_row", "ada_turned", "mod_ready"))
        sq_ready, sq_used, var_ready, rstd_ready, ut_ready, uh_ready, u_ready = (sem(n) for n in (
            "sq_ready", "sq_used", "var_ready", "rstd_ready", "ut_ready", "uh_ready", "u_ready"))
        sil_ready, hid_hi, hid_ready = sem("sil_ready"), sem("hid_hi"), sem("hid_ready")
        wab_reloaded, wab_hi, wab_lo = sem("wab_reloaded"), sem("wab_hi"), sem("wab_lo")
        ab_sum, ab_z, ab_exp, g_ready, gc_sum, gc_exp, tab_ready = (sem(n) for n in (
            "ab_sum", "ab_z", "ab_exp", "g_ready", "gc_sum", "gc_exp", "tab_ready"))
        E = {n: sem(n) for n in (
            "hv_ready", "hb_ready", "pre_ready", "conv_ready", "silu_ready", "hsq_ready", "l2_sum", "l2_var", "l2_rstd",
            "kn_ready", "qn_ready", "kv_turned", "ktok_ready", "vtok_ready", "gram", "kq_ready",
            "gs_ready", "gc_row", "dm_ready", "dt_ready", "eg_ready", "qt_ready", "at_ready", "atr_ready", "it_ready",
            "xt0_ready", "xt0_turned", "x0_ready", "p_sum", "pm_ready", "x_sum", "x_ready", "xt_ready",
            "ks_sum", "r_ready", "y_sum", "vn_ready", "vd_ready", "ds_sum", "s_ready", "o_sum", "osq_ready",
            "on_sum", "on_var", "on_rstd", "on_ready", "bh_ready", "head_ready")}
        dve_step, act_step = sem("dve_step"), sem("act_step")
        A = {n: sem(n) for n in (
            "a_x", "a_sq", "a_sum", "a_var", "a_rstd", "a_norm", "a_swap", "a_done", "a_vx", "a_vturn", "a_vtok",
            "s_sum", "s_max", "s_exp", "s_scaled", "s_turned", "s_pt", "s_pv", "att_hi", "att_ready")}
        C = {n: sem(n) for n in ("c_vec", "c_p4", "c_out", "c_hi", "c_ready", "br_gate", "mh_ready", "mx_ready")}
        out_ready, out_stored = sem("out_ready"), sem("out_stored")

        block = ctx.enter_context(nc.Block())

        class Steps:

            def __init__(self, eng, s):
                self.eng, self.s, self.base, self.k = eng, s, 0, 0

            def do(self, ins):
                ins.then_inc(self.s, 1)
                self.k += 1

            def sync(self):
                self.eng.wait_ge(self.s, self.base + self.k)

            @contextmanager
            def loop(self, start, stop, per):
                base, self.k = self.base + self.k, 0
                with self.eng.Fori(start, stop) as i:
                    self.base = base + (i - start) * per
                    yield i
                    assert self.k == per, (self.k, per)
                self.base, self.k = base + (stop - start) * per, 0

        def wait(eng, s, n):
            if not (isinstance(n, int) and n <= 0):
                eng.wait_ge(s, n)

        def have(eng, s, n):
            eng.wait_ge(s, n + 1)

        def conds(c0):
            return [(k, a, b) for k, a, b in ((0, 0, CTX), (1, CTX, T)) if a >= c0]

        def bc(ap, n, w):
            return ap.rearrange("p (a w) -> p a w", a=1).broadcast_to([128, n, w])

        def c4d(ap):
            return ap.rearrange("p (c t) -> p c t", c=TC)

        def modc(l, jj):
            return l * 72 + jj * 8

        def chunk(d, s):
            return (0, 1, 2, 3)[s] if d == 0 else (1, 0, 3, 2)[s]

        def hcol(kind, d, c):
            n = (kind * 2 + d) * 4 + c
            return slice(n, n + 1)

        def att_units(l):
            kinds = ((2, 3) if l == DEPTH - 1 else (0, 2, 3))
            return [(j, a, k) for j in range(4) for a in range(2) for k in kinds]

        def att_units_before(l, p):
            return sum(2 * len(att_units(k)) for k in range(l)) + p * len(att_units(l))

        @block.sync
        def _(sp):
            sp.dma_start(cst[:, :], consts_in).then_inc(consts_loaded, 16)
            sp.dma_start(vec[:, :], vecs_in).then_inc(vecs_loaded, 16)

            def load(b, r):
                sp.dma_start(raw[:, 2 * r:2 * r + 2, :],
                             stream[ds(4 * b + 2 * r, 2), :, :].rearrange("g p n -> p g n")).then_inc(raw_in[r], 16)

            load(0, 0)
            load(0, 1)
            sp.dma_start(h[:, :, :], h_in.rearrange("(k p) t -> p k t", p=128)).then_inc(h_loaded, 16)
            sp.dma_start(wab, wab_in[:, 0:KT * 32]).then_inc(wab_loaded, 16)
            sp.dma_start(rows[:, :, :].rearrange("p l n -> p (l n)"), rows_in).then_inc(wab_loaded, 16)
            with sp.Fori(1, NB) as b:
                for r in range(2):
                    sp.wait_ge(lo_ready, 4 * (b - 1) + 2 * r + 2)
                    load(b, r)
            for t in range(KT):
                sp.wait_ge(out_ready, t + 1)
                sp.dma_start(out.rearrange("(k p) t -> p k t", p=128)[:, t, :], m3[:, t, 0:SEQ]).then_inc(out_stored, 16)
            sp.wait_ge(out_stored, 16 * KT)

        @block.gpsimd
        def _(pool):
            for l in range(1, DEPTH):
                pool.wait_ge(C["mx_ready"], 8 * l)
                pool.dma_start(wab, wab_in[:, l * KT * 32:(l + 1) * KT * 32]).then_inc(wab_reloaded, 16)

        @block.scalar
        def _(act):
            steps = Steps(act, act_step)

            def split(B, j):
                if isinstance(B, int) and B >= NB:
                    return
                if j % 2 == 0:
                    act.wait_ge(raw_in[j // 2], 16 * (B + 1))
                if not (isinstance(B, int) and B == 0):
                    act.wait_ge(panel_done, 4 * (B - 1) + j + 1)
                act.activation(whi[:, j, :], raw[:, j, :], ACT.Copy).then_inc(hi_ready, 1)

            def log_exp():
                act.preload_act_table_set("natural_log_exp_and_others")

            def rsqrt(out_, in_, ready):
                steps.do(act.activation(out_, in_, ACT.Ln))
                steps.sync()
                act.activation(out_, out_, ACT.Exp, scale=-0.5).then_inc(ready, 1)

            act.sem_inc(ada_row, 1)
            act.wait_ge(consts_loaded, 16)
            act.activation(idr[:, :], ident, ACT.Copy)
            act.activation(nidr[:, :], ident, ACT.Copy, scale=-1.0).then_inc(setup_act, 1)
            act.wait_ge(vecs_loaded, 16)
            steps.do(act.activation(csil[:, :, :], vec[:, V_C:V_C + 16].rearrange("p (k c) -> p k c", c=2), ACT.Silu))
            steps.sync()
            act.wait_ge(setup_dve, 1)
            act.activation(cstat[:, :, 0:2], csil[:, :, :], ACT.Copy).then_inc(setup_act, 1)
            for j in range(4):
                split(0, j)

            def ada_panels(B):
                for j in range(4):
                    split(B + 1, j)

            def ada_evac(n, B):
                act.wait_ge(panel_done, 4 * B + 4)
                have(act, ada_turned, n)
                act.activation(arow[:, :], bank[4][0:4, :], ACT.Copy).then_inc(ada_row, 1)

            def ada_only(key):
                B0, _ = P[key]
                g0, n = P["groups"][key]
                with act.Fori(0, n) as i:
                    ada_panels(B0 + i)
                    ada_evac(g0 + i, B0 + i)

            def norm(n, l, j, c0, hcount):
                hcount(act)
                for t in range(KT):
                    wait(act, sq_used, 8 * n + t - 1)
                    act.activation(nsq[:, t % 2, c0:T], h[:, t, c0:T], ACT.Square).then_inc(sq_ready, 1)
                log_exp()
                act.wait_ge(var_ready, n + 1)
                rsqrt(nrs[:, c0:T], nvar[:, c0:T], rstd_ready)
                if j is None:
                    return
                sh = modc(l, 3 * j)
                for t in range(KT):
                    act.wait_ge(ut_ready, 8 * n + t + 1)
                    for k, a, b in conds(c0):
                        last = act.activation(uh[:, t, a:b], nut[:, t % 2, a:b], ACT.Identity,
                                              bias=mod[:, sh + t, k:k + 1])
                    last.then_inc(uh_ready, 1)

            def ffn(l, f):
                c0 = CTX if l == DEPTH - 1 and f == 1 else 0
                occ = 2 * l + f
                tile0 = occ * FT
                for p, tiles in enumerate(PIECES):
                    B0, G0 = P[("up", l, f, p)]
                    g0, rides = P[("rides", l, f, p)]
                    per = 2 if rides else 1
                    act.wait_ge(panel_done, 4 * B0)
                    with act.Fori(0, tiles // 2) as i:
                        B, G, n0 = B0 + per * i, G0 + i, tile0 + 2 * i
                        if rides:
                            ada_panels(B)
                            ada_evac(g0 + i, B)
                            B = B + 1
                        for k in range(2):
                            split(B + 1, 2 * k)
                            act.wait_ge(panel_done, 4 * B + 2 * k + 1)
                            have(act, pair_done[k], G)
                            act.activation(sil[:, k, c0:T], bank[2 * k][:, c0:T], ACT.Silu).then_inc(sil_ready, 1)
                            split(B + 1, 2 * k + 1)
                            have(act, pair_done[k], G + 1)
                            act.activation(bh[:, ds(2 * i + k, 1), c0:T].rearrange("p a t -> p (a t)"), hbuf[:, k, c0:T],
                                           ACT.Copy).then_inc(hid_hi, 1)
                    tile0 += tiles
                    B0, _ = P[("down", l, f, p)]
                    if B0 + 2 < NB:
                        with act.Fori(0, 2) as i:
                            for j in range(4):
                                split(B0 + i + 1, j)
                    else:
                        for j in range(4):
                            split(B0 + 1, j)

            def ab(l):
                if l:
                    act.wait_ge(wab_reloaded, 16 * l)
                else:
                    act.wait_ge(wab_loaded, 32)
                act.activation(wabh, wab, ACT.Copy).then_inc(wab_hi, 1)
                act.wait_ge(ab_z, 2 * l + 1)
                act.activation(SM[:, 128:192], SM[:, 64:128], ACT.Exp)
                act.activation(SM[:, 192:256], SM[:, 960:1024], ACT.Exp, scale=-1.0)
                steps.do(act.activation(SM[:, 256:272], rows[:, l, R_AL:R_AL + 16], ACT.Exp))
                steps.sync()
                act.activation(SM[:, 320:384], SM[:, 128:192], ACT.Ln, bias=1.0).then_inc(ab_exp, 1)
                act.wait_ge(ab_z, 2 * l + 2)
                act.activation(SM[:, 640:704], SM[:, 448:512], ACT.Exp)
                act.activation(SM[:, 704:768], SM[:, 512:576], ACT.Exp)
                act.activation(SM[:, 768:832], SM[:, 576:640], ACT.Exp).then_inc(ab_exp, 1)

            def prep(l, b):
                c0 = CTX if l == DEPTH - 1 else 0
                s0 = c0 // CTX
                o = l * DNH + b
                act.wait_ge(E["hv_ready"], o + 1)
                act.wait_ge(panel_done, 4 * (P[("head", l)][0] + b) + 3)
                seg = lambda ap: ap.rearrange("p (s t) -> p s t", s=2)
                for j in (1, 0, 2):
                    a = s0 if j == 0 else 0
                    act.activation(pre[:, j, a:2, 1:257], seg(bank[j][:, :])[:, a:2, :], ACT.Identity,
                                   bias=hv[:, j:j + 1]).then_inc(E["pre_ready"], 1)

            def prep_silu(l, b, n):
                c0 = CTX if l == DEPTH - 1 else 0
                o = l * DNH + b
                j = (1, 0, 2)[n]
                a = c0 if j == 0 else 0
                x = kraw if j == 1 else qkv[:, j, :]
                act.wait_ge(E["conv_ready"], 3 * o + n + 1)
                act.activation(x[:, a:T], x[:, a:T], ACT.Silu).then_inc(E["silu_ready"], 1)
                if j != 2:
                    act.wait_ge(E["silu_ready"], 3 * o + n + 1)
                    act.activation(hsq[:, n, a:T], x[:, a:T], ACT.Square).then_inc(E["hsq_ready"], 1)

            def prep_rsqrt(l, b, n):
                c0 = CTX if l == DEPTH - 1 else 0
                a = c0 if n else 0
                act.wait_ge(E["l2_var"], 2 * (l * DNH + b) + n + 1)
                rsqrt(hrs[:, n, a:T], hrs[:, n, a:T], E["l2_rstd"])

            def gate_in(l, b):
                B0, G0 = P[("head", l)]
                c0 = CTX if l == DEPTH - 1 else 0
                act.wait_ge(panel_done, 4 * (B0 + b) + 4)
                act.activation(gate[:, c0:T], bank[3][:, c0:T], ACT.Identity, bias=hv[:, 3:4]).then_inc(pair_done[1], 1)

            def turned(l, b):
                act.wait_ge(E["kv_turned"], 2 * (l * DNH + b) + 2)
                act.activation(ktok, bank[4][:, :], ACT.Copy).then_inc(E["ktok_ready"], 1)

            def head(l, b, follow):
                c0 = CTX if l == DEPTH - 1 else 0
                B = P[("head", l)][0] + b
                o = l * DNH + b - 1
                for d in range(2):
                    act.wait_ge(E["dm_ready"], 2 * o + d + 1)
                    act.activation(DT[:, d, :], DT[:, d, :], ACT.Exp).then_inc(E["dt_ready"], 1)
                for d in range(2):
                    act.activation(eg[:, d, c0:T], bank[4 + d][:, c0:T], ACT.Exp).then_inc(E["eg_ready"], 1)
                act.wait_ge(E["gram"], 2 * o + 2)
                act.activation(KQs[:, c0:T], bank[6][:, c0:T], ACT.Copy).then_inc(E["kq_ready"], 1)
                for d in range(2):
                    act.wait_ge(E["at_ready"], 2 * o + d + 1)
                    act.activation(ATr[:, d, :], AT[:, d, :], ACT.Copy).then_inc(E["atr_ready"], 1)
                    act.wait_ge(E["xt0_turned"], 2 * o + d + 1)
                    act.activation(X[:, d, :], bank[6 + d][:, :], ACT.Copy).then_inc(E["x_ready"], 1)
                for v in range(1, 7):
                    for d in range(2):
                        x = 22 * o + (4 * (v - 1) + 2 * d if v < 6 else 20 + d)
                        act.wait_ge(E["x_sum"], x + 1)
                        act.activation(X[:, d, :], bank[6 + d][:, :], ACT.Copy).then_inc(E["x_ready"], 1)
                        if v < 6:
                            act.wait_ge(E["x_sum"], x + 2)
                            act.activation(XT[:, d, :], bank[4 + d][:, :], ACT.Copy).then_inc(E["xt_ready"], 1)
                        if d == 0 and v == 1:
                            split(B + 1, 0)
                        if d == 0 and v == 5:
                            split(B + 1, 1)
                        if d == 1 and v == 1 and follow:
                            prep(l, b)
                        if d == 1 and 2 <= v < 5 and follow:
                            prep_silu(l, b, v - 2)
                        if v == 5 and d == 1:
                            have(act, pair_done[1], P[("head", l)][1] + b)
                            act.activation(gate[:, c0:T], gate[:, c0:T], ACT.Silu)
                log_exp()
                for d in range(2):
                    act.wait_ge(E["p_sum"], 18 * o + 12 + d + 1)
                    act.activation(XT[:, d, :], bank[4 + d][:, :], ACT.Copy).then_inc(E["xt_ready"], 1)
                for d in range(2):
                    act.wait_ge(E["p_sum"], 18 * o + 14 + d + 1)
                    act.activation(Pm[:, d, :], bank[6 + d][:, :], ACT.Copy).then_inc(E["pm_ready"], 1)
                split(B + 1, 2)
                for s in range(TC - 1):
                    for d in range(2):
                        c = chunk(d, s)
                        act.wait_ge(E["vn_ready"], 8 * o + 2 * s + d + 1)
                        act.activation(vd[:, d, :], vn[:, d, :], ACT.Copy,
                                       scale=hb[:, hcol(HB_KD, d, c)]).then_inc(E["vd_ready"], 1)
                    if s < 2 and follow:
                        prep_rsqrt(l, b, s)
                act.wait_ge(E["o_sum"], o + 1)
                act.activation(eo[:, 0, c0:T], bank[6][:, c0:T], ACT.Square).then_inc(E["osq_ready"], 1)
                if follow:
                    turned(l, b)
                act.wait_ge(E["on_var"], o + 1)
                rsqrt(eo[:, 1, c0:T], eo[:, 1, c0:T], E["on_rstd"])
                split(B + 1, 3)
                act.wait_ge(E["on_ready"], o + 1)
                act.activation(bh[:, ds(b - 1, 1), c0:T].rearrange("p a t -> p (a t)"), gated[:, c0:T],
                               ACT.Copy).then_inc(E["bh_ready"], 1)
                if follow:
                    gate_in(l, b)

            def heads(l):
                B0 = P[("head", l)][0]
                act.wait_ge(panel_done, 4 * B0)
                act.wait_ge(tab_ready, l + 1)
                prep(l, 0)
                split(B0 + 1, 0)
                for n in range(3):
                    prep_silu(l, 0, n)
                log_exp()
                for n in range(2):
                    prep_rsqrt(l, 0, n)
                split(B0 + 1, 1)
                turned(l, 0)
                split(B0 + 1, 2)
                split(B0 + 1, 3)
                gate_in(l, 0)
                with steps.loop(1, DNH - 1, 3) as b:
                    head(l, b, True)
                head(l, DNH - 1, True)
                head(l, DNH, False)

            def branch(l, r):
                B0, G0 = P[("br", l, r)]
                c0 = CTX if l == DEPTH - 1 else 0
                n0 = (3 * l + r) * 8
                with act.Fori(0, 4) as i:
                    for k in range(2):
                        split(B0 + i + 1, 2 * k)
                        act.wait_ge(panel_done, 4 * (B0 + i) + 2 * k + 1)
                        have(act, pair_done[k], G0 + i)
                        act.activation(sil[:, k, c0:T], bank[2 * k][:, c0:T], ACT.Sigmoid,
                                       bias=vec[:, ds(l * NVL + V_GZ + 8 * r + 2 * i + k, 1)]).then_inc(C["br_gate"], 1)
                        split(B0 + i + 1, 2 * k + 1)

            def qk_norm(na, j, bcol, c0):
                act.activation(ax[:, c0:T], bank[j][:, c0:T], ACT.Identity, bias=vec[:, bcol:bcol + 1]).then_inc(A["a_x"], 1)
                act.wait_ge(A["a_x"], na + 1)
                act.activation(asq[:, c0:T], ax[:, c0:T], ACT.Square).then_inc(A["a_sq"], 1)
                log_exp()
                act.wait_ge(A["a_var"], na + 1)
                rsqrt(ars[:, c0:T], ars[:, c0:T], A["a_rstd"])

            def attention_kv(l):
                B0, G0 = P[("kv", l)]
                L = l * NVL
                na = 10 * l
                have(act, E["head_ready"], DNH * (l + 1))
                act.wait_ge(panel_done, 4 * B0 + 4)
                for j in range(2):
                    wait(act, A["a_done"], na)
                    qk_norm(na, j, L + V_KV + j, 0)
                    na += 1
                for j in range(2):
                    n = 2 * l + j
                    if j:
                        act.wait_ge(A["a_vturn"], n)
                    else:
                        act.wait_ge(A["a_done"], na)
                    act.activation(ax, bank[2 + j][:, :], ACT.Identity, bias=vec[:, L + V_KV + 2 + j:L + V_KV + 3 + j]).then_inc(A["a_vx"], 1)
                act.wait_ge(A["a_vturn"], 2 * l + 2)

            def attention(l):
                c0 = CTX if l == DEPTH - 1 else 0
                L = l * NVL
                na = 10 * l + 2
                nu = att_units_before(l, 0)
                for p in range(2):
                    B, G = P[("q", l)][0] + p, P[("q", l)][1] + p
                    for j in range(4):
                        split(B + 1, j)
                        wait(act, A["a_done"], na)
                        qk_norm(na, j, L + V_Q + 4 * p + j, c0)
                        na += 1
                    act.wait_ge(A["a_done"], na)
                    units = att_units(l)

                    def evac_pt(u):
                        act.wait_ge(A["s_turned"], nu + u + 1)
                        act.activation(PT[:, u % 2, :], bank[6 + u % 2][:, :], ACT.Copy).then_inc(A["s_pt"], 1)

                    for u, (j, a, lat) in enumerate(units):
                        act.wait_ge(A["s_max"], nu + u + 1)
                        if u >= 2:
                            act.wait_ge(A["s_turned"], nu + u - 1)
                        for q in range(1 if lat else 2):
                            w = 512 if lat else 256
                            st = 8 * (u % 2) + q
                            last = act.activation(Pb[:, u % 2, q * w:(q + 1) * w], bank[4 + u % 2][:, q * w:(q + 1) * w], ACT.Exp,
                                                  scale=HD ** -0.5, bias=stat[:, st + 2:st + 3], accum_out=stat[:, st + 4:st + 5])
                        last.then_inc(A["s_exp"], 1)
                        if u:
                            evac_pt(u - 1)
                    evac_pt(len(units) - 1)
                    nu += len(units)
                    for j in range(4):
                        act.wait_ge(A["s_pv"], nu)
                        act.activation(bh[:, 4 * p + j, c0:T], bank[j][:, c0:T], ACT.Copy).then_inc(A["att_hi"], 1)

            def conv(l):
                B0, G0 = P[("conv", l)]
                c0 = CTX if l == DEPTH - 1 else 0
                with steps.loop(0, 2, 0) as i:
                    B = B0 + 3 * i
                    n0 = 8 * l + 4 * i
                    for t in range(4):
                        q = 3 * t
                        split(B + q // 4 + 1, q % 4)
                        act.wait_ge(panel_done, 4 * B + q + 1)
                        act.wait_ge(C["c_vec"], 2 * l + i + 1)
                        have(act, C["c_out"], n0 + t)
                        act.activation(c4[:, c0:T], bank[q % 4][:, c0:T], ACT.Identity,
                                       bias=cvec[:, t * CV:t * CV + 1]).then_inc(C["c_p4"], 1)
                        split(B + (q + 1) // 4 + 1, (q + 1) % 4)
                        split(B + (q + 2) // 4 + 1, (q + 2) % 4)
                        have(act, C["c_out"], n0 + t + 1)
                        act.activation(bh[:, ds(4 * i + t, 1), c0:T].rearrange("p a t -> p (a t)"), cz[:, t % 2, c0:T],
                                       ACT.Copy).then_inc(C["c_hi"], 1)

            def project_out(l):
                B0, G0 = P[("out", l)]
                c0 = CTX if l == DEPTH - 1 else 0
                act.wait_ge(panel_done, 4 * B0)
                have(act, pair_done[1], G0)
                for t in range(KT):
                    act.activation(uh[:, t, c0:T], m3[:, t, c0:T], ACT.Copy).then_inc(C["mh_ready"], 1)
                with act.Fori(0, 2) as i:
                    for j in range(4):
                        split(B0 + i + 1, j)

            ada_only(("ada", 0))
            n = 0
            for l in range(DEPTH):
                c_last = CTX if l == DEPTH - 1 else 0
                norm(n, l, 0, 0, (lambda e: e.wait_ge(h_loaded, 16)) if l == 0 else (lambda e: have(e, pair_done[1], P[("down", 0, 1, 2)][1] + 2)))
                ffn(l, 0)
                ada_only(("ada1", l))
                norm(n + 1, l, 1, 0, lambda e: have(e, pair_done[1], P[("down", l, 0, 2)][1] + 2))
                ab(l)
                heads(l)
                attention_kv(l)
                branch(l, 0)
                attention(l)
                branch(l, 1)
                conv(l)
                branch(l, 2)
                project_out(l)
                norm(n + 2, l, 2, c_last, lambda e: have(e, pair_done[1], P[("out", l)][1] + 2))
                ffn(l, 1)
                if l == 0:
                    ada_only(("ada2", 0))
                n += 3
            norm(n, None, None, CTX, lambda e: have(e, pair_done[1], P["gblocks"]))

        @block.vector
        def _(dve):
            steps = Steps(dve, dve_step)
            stt = dve.scalar_tensor_tensor

            def split(B, j):
                if isinstance(B, int) and B >= NB:
                    return
                dve.wait_ge(hi_ready, 4 * B + j + 1)
                dve.tensor_tensor(wlo[:, j, :], raw[:, j, :], whi[:, j, :].bitcast(f32), ALU.subtract).then_inc(lo_ready, 1)

            for s in (*pair_done, mod_ready, E["head_ready"], C["c_out"]):
                dve.sem_inc(s, 1)
            dve.memset(cstat[:, :, :].bitcast(f32), 0.0).then_inc(setup_dve, 1)
            dve.wait_ge(setup_act, 2)
            dve.wait_ge(setup_dve, 1)
            dve.tensor_tensor(cstat[:, :, 2:4], csil[:, :, :], cstat[:, :, 0:2].bitcast(f32), ALU.subtract).then_inc(setup_dve, 1)
            for j in range(4):
                split(0, j)

            def ada_panels(B):
                for j in range(4):
                    split(B + 1, j)

            def ada_mod(g, l, local):
                have(dve, ada_turned, g + 1)
                b0 = l * NVL + V_ADA + 4 * local
                bias = vec[:, ds(b0, 4)].rearrange("p (a b) -> p a b", b=1).broadcast_to([128, 4, 2])
                dve.tensor_tensor(mod[:, ds(4 * g, 4), :], bank[5][:, 0:8].rearrange("p (a b) -> p a b", b=2), bias,
                                  ALU.add).then_inc(mod_ready, 1)

            def ada_only(key):
                B0, _ = P[key]
                g0, n = P["groups"][key]
                with dve.Fori(0, n) as i:
                    ada_panels(B0 + i)
                    ada_mod(g0 + i, g0 // ADA_GROUPS, (g0 % ADA_GROUPS) + i)

            def norm(n, l, j, c0):
                if j is not None:
                    have(dve, mod_ready, ADA_GROUPS * l + 6 * (j + 1))
                    sc = modc(l, 3 * j + 1)
                    g = vec[:, l * NVL + V_NG + 8 * j:l * NVL + V_NG + 8 * j + 8]
                    g = g.rearrange("p (a b) -> p a b", b=1).broadcast_to([128, KT, 2])
                    stt(out=normA[:, :, :], in0=mod[:, sc:sc + 8, :], scalar=1.0, in1=g, op0=ALU.add, op1=ALU.mult)
                    gt = modc(l, 3 * j + 2)
                    steps.do(dve.tensor_scalar(hgate[:, :, :], mod[:, gt:gt + 8, :], 1.0 if j == 1 else 0.5, None, ALU.mult))
                    sh = modc(l, 3 * j)
                dve.wait_ge(sq_used, 8 * n + 8)
                dve.tensor_scalar(nvar[:, c0:T], bank[6][:, c0:T], 1.0 / D, EPS, ALU.mult, ALU.add).then_inc(var_ready, 1)
                dve.wait_ge(rstd_ready, n + 1)
                steps.sync()

                def low(t):
                    dve.wait_ge(uh_ready, 8 * n + t + 1)
                    for k, a, b in conds(c0):
                        last = stt(out=ul[:, t, a:b], in0=nut[:, t % 2, a:b], scalar=mod[:, sh + t, k:k + 1],
                                   in1=uh[:, t, a:b].bitcast(f32), op0=ALU.add, op1=ALU.subtract)
                    last.then_inc(u_ready, 1)

                for t in range(KT):
                    if j is None:
                        f = vec[:, V_FG + t:V_FG + t + 1]
                        stt(out=m3[:, t, 0:SEQ], in0=h[:, t, CTX:T], scalar=f, in1=nrs[:, CTX:T],
                            op0=ALU.mult, op1=ALU.mult).then_inc(out_ready, 1)
                        continue
                    wait(dve, u_ready, 8 * n + t - 1)
                    for k, a, b in conds(c0):
                        last = stt(out=nut[:, t % 2, a:b], in0=h[:, t, a:b], scalar=normA[:, t, k:k + 1],
                                   in1=nrs[:, a:b], op0=ALU.mult, op1=ALU.mult)
                    last.then_inc(ut_ready, 1)
                    if t:
                        low(t - 1)
                if j is not None:
                    low(KT - 1)

            def residual(B, G, t0, c0):
                for j in range(4):
                    split(B + 1, j)
                    dve.wait_ge(panel_done, 4 * B + j + 1)
                    for k, a, b in conds(c0):
                        t = t0 + j
                        hh = h[:, ds(t, 1), a:b].rearrange("p a t -> p (a t)")
                        last = stt(out=hh, in0=bank[j][:, a:b], scalar=hgate[:, ds(t, 1), k:k + 1].rearrange("p a t -> p (a t)"),
                                   in1=hh, op0=ALU.mult, op1=ALU.add)
                    if j % 2:
                        last.then_inc(pair_done[j // 2], 1)

            def ffn(l, f):
                c0 = CTX if l == DEPTH - 1 and f == 1 else 0
                tile0 = (2 * l + f) * FT
                for p, tiles in enumerate(PIECES):
                    B0, G0 = P[("up", l, f, p)]
                    g0, rides = P[("rides", l, f, p)]
                    per = 2 if rides else 1
                    dve.wait_ge(panel_done, 4 * B0)
                    with dve.Fori(0, tiles // 2) as i:
                        B, G, n0 = B0 + per * i, G0 + i, tile0 + 2 * i
                        if rides:
                            ada_panels(B)
                            B = B + 1
                        for k in range(2):
                            split(B + 1, 2 * k)
                            if rides and k == 0:
                                ada_mod(g0 + i, g0 // ADA_GROUPS, (g0 % ADA_GROUPS) + i)
                            dve.wait_ge(sil_ready, n0 + k + 1)
                            dve.wait_ge(panel_done, 4 * B + 2 * k + 2)
                            dve.tensor_tensor(hbuf[:, k, c0:T], sil[:, k, c0:T], bank[2 * k + 1][:, c0:T],
                                              ALU.mult).then_inc(pair_done[k], 1)
                            split(B + 1, 2 * k + 1)
                            dve.wait_ge(hid_hi, n0 + k + 1)
                            dve.tensor_tensor(bl[:, ds(2 * i + k, 1), c0:T].rearrange("p a t -> p (a t)"), hbuf[:, k, c0:T],
                                              bh[:, ds(2 * i + k, 1), c0:T].rearrange("p a t -> p (a t)").bitcast(f32),
                                              ALU.subtract).then_inc(hid_ready, 1)
                    tile0 += tiles
                    B0, G0 = P[("down", l, f, p)]
                    have(dve, pair_done[1], G0)
                    if B0 + 2 < NB:
                        with dve.Fori(0, 2) as i:
                            residual(B0 + i, G0 + i, 4 * i, c0)
                    else:
                        residual(B0, G0, 0, c0)
                        residual(B0 + 1, G0 + 1, 4, c0)
                    have(dve, pair_done[0], G0 + 2)
                    have(dve, pair_done[1], G0 + 2)

            def ab(l):
                q = lambda a: SM[:, a:a + 64]
                q3 = lambda a: q(a).rearrange("p (c n) -> p c n", c=TC)
                row = lambda a, n: rows[:, l, a:a + n].rearrange("p (c n) -> p c n", c=1).broadcast_to([128, TC, n])
                dve.wait_ge(wab_hi, l + 1)
                dve.tensor_tensor(wabl, wab, wabh.bitcast(f32), ALU.subtract).then_inc(wab_lo, 1)
                dve.wait_ge(ab_sum, l + 1)
                ps = bank[7][:, 0:128].rearrange("p (c n) -> p c n", c=TC)
                dve.tensor_tensor(q3(0), ps[:, :, 0:16], row(R_AB, 16), ALU.add)
                steps.do(dve.tensor_tensor(q3(960), ps[:, :, 16:32], row(R_AB + 16, 16), ALU.add))
                steps.sync()
                steps.do(dve.tensor_tensor(q3(0), q3(0), row(R_DT, 16), ALU.add))
                steps.sync()
                stt(out=q(64), in0=q(0), scalar=-1.0, in1=q(0), op0=ALU.mult, op1=ALU.min).then_inc(ab_z, 1)
                dve.wait_ge(ab_exp, 2 * l + 1)
                steps.do(stt(out=q(384), in0=q(0), scalar=0.0, in1=q(320), op0=ALU.max, op1=ALU.add))
                steps.do(dve.tensor_scalar(q(832), q(192), 1.0, None, ALU.add))
                steps.sync()
                al = SM[:, 256:272].rearrange("p (c n) -> p c n", c=1).broadcast_to([128, TC, 16])
                stt(out=q3(384), in0=q3(384), scalar=-1.0, in1=al, op0=ALU.mult, op1=ALU.mult).then_inc(g_ready, 1)
                steps.do(dve.reciprocal(q(832), q(832)))
                dve.wait_ge(gc_sum, l + 1)
                dve.tensor_copy(q(448), bank[7][:, 128:192])
                steps.do(dve.tensor_copy(q(512), bank[7][:, 192:256]))
                steps.sync()
                dve.tensor_tensor(q(576), q(512), q(448), ALU.subtract).then_inc(ab_z, 1)
                dve.wait_ge(ab_exp, 2 * l + 2)
                dve.wait_ge(ab_z, 2 * l + 2)
                steps.do(dve.tensor_scalar(q(640), q(640), -1.0, None, ALU.mult))
                steps.sync()
                for kind, src in ((HB_G, 384), (HB_GC, 448), (HB_NEG, 640), (HB_BETA, 832), (HB_KD, 768), (HB_TOT, 704)):
                    for d in range(2):
                        dst = tab[:, :, (kind * 2 + d) * 4:(kind * 2 + d) * 4 + 4]
                        s = q(src).rearrange("p (c d h) -> p h d c", c=TC, d=2)[:, :, d, :]
                        last = dve.tensor_copy(dst, s)
                last.then_inc(tab_ready, 1)

            def prep_in(l, b):
                G0 = P[("head", l)][1]
                v0 = V_HEAD + l * NVL + HV * b
                have(dve, pair_done[1], G0 + b)
                dve.tensor_copy(hv[:, :], vec[:, ds(v0, HV)]).then_inc(E["hv_ready"], 1)
                for j in range(3):
                    steps.do(dve.memset(pre[:, j, :, 0:1], 0.0))
                    steps.do(dve.memset(pre[:, j, :, 257:258], 0.0))
                steps.sync()

            def prep_conv(l, b, n):
                c0 = CTX if l == DEPTH - 1 else 0
                s0 = c0 // CTX
                o = l * DNH + b
                j = (1, 0, 2)[n]
                a = s0 if j == 0 else 0
                dve.wait_ge(E["hv_ready"], o + 1)
                dve.wait_ge(E["pre_ready"], 3 * o + n + 1)
                x = kraw[:, :] if j == 1 else qkv[:, j, :]
                y = x.rearrange("p (s t) -> p s t", s=2)[:, a:2, :]
                tap = lambda i: hv[:, 4 + 3 * j + i:5 + 3 * j + i]
                steps.do(dve.tensor_scalar(y, pre[:, j, a:2, 0:256], tap(0), None, ALU.mult))
                steps.sync()
                steps.do(stt(out=y, in0=pre[:, j, a:2, 1:257], scalar=tap(1), in1=y, op0=ALU.mult, op1=ALU.add))
                steps.sync()
                stt(out=y, in0=pre[:, j, a:2, 2:258], scalar=tap(2), in1=y, op0=ALU.mult, op1=ALU.add).then_inc(E["conv_ready"], 1)

            def prep_var(l, b):
                c0 = CTX if l == DEPTH - 1 else 0
                o = l * DNH + b
                dve.wait_ge(E["conv_ready"], 3 * o + 3)
                for n in range(2):
                    a = c0 if n else 0
                    dve.wait_ge(E["l2_sum"], 2 * o + n + 1)
                    dve.tensor_scalar(hrs[:, n, a:T], bank[n][:, a:T], EPS, None, ALU.add).then_inc(E["l2_var"], 1)
                dve.wait_ge(E["l2_var"], 2 * o + 2)
                dve.sem_inc(pair_done[0], 1)

            def k_norm(l, b):
                o = l * DNH + b
                dve.wait_ge(E["l2_rstd"], 2 * o + 1)
                dve.tensor_tensor(qkv[:, 1, :], kraw[:, :], hrs[:, 0, :], ALU.mult).then_inc(E["kn_ready"], 1)

            def q_norm(l, b):
                c0 = CTX if l == DEPTH - 1 else 0
                o = l * DNH + b
                dve.wait_ge(E["l2_rstd"], 2 * o + 2)
                stt(out=qkv[:, 0, c0:T], in0=qkv[:, 0, c0:T], scalar=128 ** -0.5, in1=hrs[:, 1, c0:T],
                    op0=ALU.mult, op1=ALU.mult).then_inc(E["qn_ready"], 1)

            def turned(l, b):
                dve.wait_ge(E["kv_turned"], 2 * (l * DNH + b) + 1)
                dve.tensor_copy(vtok, bank[5][:, :]).then_inc(E["vtok_ready"], 1)

            def head(l, b, follow):
                c0 = CTX if l == DEPTH - 1 else 0
                B = P[("head", l)][0] + b
                cs = [c for c in range(TC) if 128 * c >= c0]
                o = l * DNH + b - 1
                dve.tensor_copy(hb[:, :], tab[:, ds(b - 1, 1), :].rearrange("p a n -> p (a n)")).then_inc(E["hb_ready"], 1)
                dve.wait_ge(E["hb_ready"], o + 1)
                for d in range(2):
                    dve.wait_ge(E["gc_row"], 2 * o + d + 1)
                    for c in range(TC):
                        last = stt(out=DT[:, d, 128 * c:128 * c + 128], in0=bank[4 + d][:, 128 * c:128 * c + 128],
                                   scalar=hb[:, hcol(HB_GC, d, c)], in1=cst[:, C_NM + 128 * d:C_NM + 128 * d + 128],
                                   op0=ALU.subtract, op1=ALU.add)
                    last.then_inc(E["dm_ready"], 1)
                dve.wait_ge(E["gram"], 2 * o + 1)
                dve.tensor_tensor(c4d(Gs), c4d(bank[7][:, :]), bc(cst[:, C_OFF:C_OFF + 128], TC, 128), ALU.mult).then_inc(E["gs_ready"], 1)
                dve.wait_ge(E["gs_ready"], o + 1)
                for d in range(2):
                    dve.wait_ge(E["dt_ready"], 2 * o + d + 1)
                    for c in range(TC):
                        s = slice(128 * c, 128 * c + 128)
                        last = stt(out=AT[:, d, s], in0=Gs[:, s], scalar=hb[:, hcol(HB_BETA, d, c)], in1=DT[:, d, s],
                                   op0=ALU.mult, op1=ALU.mult)
                    last.then_inc(E["at_ready"], 1)
                    dve.wait_ge(E["at_ready"], 2 * o + d + 1)
                    steps.do(dve.tensor_tensor(c4d(IT[:, d, :]), c4d(AT[:, d, :]), bc(cst[:, C_LV:C_LV + 128], TC, 128), ALU.mult))
                    steps.sync()
                    dve.tensor_tensor(c4d(XT[:, d, :]), c4d(IT[:, d, :]), bc(ident, TC, 128), ALU.add).then_inc(E["xt0_ready"], 1)
                for v in range(1, 7):
                    mask = bc(cst[:, C_LV + 128 * v:C_LV + 128 * v + 128], TC, 128)
                    for d in range(2):
                        dve.wait_ge(E["p_sum"], 18 * o + 2 * (v - 1) + d + 1)
                        dve.tensor_tensor(c4d(Pm[:, d, :]), c4d(bank[3][:, :]), mask, ALU.mult).then_inc(E["pm_ready"], 1)
                        if v == 1:
                            dve.wait_ge(E["eg_ready"], 2 * o + d + 1)
                            dve.wait_ge(E["qn_ready"], o + 1)
                            dve.tensor_tensor(Qt[:, d, c0:T], qkv[:, 0, c0:T], eg[:, d, c0:T], ALU.mult).then_inc(E["qt_ready"], 1)
                            dve.wait_ge(E["kq_ready"], o + 1)
                            dve.wait_ge(E["xt0_ready"], 4 * o + d + 1)
                            dve.tensor_tensor(IT[:, d, c0:T], KQs[:, c0:T], DT[:, d, c0:T], ALU.mult).then_inc(E["it_ready"], 1)
                        if v == 2 and d == 0:
                            if follow:
                                dve.wait_ge(E["qt_ready"], 2 * o + 2)
                                prep_in(l, b)
                            split(B + 1, 0)
                        if 2 <= v < 5 and d == 1 and follow:
                            prep_conv(l, b, v - 2)
                        if v == 5 and d == 1:
                            split(B + 1, 1)
                if follow:
                    prep_var(l, b)
                for d in range(2):
                    dve.wait_ge(E["p_sum"], 18 * o + 16 + d + 1)
                    dve.wait_ge(E["it_ready"], 2 * o + d + 1)
                    last = dve.tensor_tensor(XTf[:, d, :], XT[:, d, :].bitcast(f32), bank[4 + d][:, :], ALU.subtract)
                    last.then_inc(E["xt0_ready"], 1)
                for s in range(TC):
                    for d in range(2):
                        c = chunk(d, s)
                        if s:
                            dve.wait_ge(E["ks_sum"], 6 * o + 2 * (s - 1) + d + 1)
                            stt(out=Rr[:, d, :], in0=bank[4 + d][:, 0:128], scalar=hb[:, hcol(HB_NEG, d, c)],
                                in1=vtok[:, 128 * c:128 * c + 128], op0=ALU.mult, op1=ALU.add).then_inc(E["r_ready"], 1)
                    for d in range(2):
                        c = chunk(d, s)
                        dve.wait_ge(E["y_sum"], 8 * o + 2 * s + d + 1)
                        dve.tensor_scalar(vn[:, d, :], bank[4 + d][:, 128:256], hb[:, hcol(HB_BETA, d, c)], None,
                                          ALU.mult).then_inc(E["vn_ready"], 1)
                    if s < TC - 1:
                        for d in range(2):
                            c = chunk(d, s)
                            dve.wait_ge(E["ds_sum"], 6 * o + 2 * s + d + 1)
                            if s == 0:
                                dve.tensor_copy(St[:, 0, d, :], bank[4 + d][:, 256:384]).then_inc(E["s_ready"], 1)
                            else:
                                dve.wait_ge(E["s_ready"], 6 * o + 2 * (s - 1) + d + 1)
                                stt(out=St[:, s % 2, d, :], in0=St[:, (s - 1) % 2, d, :], scalar=hb[:, hcol(HB_TOT, d, c)],
                                    in1=bank[4 + d][:, 256:384], op0=ALU.mult, op1=ALU.add).then_inc(E["s_ready"], 1)
                    if s == 0:
                        split(B + 1, 2)
                if follow:
                    k_norm(l, b)
                dve.wait_ge(E["on_sum"], o + 1)
                dve.tensor_scalar(eo[:, 1, c0:T], bank[7][:, c0:T], 1.0 / 128, EPS, ALU.mult, ALU.add).then_inc(E["on_var"], 1)
                if follow:
                    turned(l, b)
                    q_norm(l, b)
                dve.wait_ge(E["on_rstd"], o + 1)
                steps.do(stt(out=eo[:, 0, c0:T], in0=bank[6][:, c0:T], scalar=vec[:, l * NVL + V_DNG:l * NVL + V_DNG + 1],
                             in1=eo[:, 1, c0:T], op0=ALU.mult, op1=ALU.mult))
                steps.sync()
                dve.tensor_tensor(gated[:, c0:T], gate[:, c0:T], eo[:, 0, c0:T], ALU.mult).then_inc(E["on_ready"], 1)
                split(B + 1, 3)
                dve.wait_ge(E["bh_ready"], o + 1)
                dve.tensor_tensor(bl[:, ds(b - 1, 1), c0:T].rearrange("p a t -> p (a t)"), gated[:, c0:T],
                                  bh[:, ds(b - 1, 1), c0:T].rearrange("p a t -> p (a t)").bitcast(f32),
                                  ALU.subtract).then_inc(E["head_ready"], 1)

            HSTEPS = 6 + 2 + 6 + 1
            def heads(l):
                B0 = P[("head", l)][0]
                dve.wait_ge(panel_done, 4 * B0)
                prep_in(l, 0)
                split(B0 + 1, 0)
                for n in range(3):
                    prep_conv(l, 0, n)
                prep_var(l, 0)
                k_norm(l, 0)
                split(B0 + 1, 1)
                turned(l, 0)
                q_norm(l, 0)
                split(B0 + 1, 2)
                split(B0 + 1, 3)
                with steps.loop(1, DNH - 1, HSTEPS) as b:
                    head(l, b, True)
                head(l, DNH - 1, True)
                head(l, DNH, False)

            def branch(l, r):
                B0, G0 = P[("br", l, r)]
                c0 = CTX if l == DEPTH - 1 else 0
                n0 = (3 * l + r) * 8
                with steps.loop(0, 4, 0 if r == 0 else 2) as i:
                    for k in range(2):
                        split(B0 + i + 1, 2 * k)
                        dve.wait_ge(panel_done, 4 * (B0 + i) + 2 * k + 2)
                        dve.wait_ge(C["br_gate"], n0 + 2 * i + k + 1)
                        mt = m3[:, ds(2 * i + k, 1), c0:T].rearrange("p a t -> p (a t)")
                        if r == 0:
                            dve.tensor_tensor(mt, sil[:, k, c0:T], bank[2 * k + 1][:, c0:T], ALU.mult).then_inc(pair_done[k], 1)
                        else:
                            steps.do(dve.tensor_tensor(hbuf[:, k, c0:T], sil[:, k, c0:T], bank[2 * k + 1][:, c0:T], ALU.mult))
                            steps.sync()
                            dve.tensor_tensor(mt, mt, hbuf[:, k, c0:T], ALU.add).then_inc(pair_done[k], 1)
                        split(B0 + i + 1, 2 * k + 1)
                for k in range(2):
                    have(dve, pair_done[k], G0 + 4)

            def qk_norm(na, gcol, dst, c0):
                dve.wait_ge(A["a_sum"], na + 1)
                dve.tensor_scalar(ars[:, c0:T], bank[4][:, c0:T], 1.0 / HD, EPS, ALU.mult, ALU.add).then_inc(A["a_var"], 1)
                dve.wait_ge(A["a_rstd"], na + 1)
                stt(out=dst[:, c0:T], in0=ax[:, c0:T], scalar=vec[:, gcol:gcol + 1], in1=ars[:, c0:T],
                    op0=ALU.mult, op1=ALU.mult).then_inc(A["a_norm"], 1)
                dve.wait_ge(A["a_swap"], na + 1)
                steps.do(dve.tensor_tensor(asw[:, 0:256], bank[5][:, 0:256], cst[:, C_SIN:C_SIN + 256], ALU.mult))
                steps.do(dve.tensor_tensor(asw[:, 256:512], dst[:, CTX:T], cst[:, C_COS:C_COS + 256], ALU.mult))
                steps.sync()
                dve.tensor_tensor(dst[:, CTX:T], asw[:, 0:256], asw[:, 256:512], ALU.add).then_inc(A["a_done"], 1)

            def attention_kv(l):
                L = l * NVL
                na = 10 * l
                for j in range(2):
                    qk_norm(na, L + V_KG, kT[:, j, :], 0)
                    na += 1
                for j in range(2):
                    dve.wait_ge(A["a_vturn"], 2 * l + j + 1)
                    dve.tensor_copy(vt[:, j, :, :].rearrange("p c f -> p (c f)"), bank[4 + j][:, :]).then_inc(A["a_vtok"], 1)
                dve.wait_ge(A["a_vtok"], 2 * l + 2)
                dve.sem_inc(pair_done[0], 1)
                dve.sem_inc(pair_done[1], 1)

            def attention(l):
                c0 = CTX if l == DEPTH - 1 else 0
                L = l * NVL
                na = 10 * l + 2
                nu = att_units_before(l, 0)
                for p in range(2):
                    B, G = P[("q", l)][0] + p, P[("q", l)][1] + p
                    for j in range(4):
                        split(B + 1, j)
                        qk_norm(na, L + V_QG, qx[:, j, :], c0)
                        na += 1
                    dve.wait_ge(A["a_done"], na)
                    units = att_units(l)

                    def scale_p(u):
                        lat = units[u][2]
                        n = 1 if lat else 2
                        dve.wait_ge(A["s_exp"], nu + u + 1)
                        st = 8 * (u % 2)
                        steps.do(dve.reciprocal(stat[:, st + 6:st + 6 + n], stat[:, st + 4:st + 4 + n]))
                        steps.sync()
                        for q in range(n):
                            w = 512 // n
                            last = dve.tensor_scalar(Pb[:, u % 2, q * w:(q + 1) * w], Pb[:, u % 2, q * w:(q + 1) * w],
                                                     stat[:, st + 6 + q:st + 7 + q], None, ALU.mult)
                        last.then_inc(A["s_scaled"], 1)

                    for u, (j, a, lat) in enumerate(units):
                        n = 1 if lat else 2
                        st = 8 * (u % 2)
                        dve.wait_ge(A["s_sum"], nu + u + 1)
                        steps.do(dve.reduce_max(stat[:, st:st + n], bank[4 + u % 2][:, :].rearrange("p (n k) -> p n k", n=n), AX.X))
                        steps.sync()
                        dve.tensor_scalar(stat[:, st + 2:st + 2 + n], stat[:, st:st + n], -HD ** -0.5, None,
                                          ALU.mult).then_inc(A["s_max"], 1)
                        if u:
                            scale_p(u - 1)
                    scale_p(len(units) - 1)
                    nu += len(units)
                    for j in range(4):
                        dve.wait_ge(A["att_hi"], 8 * l + 4 * p + j + 1)
                        last = dve.tensor_tensor(bl[:, 4 * p + j, c0:T], bank[j][:, c0:T], bh[:, 4 * p + j, c0:T].bitcast(f32), ALU.subtract)
                        if j % 2:
                            last.then_inc(pair_done[j // 2], 1)
                        else:
                            last.then_inc(A["att_ready"], 1)

            def conv(l):
                B0, G0 = P[("conv", l)]
                c0 = CTX if l == DEPTH - 1 else 0
                s0 = c0 // CTX
                two = lambda ap: ap.rearrange("p (s t) -> p s t", s=2)[:, s0:2, :]
                for k in (0, 257):
                    steps.do(dve.memset(cpr[:, :, k:k + 1], 0.0))
                steps.sync()
                with steps.loop(0, 2, 4 * 4 - 2) as i:
                    B = B0 + 3 * i
                    n0 = 8 * l + 4 * i
                    dve.tensor_copy(cvec, vec[:, ds(l * NVL + V_CONV + 4 * CV * i, 4 * CV)]).then_inc(C["c_vec"], 1)
                    dve.wait_ge(C["c_vec"], 2 * l + i + 1)
                    for t in range(4):
                        q = 3 * t
                        v = lambda n: cvec[:, t * CV + n:t * CV + n + 1]
                        split(B + q // 4 + 1, q % 4)
                        split(B + (q + 1) // 4 + 1, (q + 1) % 4)
                        dve.wait_ge(C["c_p4"], n0 + t + 1)
                        dve.wait_ge(panel_done, 4 * B + q + 2)
                        ins = stt(out=cpr[:, s0:2, 1:257], in0=two(bank[(q + 1) % 4][:, :]), scalar=v(1), in1=two(c4[:, :]),
                                  op0=ALU.add, op1=ALU.mult)
                        if t in (0, 2):
                            ins.then_inc(pair_done[0 if t == 0 else 1], 1)
                            have(dve, pair_done[0 if t == 0 else 1], (G0 + 3 * i + (0 if t == 0 else 1)) + 1)
                        else:
                            steps.do(ins)
                            steps.sync()
                        y = two(cy[:, :])
                        ins = dve.tensor_scalar(y, cpr[:, s0:2, 0:256], v(3), None, ALU.mult)
                        if t in (1, 3):
                            k = 1 if t == 1 else 0
                            ins.then_inc(pair_done[k], 1)
                            have(dve, pair_done[k], G0 + 3 * i + (1 if t == 1 else 3))
                        else:
                            steps.do(ins)
                            steps.sync()
                        steps.do(stt(out=y, in0=cpr[:, s0:2, 1:257], scalar=v(4), in1=y, op0=ALU.mult, op1=ALU.add))
                        steps.sync()
                        steps.do(stt(out=y, in0=cpr[:, s0:2, 2:258], scalar=v(5), in1=y, op0=ALU.mult, op1=ALU.add))
                        steps.sync()
                        split(B + (q + 2) // 4 + 1, (q + 2) % 4)
                        dve.wait_ge(panel_done, 4 * B + q + 3)
                        z = cz[:, t % 2, :]
                        stt(out=z[:, c0:T], in0=bank[(q + 2) % 4][:, c0:T], scalar=v(2), in1=cy[:, c0:T],
                            op0=ALU.add, op1=ALU.mult).then_inc(C["c_out"], 1)
                        dve.wait_ge(C["c_hi"], n0 + t + 1)
                        ins = dve.tensor_tensor(bl[:, ds(4 * i + t, 1), c0:T].rearrange("p a t -> p (a t)"), z[:, c0:T],
                                                bh[:, ds(4 * i + t, 1), c0:T].rearrange("p a t -> p (a t)").bitcast(f32), ALU.subtract)
                        if t == 1:
                            ins.then_inc(pair_done[0], 1)
                        elif t == 3:
                            ins.then_inc(pair_done[1], 1)
                        else:
                            steps.do(ins)

            def project_out(l):
                B0, G0 = P[("out", l)]
                c0 = CTX if l == DEPTH - 1 else 0
                for t in range(KT):
                    dve.wait_ge(C["mh_ready"], 8 * l + t + 1)
                    dve.tensor_tensor(ul[:, t, c0:T], m3[:, t, c0:T], uh[:, t, c0:T].bitcast(f32), ALU.subtract).then_inc(C["mx_ready"], 1)
                with dve.Fori(0, 2) as i:
                    residual(B0 + i, G0 + i, 4 * i, c0)
                have(dve, pair_done[0], G0 + 2)
                have(dve, pair_done[1], G0 + 2)

            ada_only(("ada", 0))
            n = 0
            for l in range(DEPTH):
                c_last = CTX if l == DEPTH - 1 else 0
                norm(n, l, 0, 0)
                ffn(l, 0)
                ada_only(("ada1", l))
                norm(n + 1, l, 1, 0)
                ab(l)
                heads(l)
                attention_kv(l)
                branch(l, 0)
                attention(l)
                branch(l, 1)
                conv(l)
                branch(l, 2)
                project_out(l)
                norm(n + 2, l, 2, c_last)
                ffn(l, 1)
                if l == 0:
                    ada_only(("ada2", 0))
                n += 3
            norm(n, None, None, CTX)

        @block.tensor
        def _(pe):
            mm = pe.matmul

            def panel(B, j, xh, xl, c0, kts=KT, ready=None, lo=0, hi=None):
                hi = 3 * kts if hi is None else hi
                if lo == 0:
                    pe.wait_ge(lo_ready, 4 * B + j + 1)
                w = lambda t, a: a[:, j, 128 * t:128 * t + 128]
                for n in range(lo, hi):
                    t, r = n // 3, n % 3
                    if ready is not None and r == 0:
                        pe.wait_ge(ready[0], ready[1] + t + 1)
                    a, x = ((whi, xh), (whi, xl), (wlo, xh))[r]
                    last = mm(bank[j][:, c0:T], w(t, a), x[:, t, c0:T], start=n == 0, stop=n == 3 * kts - 1)
                if hi == 3 * kts:
                    last.then_inc(panel_done, 1)

            def pair_free(G, j):
                if j % 2 == 0:
                    have(pe, pair_done[j // 2], G)

            def ada_panels(B, g):
                have(pe, ada_row, g)
                for j in range(4):
                    pe.wait_ge(lo_ready, 4 * B + j + 1)
                    for t in range(2):
                        for w in (whi, wlo):
                            last = mm(bank[4][:, :], cstat[:, 2 * j + t, :], w[:, j, 512 * t:512 * t + 512],
                                      start=(j, t) == (0, 0) and w is whi, stop=(j, t) == (3, 1) and w is wlo)
                    last.then_inc(panel_done, 1)

            def ada_turn(g):
                have(pe, ada_row, g + 1)
                have(pe, mod_ready, g)
                for t in range(4):
                    last = mm(bank[5][:, 2 * t:2 * t + 2], arow[:, 128 * t:128 * t + 128], cst[0:4, C_SEL:C_SEL + 2],
                              start=True, stop=True)
                last.then_inc(ada_turned, 1)

            def ada_only(key):
                B0, _ = P[key]
                g0, n = P["groups"][key]
                with pe.Fori(0, n) as i:
                    ada_panels(B0 + i, g0 + i)
                    ada_turn(g0 + i)

            def norm(n, c0):
                for t in range(KT):
                    pe.wait_ge(sq_ready, 8 * n + t + 1)
                    if t == 0:
                        wait(pe, var_ready, n)
                    mm(bank[6][:, c0:T], ones, nsq[:, t % 2, c0:T], start=t == 0, stop=t == KT - 1).then_inc(sq_used, 1)

            def ffn(l, f, n):
                c0 = CTX if l == DEPTH - 1 and f == 1 else 0
                tile0 = (2 * l + f) * FT
                for p, tiles in enumerate(PIECES):
                    B0, G0 = P[("up", l, f, p)]
                    g0, rides = P[("rides", l, f, p)]
                    per = 2 if rides else 1
                    with pe.Fori(0, tiles // 2) as i:
                        B, G = B0 + per * i, G0 + i
                        if rides:
                            ada_panels(B, g0 + i)
                            B = B + 1
                        for j in range(4):
                            pair_free(G, j)
                            panel(B, j, uh, ul, c0, ready=(u_ready, 8 * n) if j == 0 and p == 0 else None)
                            if rides and j == 0:
                                ada_turn(g0 + i)
                    tile0 += tiles
                    B0, G0 = P[("down", l, f, p)]
                    pe.wait_ge(hid_ready, tile0)
                    with pe.Fori(0, 2) as i:
                        for j in range(4):
                            pair_free(G0 + i, j)
                            panel(B0 + i, j, bh, bl, c0, kts=tiles)

            def ab(l, n):
                pe.wait_ge(u_ready, 8 * n + 8)
                pe.wait_ge(wab_lo, l + 1)
                for c in range(TC):
                    s = slice(128 * c, 128 * c + 128)
                    for t in range(KT):
                        for r, (x, w) in enumerate(((uh, wabh), (ul, wabh), (uh, wabl))):
                            last = mm(bank[7][:, 32 * c:32 * c + 32], x[:, t, s], w[:, 32 * t:32 * t + 32],
                                      start=t == 0 and r == 0, stop=t == KT - 1 and r == 2)
                last.then_inc(ab_sum, 1)
                pe.wait_ge(g_ready, l + 1)
                g = SM[:, 384:448].rearrange("p (c n) -> p c n", c=TC)
                for c in range(TC):
                    for d in range(2):
                        mm(bank[7][:, 128 + 16 * c + 8 * d:136 + 16 * c + 8 * d], cst[:, C_CUM + 128 * d:C_CUM + 128 * d + 128],
                           g[:, c, 8 * d:8 * d + 8], start=True, stop=True)
                    last = mm(bank[7][:, 192 + 16 * c:208 + 16 * c], ones, g[:, c, :], start=True, stop=True)
                last.then_inc(gc_sum, 1)

            def head(l, b, follow):
                B0, G0 = P[("head", l)]
                c0 = CTX if l == DEPTH - 1 else 0
                B, G = B0 + b, G0 + b
                issued = [24]

                def project(n):
                    while n:
                        k_, at = issued[0] // 24, issued[0] % 24
                        k = min(n, 24 - at)
                        j, nxt = k_ % 4, k_ // 4
                        if at == 0:
                            pair_free(G + nxt, j)
                        if not follow:
                            a = 0
                        elif nxt:
                            a = 0 if isinstance(b, int) and b == DNH - 1 else c0
                        else:
                            a = c0 if j == 3 else 0
                        panel(B + nxt, j, uh, ul, a, lo=at, hi=at + k)
                        issued[0] += k
                        n -= k

                o = l * DNH + b - 1
                cs = [c for c in range(TC) if 128 * c >= c0]
                sl = lambda c: slice(128 * c, 128 * c + 128)
                pe.wait_ge(E["hb_ready"], o + 1)
                for d in range(2):
                    pe.wait_ge(E["vtok_ready" if d else "ktok_ready"], o + 1)
                    for c in range(TC):
                        last = mm(bank[4 + d][:, sl(c)], hb[:, hcol(HB_G, d, c)].broadcast_to([128, 128]),
                                  cst[:, C_CUM + 128 * d:C_CUM + 128 * d + 128], start=True, stop=True)
                    last.then_inc(E["gc_row"], 1)
                have(pe, E["head_ready"], o)
                for c in range(TC):
                    last = mm(bank[7][:, sl(c)], qkv[:, 1, sl(c)], qkv[:, 1, sl(c)], start=True, stop=True)
                last.then_inc(E["gram"], 1)
                pe.wait_ge(E["qn_ready"], o + 1)
                for c in cs:
                    last = mm(bank[6][:, sl(c)], qkv[:, 1, sl(c)], qkv[:, 0, sl(c)], start=True, stop=True)
                last.then_inc(E["gram"], 1)
                project(28)
                for d in range(2):
                    pe.wait_ge(E["xt0_ready"], 4 * o + d + 1)
                    if d == 0:
                        pe.wait_ge(E["kq_ready"], o + 1)
                    else:
                        pe.wait_ge(E["gs_ready"], o + 1)
                    for c in range(TC):
                        mm(bank[6 + d][:, sl(c)], XT[:, d, sl(c)], idr[:, :], start=c == 0, stop=False, skip_group_check=True)
                    pe.wait_ge(E["eg_ready"], 2 * o + d + 1)
                    mm(bank[4 + d][:, :], idr[:, :], XT[:, d, :], start=True, stop=False,
                       skip_group_check=True).then_inc(E["xt0_turned"], 1)
                    project(10)

                def product(v, d):
                    if v == 1:
                        pe.wait_ge(E["atr_ready"], 2 * o + d + 1)
                    pe.wait_ge(E["x_ready"], 14 * o + 2 * (v - 1) + d + 1)
                    if (v, d) != (1, 0):
                        pe.wait_ge(E["pm_ready"], 14 * o + 2 * (v - 1) + d)
                    for c in range(TC):
                        last = mm(bank[3][:, sl(c)], ATr[:, d, sl(c)], X[:, d, sl(c)], start=True, stop=True)
                    last.then_inc(E["p_sum"], 1)

                def add(v, d):
                    pe.wait_ge(E["pm_ready"], 14 * o + 2 * (v - 1) + d + 1)
                    if v > 1:
                        pe.wait_ge(E["xt_ready"], 12 * o + 2 * (v - 2) + d + 1)
                    for c in range(TC):
                        last = mm(bank[6 + d][:, sl(c)], XT[:, d, sl(c)], Pm[:, d, sl(c)], start=False, stop=False, skip_group_check=True)
                    last.then_inc(E["x_sum"], 1)
                    if v < 6:
                        for c in range(TC):
                            last = mm(bank[4 + d][:, sl(c)], Pm[:, d, sl(c)], XT[:, d, sl(c)], start=False, stop=False, skip_group_check=True)
                        last.then_inc(E["x_sum"], 1)

                product(1, 0)
                for v in range(1, 7):
                    add(v, 0)
                    product(v, 1)
                    if follow and v in (4, 5):
                        n = v - 4
                        a = c0 if n else 0
                        pe.wait_ge(E["hsq_ready"], 2 * (o + 1) + n + 1)
                        mm(bank[n][:, a:T], ones, hsq[:, n, a:T], start=True, stop=True).then_inc(E["l2_sum"], 1)
                    if v < 6:
                        product(v + 1, 0)
                    add(v, 1)
                for d in range(2):
                    pe.wait_ge(E["x_ready"], 14 * o + 12 + d + 1)
                    for c in range(TC):
                        last = pe.transpose(bank[4 + d][:, sl(c)], X[:, d, sl(c)].bitcast(f32), ident)
                    last.then_inc(E["p_sum"], 1)
                for d in range(2):
                    mm(bank[6 + d][:, :], idr[:, :], X[:, d, :], start=True, stop=False, skip_group_check=True)
                    mm(bank[6 + d][:, :], nidr[:, :], bc(idr[:, :], TC, 128), start=False, stop=False, skip_group_check=True)
                    for c in range(TC):
                        last = mm(bank[6 + d][:, sl(c)], AT[:, d, sl(c)], X[:, d, sl(c)].bitcast(f32), start=False, stop=False,
                                  skip_group_check=True)
                    last.then_inc(E["p_sum"], 1)
                project(2)
                for d in range(2):
                    pe.wait_ge(E["xt_ready"], 12 * o + 10 + d + 1)
                    pe.wait_ge(E["pm_ready"], 14 * o + 12 + d + 1)
                    for c in range(TC):
                        last = mm(bank[4 + d][:, sl(c)], Pm[:, d, sl(c)], XT[:, d, sl(c)], start=True, stop=True)
                    last.then_inc(E["p_sum"], 1)
                project(4)
                first = [True]
                for s in range(TC):
                    if s:
                        for d in range(2):
                            c = chunk(d, s)
                            pe.wait_ge(E["s_ready"], 6 * o + 2 * (s - 1) + d + 1)
                            mm(bank[4 + d][:, 0:128], qkv[:, 1, sl(c)], St[:, (s - 1) % 2, d, :], start=True, stop=True).then_inc(E["ks_sum"], 1)
                        project(1)
                    for d in range(2):
                        c = chunk(d, s)
                        if s == 0:
                            pe.wait_ge(E["xt0_ready"], 4 * o + 2 + d + 1)
                            r = vtok[:, sl(c)]
                        else:
                            pe.wait_ge(E["r_ready"], 6 * o + 2 * (s - 1) + d + 1)
                            r = Rr[:, d, :]
                        mm(bank[4 + d][:, 128:256], XTf[:, d, sl(c)], r, start=True, stop=True).then_inc(E["y_sum"], 1)
                    project(1)
                    for d in range(2):
                        c = chunk(d, s)
                        if s < TC - 1:
                            pe.wait_ge(E["vd_ready"], 6 * o + 2 * s + d + 1)
                            mm(bank[4 + d][:, 256:384], ktok[:, sl(c)], vd[:, d, :], start=True, stop=True).then_inc(E["ds_sum"], 1)
                    for d in range(2):
                        c = chunk(d, s)
                        pe.wait_ge(E["vn_ready"], 8 * o + 2 * s + d + 1)
                        if first[0]:
                            pe.wait_ge(E["qt_ready"], 2 * o + 2)
                            pe.wait_ge(E["it_ready"], 2 * o + 2)
                        if c not in cs:
                            continue
                        if s:
                            mm(bank[6][:, sl(c)], St[:, (s - 1) % 2, d, :], Qt[:, d, sl(c)], start=first[0], stop=False, skip_group_check=True)
                            first[0] = False
                        last = mm(bank[6][:, sl(c)], vn[:, d, :], IT[:, d, sl(c)], start=first[0],
                                  stop=False, skip_group_check=True)
                        first[0] = False
                    project(1)
                last.then_inc(E["o_sum"], 1)
                if follow:
                    v_turn(l, b)
                project(96 - issued[0])
                pe.wait_ge(E["osq_ready"], o + 1)
                mm(bank[7][:, c0:T], ones, eo[:, 0, c0:T], start=True, stop=True).then_inc(E["on_sum"], 1)
                if follow:
                    k_turn(l, b)
                    project(24)

            def v_turn(l, b):
                pe.wait_ge(E["silu_ready"], 3 * (l * DNH + b) + 3)
                for c in range(TC):
                    last = pe.transpose(bank[5][:, 128 * c:128 * c + 128], qkv[:, 2, 128 * c:128 * c + 128], ident)
                last.then_inc(E["kv_turned"], 1)

            def k_turn(l, b):
                pe.wait_ge(E["kn_ready"], l * DNH + b + 1)
                for c in range(TC):
                    last = pe.transpose(bank[4][:, 128 * c:128 * c + 128], qkv[:, 1, 128 * c:128 * c + 128], ident)
                last.then_inc(E["kv_turned"], 1)

            def heads(l):
                B0, G0 = P[("head", l)]
                c0 = CTX if l == DEPTH - 1 else 0
                o = l * DNH
                for j in range(4):
                    pair_free(G0, j)
                    panel(B0, j, uh, ul, c0 if j in (0, 3) else 0)
                for n in range(2):
                    a = c0 if n else 0
                    pe.wait_ge(E["hsq_ready"], 2 * o + n + 1)
                    mm(bank[n][:, a:T], ones, hsq[:, n, a:T], start=True, stop=True).then_inc(E["l2_sum"], 1)
                v_turn(l, 0)
                k_turn(l, 0)
                pair_free(G0 + 1, 0)
                panel(B0 + 1, 0, uh, ul, c0)
                with pe.Fori(1, DNH - 1) as b:
                    head(l, b, True)
                head(l, DNH - 1, True)
                head(l, DNH, False)

            def branch(l, r, ready):
                B0, G0 = P[("br", l, r)]
                c0 = CTX if l == DEPTH - 1 else 0
                for s, n in ready:
                    have(pe, s, n)
                with pe.Fori(0, 4) as i:
                    for j in range(4):
                        pair_free(G0 + i, j)
                        panel(B0 + i, j, *((uh, ul) if j % 2 == 0 else (bh, bl)), c0)

            def qk_sum(na, c0):
                pe.wait_ge(A["a_sq"], na + 1)
                mm(bank[4][:, c0:T], cst[:, C_BLK:C_BLK + 128], asq[:, c0:T], start=True, stop=True).then_inc(A["a_sum"], 1)

            def qk_swap(na, dst):
                pe.wait_ge(A["a_norm"], na + 1)
                mm(bank[5][:, 0:256], cst[:, C_PERM:C_PERM + 128], dst[:, CTX:T], start=True, stop=True).then_inc(A["a_swap"], 1)

            def attention_kv(l):
                na = 10 * l
                for j in range(2):
                    qk_sum(na, 0)
                    qk_swap(na, kT[:, j, :])
                    na += 1
                pe.wait_ge(A["a_done"], na)
                for j in range(2):
                    pe.wait_ge(A["a_vx"], 2 * l + j + 1)
                    for c in range(TC):
                        last = pe.transpose(bank[4 + j][:, 128 * c:128 * c + 128], ax[:, 128 * c:128 * c + 128], ident)
                    last.then_inc(A["a_vturn"], 1)
                pe.wait_ge(A["a_vtok"], 2 * l + 2)

            def attention(l):
                c0 = CTX if l == DEPTH - 1 else 0
                na = 10 * l + 2
                nu = att_units_before(l, 0)
                for p in range(2):
                    B, G = P[("q", l)][0] + p, P[("q", l)][1] + p
                    for j in range(5):
                        if j < 4:
                            pair_free(G, j)
                            panel(B, j, uh, ul, c0, hi=12)
                        if j:
                            qk_sum(na, c0)
                        if j < 4:
                            panel(B, j, uh, ul, c0, lo=12)
                        if j:
                            qk_swap(na, qx[:, j - 1, :])
                            na += 1
                    pe.wait_ge(A["a_done"], na)
                    units = att_units(l)

                    def turn(u):
                        pe.wait_ge(A["s_scaled"], nu + u + 1)
                        for k in range(4):
                            last = pe.transpose(bank[6 + u % 2][:, 128 * k:128 * k + 128], Pb[:, u % 2, 128 * k:128 * k + 128], ident)
                        last.then_inc(A["s_turned"], 1)

                    def pv(u):
                        j, a, kind = units[u]
                        pe.wait_ge(A["s_pt"], nu + u + 1)
                        rows_ = slice(64 * a, 64 * a + 64)
                        v = lambda kt: vt[:, p, kt, 64 * a:64 * a + 64]
                        pt = lambda k: PT[:, u % 2, 128 * k:128 * k + 128]
                        if kind:
                            for kt in range(4):
                                last = mm(bank[j][rows_, 128 * kind:128 * kind + 128], v(kt), pt(kt), start=kt == 0, stop=kt == 3)
                        else:
                            for q in range(2):
                                for kt in range(2):
                                    last = mm(bank[j][rows_, 128 * q:128 * q + 128], v(kt), pt(2 * q + kt), start=kt == 0, stop=kt == 1)
                        last.then_inc(A["s_pv"], 1)

                    def scores(u):
                        j, a, kind = units[u]
                        if u >= 2:
                            pe.wait_ge(A["s_exp"], nu + u - 1)
                        r = slice(64 * a, 64 * a + 64)
                        if kind:
                            last = mm(bank[4 + u % 2][:, :], qx[r, j, 128 * kind:128 * kind + 128], kT[r, p, :], start=True, stop=True)
                        else:
                            for q in range(2):
                                last = mm(bank[4 + u % 2][:, 256 * q:256 * q + 256], qx[r, j, 128 * q:128 * q + 128], kT[r, p, 0:CTX],
                                          start=True, stop=True)
                        last.then_inc(A["s_sum"], 1)

                    n = len(units)
                    scores(0)
                    for u in range(n + 2):
                        if u + 1 < n:
                            scores(u + 1)
                        if u >= 2:
                            pv(u - 2)
                        if 1 <= u <= n:
                            turn(u - 1)
                    nu += n

            def conv(l):
                B0, G0 = P[("conv", l)]
                c0 = CTX if l == DEPTH - 1 else 0
                with pe.Fori(0, 2) as i:
                    for q in range(12):
                        pair_free(G0 + 3 * i + q // 4, q % 4)
                        panel(B0 + 3 * i + q // 4, q % 4, uh, ul, c0)

            def project_out(l):
                B0, G0 = P[("out", l)]
                c0 = CTX if l == DEPTH - 1 else 0
                with pe.Fori(0, 2) as i:
                    for j in range(4):
                        pair_free(G0 + i, j)
                        panel(B0 + i, j, uh, ul, c0, ready=(C["mx_ready"], 8 * l) if j == 0 else None)

            pe.sem_inc(ada_turned, 1)
            pe.wait_ge(setup_act, 2)
            pe.wait_ge(setup_dve, 2)
            pe.wait_ge(consts_loaded, 16)
            ada_only(("ada", 0))
            n = 0
            for l in range(DEPTH):
                c_last = CTX if l == DEPTH - 1 else 0
                norm(n, 0)
                ffn(l, 0, n)
                ada_only(("ada1", l))
                norm(n + 1, 0)
                ab(l, n + 1)
                heads(l)
                attention_kv(l)
                branch(l, 0, [(pair_done[1], P[("kv", l)][1] + 1)])
                attention(l)
                branch(l, 1, [(pair_done[0], P[("q", l)][1] + 2), (pair_done[1], P[("q", l)][1] + 2)])
                conv(l)
                branch(l, 2, [(pair_done[1], P[("conv", l)][1] + 6)])
                project_out(l)
                norm(n + 2, c_last)
                ffn(l, 1, n + 2)
                if l == 0:
                    ada_only(("ada2", 0))
                n += 3
            norm(n, CTX)


def _tables():
    c = np.zeros((128, NC), np.float32)
    i = np.arange(128)
    c[:, C_ID:C_ID + 128] = np.eye(128)
    c[:, C_OFF:C_OFF + 128] = 1 - np.eye(128)
    c[:, C_ONE:C_ONE + 128] = 1
    c[:, C_BLK:C_BLK + 128] = (i[:, None] // 64) == (i[None, :] // 64)
    c[:, C_PERM:C_PERM + 128] = (i[:, None] ^ 32) == i[None, :]
    for v in range(7):
        s = 1 << v
        c[:, C_LV + 128 * v:C_LV + 128 * v + 128] = -1.0 * (
            (i[:, None] // (2 * s) == i[None, :] // (2 * s)) & (i[:, None] // s != i[None, :] // s))
    for d in range(2):
        ok = (i[None, :] >= i[:, None]) if d == 0 else (i[None, :] <= i[:, None])
        c[:, C_NM + 128 * d:C_NM + 128 * d + 128] = np.where(ok, 0.0, NEG)
        c[:, C_CUM + 128 * d:C_CUM + 128 * d + 128] = ok
    GW = 64
    t = np.arange(SEQ)
    inv = (10000.0 ** (-np.arange(16, dtype=np.float32) / 16)).astype(np.float32)
    ang = np.concatenate([(t // GW).astype(np.float32)[:, None] * inv, (t % GW).astype(np.float32)[:, None] * inv], 1)
    cos, sin = np.cos(ang).T, np.sin(ang).T
    c[:, C_COS:C_COS + 256] = np.tile(cos, (4, 1))
    c[:, C_SIN:C_SIN + 256] = np.tile(np.concatenate([-sin, sin]), (2, 1))
    c[0, C_SEL] = c[2, C_SEL] = c[1, C_SEL + 1] = c[3, C_SEL + 1] = 1
    return c


def _q_order():
    heads = [(2 * p + a) * 4 + i for p in range(2) for i in range(4) for a in range(2)]
    return np.concatenate([np.arange(64 * x, 64 * x + 64) for x in heads])


def _panels(w):
    k, mm = w.shape
    p = w.reshape(k // 128, 128, mm // 128, 128).transpose(2, 1, 0, 3)
    if k < 1024:
        p = np.concatenate([p, np.zeros((p.shape[0], 128, 8 - k // 128, 128), np.float32)], 2)
    return p.reshape(-1, 128, 1024)


def _stream(w_ada, ffn_w1, ffn_w3, ffn_w2, w_in, w_br, w_out):
    P = plan()
    s = np.zeros((4 * P["blocks"], 128, 1024), np.float32)

    def put(key, panels):
        b = P[key][0]
        s[4 * b:4 * b + len(panels)] = panels

    def ada(g):
        l, n = g // ADA_GROUPS, g % ADA_GROUPS
        w = w_ada[l][:, 512 * n:512 * n + 512]
        return w.reshape(4, 2, 128, 512).transpose(0, 2, 1, 3).reshape(4, 128, 1024)

    def ada_run(key, n):
        b, (g0, _) = P[key][0], P["groups"][key]
        for i in range(n):
            s[4 * (b + i):4 * (b + i) + 4] = ada(g0 + i)

    qo = _q_order()
    for l in range(DEPTH):
        wi = w_in[l]
        if l == 0:
            ada_run(("ada", 0), 6)
        for f in range(2):
            at = 0
            for p, tiles in enumerate(PIECES):
                b = P[("up", l, f, p)][0]
                g0, rides = P[("rides", l, f, p)]
                cols = slice(128 * at, 128 * (at + tiles))
                w1, w3 = _panels(ffn_w1[l, f][:, cols]), _panels(ffn_w3[l, f][:, cols])
                for i in range(tiles // 2):
                    if rides:
                        s[4 * b:4 * b + 4] = ada(g0 + i)
                        b += 1
                    for k in range(2):
                        s[4 * b + 2 * k], s[4 * b + 2 * k + 1] = w1[2 * i + k], w3[2 * i + k]
                    b += 1
                put(("down", l, f, p), _panels(ffn_w2[l, f][cols]))
                at += tiles
            if f == 0:
                ada_run(("ada1", l), 1)
                parts = [_panels(wi[:, o:o + 1024]) for o in (ODN, ODN + 1024, ODN + 2048, OG)]
                put(("head", l), np.stack(parts, 1).reshape(-1, 128, 1024))
                for r, br in enumerate((2, 0, 1)):
                    wb = w_br[l, br]
                    if br == 0:
                        wb = wb[qo]
                    pr = np.stack([_panels(wi[:, OGZ + 1024 * br:OGZ + 1024 * br + 1024]), _panels(wb)], 1)
                    put(("br", l, r), pr.reshape(-1, 128, 1024))
                put(("kv", l), _panels(wi[:, OK:OK + 512]))
                put(("q", l), _panels(wi[:, OQ:OQ + 1024][:, qo]))
                parts = [_panels(wi[:, o:o + 1024]) for o in (O4, O5, O3)]
                put(("conv", l), np.stack(parts, 1).reshape(-1, 128, 1024))
                put(("out", l), _panels(w_out[l]))
            elif l == 0:
                ada_run(("ada2", 0), 2)
    return s


def _fm(v):
    return v.reshape(-1, 128).T


def _vectors(c, c_ctx, b_ada, norm_g, b_in, q_norm_g, k_norm_g, sc_conv, dn_conv, dn_norm_g, final_norm_g):
    v = np.zeros((128, NV), np.float32)
    for l in range(DEPTH):
        L, b = l * NVL, b_in[l]

        def put(at, x):
            v[:, L + at:L + at + x.shape[1]] = x

        put(V_KV, _fm(b[OK:OK + 512]))
        put(V_Q, _fm(b[OQ:OQ + 1024][_q_order()]))
        put(V_QG, np.concatenate([q_norm_g[l], q_norm_g[l]])[:, None])
        put(V_KG, np.concatenate([k_norm_g[l], k_norm_g[l]])[:, None])
        for n in range(DNH):
            at = V_HEAD + HV * n
            for j, o in enumerate((ODN, ODN + 1024, ODN + 2048, OG)):
                put(at + j, b[o + 128 * n:o + 128 * n + 128][:, None])
            for j in range(3):
                put(at + 4 + 3 * j, dn_conv[l][:, 1024 * j + 128 * n:1024 * j + 128 * n + 128].T)
        for n in range(KT):
            at = V_CONV + CV * n
            for j, o in enumerate((O4, O5, O3)):
                put(at + j, b[o + 128 * n:o + 128 * n + 128][:, None])
            put(at + 3, sc_conv[l][:, 128 * n:128 * n + 128].T)
        for r, br in enumerate((2, 0, 1)):
            put(V_GZ + 8 * r, _fm(b[OGZ + 1024 * br:OGZ + 1024 * br + 1024]))
        put(V_NG, _fm(norm_g[l].reshape(-1)))
        put(V_DNG, dn_norm_g[l][:, None])
        put(V_ADA, _fm(b_ada[l]))
    v[:, V_FG:V_FG + KT] = _fm(final_norm_g)
    v[:, V_C:V_C + 2 * KT:2] = _fm(c_ctx)
    v[:, V_C + 1:V_C + 2 * KT:2] = _fm(c[0])
    return v


def _rows(b_in, dn_dt_bias, dn_a_log):
    r = np.zeros((DEPTH, NR), np.float32)
    for l in range(DEPTH):
        r[l, R_AB:R_AB + 32] = b_in[l, OAB:OAB + 32]
        r[l, R_DT:R_DT + 16] = dn_dt_bias[l].reshape(-1)
        r[l, R_AL:R_AL + 16] = dn_a_log[l].reshape(-1)
    return np.ascontiguousarray(np.broadcast_to(r.reshape(1, -1), (128, DEPTH * NR)))


def kernel(**inputs):
    import concourse.bacc as bacc
    from concourse.bass_utils import run_bass_kernel_spmd

    a = {k: np.asarray(v) for k, v in inputs.items()}
    arrays = {
        "stream": _stream(*(a[k] for k in ("w_ada", "ffn_w1", "ffn_w3", "ffn_w2", "w_in", "w_br", "w_out"))),
        "h_in": np.ascontiguousarray(np.concatenate([a["ctx"][0], a["x"][0]]).T),
        "vecs": _vectors(*(a[k] for k in ("c", "c_ctx", "b_ada", "norm_g", "b_in", "q_norm_g", "k_norm_g", "sc_conv",
                                          "dn_conv", "dn_norm_g", "final_norm_g"))),
        "rows": _rows(a["b_in"], a["dn_dt_bias"], a["dn_a_log"]),
        "wab": np.ascontiguousarray(a["w_in"][:, :, OAB:OAB + 32].reshape(DEPTH, KT, 128, 32).transpose(2, 0, 1, 3)).reshape(128, -1),
        "consts": _tables(),
    }
    nc = bacc.Bacc("TRN2", target_bir_lowering=False, num_devices=1)
    aps = [nc.dram_tensor(k, v.shape, mybir.dt.float32, kind="ExternalInput").ap() for k, v in arrays.items()]
    out = nc.dram_tensor("out", (D, SEQ), mybir.dt.float32, kind="ExternalOutput").ap()
    build(nc, *aps, out)
    r = run_bass_kernel_spmd(nc, [arrays], core_ids=[0])
    return np.ascontiguousarray(np.asarray(r.results[0]["out"]).T)[None]
```

```python
from contextlib import ExitStack, contextmanager

import numpy as np
import concourse.bass as bass
from concourse import mybir

D = 1024
KT = D // 128
SEQ, CTX = 256, 256
T = CTX + SEQ
TC = T // 128
DEPTH = 2
HD = 64
NH, NKV = 16, 4
DNH = 8
DFF = 2816
FT = DFF // 128
EPS = 1e-6
NEG = -1.0e30
PIECES = (8, 8, 6)
assert sum(PIECES) == FT

OQ, OK, OV = 0, 1024, 1280
O3, O4, O5 = 1536, 2560, 3584
ODN, OG, OAB, OGZ = 4608, 7680, 8704, 8736
D_IN = 11808

V_KV = 0
V_Q = 4
V_QG, V_KG = 12, 13
V_HEAD = 14
HV = 13
V_CONV = V_HEAD + DNH * HV
CV = 6
V_GZ = V_CONV + KT * CV
V_NG = V_GZ + 24
V_DNG = V_NG + 24
V_ADA = V_DNG + 1
NVL = V_ADA + 72
V_FG = 2 * NVL
V_C = V_FG + KT
NV = V_C + 2 * KT

C_ID, C_OFF, C_ONE, C_BLK, C_PERM = 0, 128, 256, 384, 512
C_LV = 640
C_NM = C_LV + 7 * 128
C_CUM = C_NM + 256
C_COS, C_SIN = C_CUM + 256, C_CUM + 512
C_SEL = C_CUM + 768
NC = C_SEL + 2

R_AB, R_DT, R_AL = 0, 32, 48
NR = 64

HB_G, HB_GC, HB_NEG, HB_BETA, HB_KD, HB_TOT = range(6)
HBN = 48

ADA_GROUPS = 18


def plan():
    at, blk, gblk = {}, 0, 0

    def take(key, nblocks, gemm=True):
        nonlocal blk, gblk
        at[key] = (blk, gblk)
        blk += nblocks
        gblk += nblocks if gemm else 0

    groups = 0
    at["groups"] = {}

    def ada(key, n):
        nonlocal groups
        at["groups"][key] = (groups, n)
        groups += n
        take(key, n, False)

    for l in range(DEPTH):
        if l == 0:
            ada(("ada", 0), 6)
        for f in range(2):
            for p, tiles in enumerate(PIECES):
                n = tiles // 2
                rides = n if (f == 0 or (l == 0 and p == 0)) else 0
                at[("rides", l, f, p)] = (groups, rides)
                groups += rides
                at[("up", l, f, p)] = (blk, gblk)
                blk += n + rides
                gblk += n
                take(("down", l, f, p), 2)
            if f == 0:
                ada(("ada1", l), 1)
                take(("head", l), DNH)
                take(("kv", l), 1)
                take(("br", l, 0), 4)
                take(("q", l), 2)
                take(("br", l, 1), 4)
                take(("conv", l), 6)
                take(("br", l, 2), 4)
                take(("out", l), 2)
            elif l == 0:
                ada(("ada2", l), 2)
    assert groups == DEPTH * ADA_GROUPS
    at["blocks"], at["gblocks"] = blk, gblk
    return at


def build(nc, stream, h_in, vecs_in, rows_in, wab_in, consts_in, out):
    f32, f32r = mybir.dt.float32, mybir.dt.float32r
    ALU, ACT, AX = mybir.AluOpType, mybir.ActivationFunctionType, mybir.AxisListType
    ds = bass.ds
    P = plan()
    NB = P["blocks"]

    ctx = ExitStack()
    with ctx:
        def sb(name, shape, dt=f32):
            return ctx.enter_context(nc.sbuf_tensor(name, shape, dt))

        def sem(name):
            return ctx.enter_context(nc.semaphore(name))

        raw = sb("raw", [128, 4, 1024])
        whi = sb("whi", [128, 4, 1024], f32r)
        wlo = sb("wlo", [128, 4, 1024], f32r)
        h = sb("h", [128, KT, T])
        uh = sb("uh", [128, KT, T], f32r)
        ul = sb("ul", [128, KT, T], f32r)
        bh = sb("bh", [128, KT, T], f32r)
        bl = sb("bl", [128, KT, T], f32r)
        m = sb("m", [128, KT * T])
        cst = sb("cst", [128, NC])
        vec = sb("vec", [128, NV])
        rows = sb("row_vectors", [128, DEPTH, NR])
        kraw = sb("kraw", [128, T])
        idr = sb("idr", [128, 128], f32r)
        nidr = sb("nidr", [128, 128], f32r)
        cstat = sb("cstat", [128, KT, 128], f32r)
        csil = sb("csil", [128, KT, 2])
        mod = sb("mod", [128, DEPTH * 72, 2])
        normA = sb("normA", [128, KT, 2])
        hgate = sb("hgate", [128, KT, 2])
        tab = sb("tab", [128, DNH, HBN])
        hv = sb("hv", [128, HV])
        hb = sb("hb", [128, HBN])
        stat = sb("stat", [128, 32])
        scr = sb("scr", [128, 6160])
        scr_r = sb("scr_r", [128, 4, 2 * 512], f32r)
        bank = [ctx.enter_context(nc.psum_tensor(f"bank{i}", [128, 512], f32)) for i in range(8)]

        wab = m[:, 0:KT * 32]
        m3 = m[:, :].rearrange("p (k t) -> p k t", k=KT)
        ident = cst[:, C_ID:C_ID + 128]
        ones = cst[:, C_ONE:C_ONE + 128]

        def s_(a, n):
            return scr[:, a:a + n]

        nsq = s_(0, 1024).rearrange("p (a t) -> p a t", a=2)
        nvar, nrs = s_(1024, 512), s_(1536, 512)
        nut = s_(2048, 1024).rearrange("p (a t) -> p a t", a=2)
        sil = s_(3072, 1024).rearrange("p (a t) -> p a t", a=2)
        hbuf = s_(4096, 1024).rearrange("p (a t) -> p a t", a=2)
        arow = scr[0:4, 5120:5632]
        SM = s_(5120, 1024)

        pre = s_(0, 3 * 516).rearrange("p (j s t) -> p j s t", j=3, s=2)
        eg = s_(0, 1024).rearrange("p (d t) -> p d t", d=2)
        qkv = s_(1548, 1536).rearrange("p (j t) -> p j t", j=3)
        gate = s_(3084, 512)
        ktok = s_(3596, 512)
        vtok = s_(4108, 512)
        Gs = s_(4620, 512)
        KQs = s_(5132, 512)
        St = s_(5644, 512).rearrange("p (b d e) -> p b d e", b=2, d=2)
        Rr = s_(4620, 256).rearrange("p (d e) -> p d e", d=2)
        vn = s_(4876, 256).rearrange("p (d e) -> p d e", d=2)
        vd = s_(5132, 256).rearrange("p (d e) -> p d e", d=2)
        hsq = s_(4620, 1024).rearrange("p (d t) -> p d t", d=2)
        hrs = s_(0, 1024).rearrange("p (d t) -> p d t", d=2)
        DT = m[:, 0:1024].rearrange("p (d t) -> p d t", d=2)
        Qt = m[:, 1024:2048].rearrange("p (d t) -> p d t", d=2)
        eo = Qt
        AT = m[:, 2048:3072].rearrange("p (d t) -> p d t", d=2)
        IT = m[:, 3072:4096].rearrange("p (d t) -> p d t", d=2)
        XTf = DT
        ATr, X, XT, Pm = (scr_r[:, k, :].rearrange("p (d t) -> p d t", d=2) for k in range(4))
        wabh, wabl = scr_r[:, 0, 0:256], scr_r[:, 0, 256:512]

        kT = s_(0, 1024).rearrange("p (a t) -> p a t", a=2)
        vt = s_(1024, 1024).rearrange("p (a c f) -> p a c f", a=2, c=TC)
        qx = s_(2048, 2048).rearrange("p (a t) -> p a t", a=4)
        asq, ars = s_(4096, 512), s_(4608, 512)
        asw, ax = s_(5120, 512), s_(5632, 512)
        Pb = s_(4096, 1024).rearrange("p (a t) -> p a t", a=2)
        PT = s_(5120, 1024).rearrange("p (a t) -> p a t", a=2)
        c4 = s_(0, 512)
        cpr = s_(512, 516).rearrange("p (s t) -> p s t", s=2)
        cy = s_(1028, 512)
        cz = s_(1540, 1024).rearrange("p (a t) -> p a t", a=2)
        cvec = s_(2600, 4 * CV)

        raw_in = [sem("raw_in0"), sem("raw_in1")]
        hi_ready, lo_ready, panel_done = sem("hi_ready"), sem("lo_ready"), sem("panel_done")
        pair_done = [sem("pair_done0"), sem("pair_done1")]
        consts_loaded, vecs_loaded, h_loaded, wab_loaded = (sem(n) for n in (
            "consts_loaded", "vecs_loaded", "h_loaded", "wab_loaded"))
        setup_act, setup_dve = sem("setup_act"), sem("setup_dve")
        ada_row, ada_turned, mod_ready = (sem(n) for n in ("ada_row", "ada_turned", "mod_ready"))
        res_ready, norm_gain = sem("res_ready"), sem("norm_gain")
        sq_ready, sq_used, var_ready, rstd_ready, ut_ready, uh_ready, u_ready = (sem(n) for n in (
            "sq_ready", "sq_used", "var_ready", "rstd_ready", "ut_ready", "uh_ready", "u_ready"))
        sil_ready, hid_hi, hid_ready = sem("sil_ready"), sem("hid_hi"), sem("hid_ready")
        wab_reloaded, wab_hi, wab_lo = sem("wab_reloaded"), sem("wab_hi"), sem("wab_lo")
        ab_sum, ab_z, ab_exp, g_ready, gc_sum, tab_ready = (sem(n) for n in (
            "ab_sum", "ab_z", "ab_exp", "g_ready", "gc_sum", "tab_ready"))
        E = {n: sem(n) for n in (
            "hv_ready", "hb_ready", "pre_ready", "conv_ready", "silu_ready", "hsq_ready", "l2_sum", "l2_var", "l2_rstd",
            "kn_ready", "qn_ready", "kv_turned", "ktok_ready", "vtok_ready", "gram", "kq_ready",
            "gs_ready", "gc_row", "dm_ready", "dt_ready", "eg_ready", "qt_ready", "at_ready", "atr_ready", "it_ready",
            "xt0_ready", "xt0_turned", "p_sum", "pm_ready", "x_sum", "x_ready", "xt_ready",
            "ks_sum", "r_ready", "y_sum", "vn_ready", "vd_ready", "ds_sum", "s_ready", "o_sum", "osq_ready",
            "on_sum", "on_var", "on_rstd", "on_ready", "bh_ready", "head_ready")}
        dve_step, act_step = sem("dve_step"), sem("act_step")
        A = {n: sem(n) for n in (
            "a_x", "a_sq", "a_sum", "a_var", "a_rstd", "a_norm", "a_swap", "a_done", "a_vx", "a_vturn", "a_vtok",
            "s_sum", "s_max", "s_exp", "s_scaled", "s_turned", "s_pt", "s_pv", "att_hi", "att_ready")}
        C = {n: sem(n) for n in ("c_vec", "c_p4", "c_out", "c_hi", "br_gate", "mh_ready", "mx_ready")}
        out_ready, out_stored = sem("out_ready"), sem("out_stored")

        block = ctx.enter_context(nc.Block())

        class Steps:

            def __init__(self, eng, s):
                self.eng, self.s, self.base, self.k = eng, s, 0, 0

            def do(self, ins):
                ins.then_inc(self.s, 1)
                self.k += 1

            def sync(self):
                self.eng.wait_ge(self.s, self.base + self.k)

            @contextmanager
            def loop(self, start, stop, per):
                base, self.k = self.base + self.k, 0
                with self.eng.Fori(start, stop) as i:
                    self.base = base + (i - start) * per
                    yield i
                    assert self.k == per, (self.k, per)
                self.base, self.k = base + (stop - start) * per, 0

        def wait(eng, s, n):
            if not (isinstance(n, int) and n <= 0):
                eng.wait_ge(s, n)

        def have(eng, s, n):
            eng.wait_ge(s, n + 1)

        def conds(c0):
            return [(k, a, b) for k, a, b in ((0, 0, CTX), (1, CTX, T)) if a >= c0]

        def bc(ap, n, w):
            return ap.rearrange("p (a w) -> p a w", a=1).broadcast_to([128, n, w])

        def c4d(ap):
            return ap.rearrange("p (c t) -> p c t", c=TC)

        def norm_conds(n):
            return CTX if n >= 3 * DEPTH - 1 else 0

        def first_split(l, j):
            key = {0: ("up", l, 0, 0), 2: ("up", l, 1, 0)}.get(j)
            return P[key][0] + 1 if key and P[("rides", *key[1:])][1] else None

        def modc(l, jj):
            return l * 72 + jj * 8

        def chunk(d, s):
            return (0, 1, 2, 3)[s] if d == 0 else (1, 0, 3, 2)[s]

        def state_bank(d, follow):
            return (bank[7] if d == 0 else bank[2] if follow else bank[5])[:, 256:384]

        def hcol(kind, d, c):
            n = (kind * 2 + d) * 4 + c
            return slice(n, n + 1)

        def att_units(l):
            kinds = ((2, 3) if l == DEPTH - 1 else (0, 2, 3))
            return [(j, a, k) for j in range(4) for a in range(2) for k in kinds]

        def att_units_before(l, p):
            return sum(2 * len(att_units(k)) for k in range(l)) + p * len(att_units(l))

        @block.sync
        def _(sp):
            sp.dma_start(cst[:, :], consts_in).then_inc(consts_loaded, 16)
            sp.dma_start(vec[:, :], vecs_in).then_inc(vecs_loaded, 16)

            def load(b, r):
                sp.dma_start(raw[:, 2 * r:2 * r + 2, :],
                             stream[ds(4 * b + 2 * r, 2), :, :].rearrange("g p n -> p g n")).then_inc(raw_in[r], 16)

            load(0, 0)
            load(0, 1)
            sp.dma_start(h[:, :, :], h_in.rearrange("(k p) t -> p k t", p=128)).then_inc(h_loaded, 16)
            sp.dma_start(wab, wab_in[:, 0:KT * 32]).then_inc(wab_loaded, 16)
            sp.dma_start(rows[:, :, :].rearrange("p l n -> p (l n)"), rows_in).then_inc(wab_loaded, 16)
            with sp.Fori(1, NB) as b:
                for r in range(2):
                    sp.wait_ge(lo_ready, 4 * (b - 1) + 2 * r + 2)
                    load(b, r)
            for t in range(KT):
                sp.wait_ge(out_ready, t + 1)
                sp.dma_start(out.rearrange("(k p) t -> p k t", p=128)[:, t, :], m3[:, t, 0:SEQ]).then_inc(out_stored, 16)
            sp.wait_ge(out_stored, 16 * KT)

        @block.gpsimd
        def _(pool):
            for l in range(1, DEPTH):
                pool.wait_ge(C["mx_ready"], 8 * l)
                pool.dma_start(wab, wab_in[:, l * KT * 32:(l + 1) * KT * 32]).then_inc(wab_reloaded, 16)

        @block.scalar
        def _(act):
            steps = Steps(act, act_step)

            def split(B, j):
                if isinstance(B, int) and B >= NB:
                    return
                if j % 2 == 0:
                    act.wait_ge(raw_in[j // 2], 16 * (B + 1))
                if not (isinstance(B, int) and B == 0):
                    act.wait_ge(panel_done, 4 * (B - 1) + j + 1)
                act.activation(whi[:, j, :], raw[:, j, :], ACT.Copy).then_inc(hi_ready, 1)

            def log_exp():
                act.preload_act_table_set("natural_log_exp_and_others")

            def rsqrt(out_, in_, ready):
                steps.do(act.activation(out_, in_, ACT.Ln))
                steps.sync()
                act.activation(out_, out_, ACT.Exp, scale=-0.5).then_inc(ready, 1)

            act.sem_inc(ada_row, 1)
            act.wait_ge(consts_loaded, 16)
            act.activation(idr[:, :], ident, ACT.Copy)
            act.activation(nidr[:, :], ident, ACT.Copy, scale=-1.0).then_inc(setup_act, 1)
            act.wait_ge(vecs_loaded, 16)
            steps.do(act.activation(csil[:, :, :], vec[:, V_C:V_C + 16].rearrange("p (k c) -> p k c", c=2), ACT.Silu))
            steps.sync()
            act.wait_ge(setup_dve, 1)
            act.activation(cstat[:, :, 0:2], csil[:, :, :], ACT.Copy).then_inc(setup_act, 1)
            for j in range(4):
                split(0, j)

            def ada_panels(B):
                for j in range(4):
                    split(B + 1, j)

            def ada_evac(n, B):
                act.wait_ge(panel_done, 4 * B + 4)
                have(act, ada_turned, n)
                act.activation(arow[:, :], bank[4][0:4, :], ACT.Copy).then_inc(ada_row, 1)

            def ada_only(key):
                B0, _ = P[key]
                g0, n = P["groups"][key]
                with act.Fori(0, n) as i:
                    ada_panels(B0 + i)
                    ada_evac(g0 + i, B0 + i)

            def square(n, t):
                c0 = norm_conds(n)
                wait(act, sq_used, 8 * n + t - 1)
                act.activation(nsq[:, t % 2, c0:T], h[:, t, c0:T], ACT.Square).then_inc(sq_ready, 1)

            def norm_rstd(n):
                c0 = norm_conds(n)
                log_exp()
                act.wait_ge(var_ready, n + 1)
                rsqrt(nrs[:, c0:T], nvar[:, c0:T], rstd_ready)

            def norm(n, l, j):
                c0 = norm_conds(n)
                sh = modc(l, 3 * j)
                B = first_split(l, j)
                act.wait_ge(norm_gain, n + 1)
                for t in range(KT):
                    if B is not None and t in (0, 4):
                        split(B, t // 2)
                        split(B, t // 2 + 1)
                    act.wait_ge(ut_ready, 8 * n + t + 1)
                    for k, a, b in conds(c0):
                        steps.do(act.activation(nut[:, t % 2, a:b], nut[:, t % 2, a:b], ACT.Identity,
                                                scale=normA[:, t, k:k + 1], bias=mod[:, sh + t, k:k + 1]))
                    steps.sync()
                    act.activation(uh[:, t, c0:T], nut[:, t % 2, c0:T], ACT.Copy).then_inc(uh_ready, 1)

            def last_residual(B0, G0, n):
                for i in range(2):
                    for j in range(4):
                        t = 4 * i + j
                        if j % 2:
                            have(act, pair_done[j // 2], G0 + i + 1)
                        else:
                            act.wait_ge(res_ready, 4 * (n - 1) + t // 2 + 1)
                        square(n, t)
                        split(B0 + i + 1, j)

            def ffn(l, f):
                c0 = CTX if l == DEPTH - 1 and f == 1 else 0
                occ = 2 * l + f
                tile0 = occ * FT
                for p, tiles in enumerate(PIECES):
                    B0, G0 = P[("up", l, f, p)]
                    g0, rides = P[("rides", l, f, p)]
                    per = 2 if rides else 1
                    act.wait_ge(panel_done, 4 * B0)

                    def step(i, first):
                        B, G, n0 = B0 + per * i, G0 + i, tile0 + 2 * i
                        if rides:
                            if not first:
                                ada_panels(B)
                            ada_evac(g0 + i, B)
                            B = B + 1
                        for k in range(2):
                            split(B + 1, 2 * k)
                            act.wait_ge(panel_done, 4 * B + 2 * k + 1)
                            have(act, pair_done[k], G)
                            act.activation(sil[:, k, c0:T], bank[2 * k][:, c0:T], ACT.Silu).then_inc(sil_ready, 1)
                            split(B + 1, 2 * k + 1)
                            have(act, pair_done[k], G + 1)
                            act.activation(bh[:, ds(2 * i + k, 1), c0:T].rearrange("p a t -> p (a t)"), hbuf[:, k, c0:T],
                                           ACT.Copy).then_inc(hid_hi, 1)

                    if p == 0:
                        step(0, True)
                    with act.Fori(1 if p == 0 else 0, tiles // 2) as i:
                        step(i, False)
                    tile0 += tiles
                    B0, G0 = P[("down", l, f, p)]
                    if p == len(PIECES) - 1:
                        last_residual(B0, G0, 3 * l + 1 + 2 * f)
                        continue
                    with act.Fori(0, 2) as i:
                        for j in range(4):
                            split(B0 + i + 1, j)

            def ab(l):
                if l:
                    act.wait_ge(wab_reloaded, 16 * l)
                else:
                    act.wait_ge(wab_loaded, 32)
                act.activation(wabh, wab, ACT.Copy).then_inc(wab_hi, 1)
                act.wait_ge(ab_z, 2 * l + 1)
                act.activation(SM[:, 128:192], SM[:, 64:128], ACT.Exp)
                act.activation(SM[:, 192:256], SM[:, 960:1024], ACT.Exp, scale=-1.0)
                steps.do(act.activation(SM[:, 256:272], rows[:, l, R_AL:R_AL + 16], ACT.Exp))
                steps.sync()
                act.activation(SM[:, 320:384], SM[:, 128:192], ACT.Ln, bias=1.0).then_inc(ab_exp, 1)
                act.wait_ge(ab_z, 2 * l + 2)
                act.activation(SM[:, 640:704], SM[:, 448:512], ACT.Exp)
                act.activation(SM[:, 704:768], SM[:, 512:576], ACT.Exp)
                act.activation(SM[:, 768:832], SM[:, 576:640], ACT.Exp).then_inc(ab_exp, 1)

            def prep_in(l, b, n):
                s0 = 1 if l == DEPTH - 1 else 0
                j = (1, 0, 2)[n]
                a = s0 if j == 0 else 0
                act.wait_ge(E["hv_ready"], l * DNH + b + 1)
                act.wait_ge(panel_done, 4 * (P[("head", l)][0] + b) + (3 if j == 2 else 2))
                act.activation(pre[:, j, a:2, 1:257], bank[j][:, :].rearrange("p (s t) -> p s t", s=2)[:, a:2, :], ACT.Identity,
                               bias=hv[:, j:j + 1]).then_inc(E["pre_ready"], 1)

            def prep_silu(l, b, n):
                c0 = CTX if l == DEPTH - 1 else 0
                o = l * DNH + b
                j = (1, 0, 2)[n]
                a = c0 if j == 0 else 0
                x = kraw if j == 1 else qkv[:, j, :]
                act.wait_ge(E["conv_ready"], 3 * o + n + 1)
                act.activation(x[:, a:T], x[:, a:T], ACT.Silu).then_inc(E["silu_ready"], 1)
                if j != 2:
                    act.wait_ge(E["silu_ready"], 3 * o + n + 1)
                    act.activation(hsq[:, n, a:T], x[:, a:T], ACT.Square).then_inc(E["hsq_ready"], 1)

            def prep_rsqrt(l, b, n):
                c0 = CTX if l == DEPTH - 1 else 0
                a = c0 if n else 0
                act.wait_ge(E["l2_var"], 2 * (l * DNH + b) + n + 1)
                rsqrt(hrs[:, n, a:T], hrs[:, n, a:T], E["l2_rstd"])

            def gate_in(l, b):
                B0, G0 = P[("head", l)]
                c0 = CTX if l == DEPTH - 1 else 0
                act.wait_ge(panel_done, 4 * (B0 + b) + 4)
                act.activation(gate[:, c0:T], bank[3][:, c0:T], ACT.Identity, bias=hv[:, 3:4]).then_inc(pair_done[1], 1)

            def output_and_front(l, b, output, front):
                c0 = CTX if l == DEPTH - 1 else 0
                o, f = l * DNH + b - 1, l * DNH + b

                def decay(d):
                    act.wait_ge(E["dm_ready"], 2 * f + d + 1)
                    act.activation(DT[:, d, :], DT[:, d, :], ACT.Exp).then_inc(E["dt_ready"], 1)

                def low_a(d):
                    act.wait_ge(E["at_ready"], 2 * f + d + 1)
                    act.activation(ATr[:, d, :], AT[:, d, :], ACT.Copy).then_inc(E["atr_ready"], 1)

                def x_first(d):
                    act.wait_ge(E["xt0_turned"], 2 * f + d + 1)
                    act.activation(X[:, d, :], bank[6 + d][:, :], ACT.Copy).then_inc(E["x_ready"], 1)

                if output:
                    act.wait_ge(E["o_sum"], o + 1)
                    act.activation(eo[:, 0, c0:T], bank[6][:, c0:T], ACT.Square).then_inc(E["osq_ready"], 1)
                if front:
                    decay(0)
                if output:
                    act.wait_ge(E["on_var"], o + 1)
                    rsqrt(eo[:, 1, c0:T], eo[:, 1, c0:T], E["on_rstd"])
                if front:
                    decay(1)
                    act.activation(eg[:, 0, c0:T], bank[4][:, c0:T], ACT.Exp).then_inc(E["eg_ready"], 1)
                    act.wait_ge(E["kv_turned"], 2 * f + 2)
                    act.activation(ktok, bank[1][:, :], ACT.Copy).then_inc(E["ktok_ready"], 1)
                    act.wait_ge(E["qn_ready"], f + 1)
                    act.activation(eg[:, 1, c0:T], bank[5][:, c0:T], ACT.Exp).then_inc(E["eg_ready"], 1)
                if output:
                    act.wait_ge(E["on_ready"], o + 1)
                    act.activation(bh[:, ds(b - 1, 1), c0:T].rearrange("p a t -> p (a t)"), gate[:, c0:T],
                                   ACT.Copy).then_inc(E["bh_ready"], 1)
                if not front:
                    return
                low_a(0)
                act.wait_ge(E["gram"], 2 * f + 2)
                act.activation(KQs[:, c0:T], bank[2][:, c0:T], ACT.Copy).then_inc(E["kq_ready"], 1)
                x_first(0)
                low_a(1)
                if output:
                    have(act, E["head_ready"], o + 1)
                gate_in(l, b)
                x_first(1)

            def head(l, b, follow):
                c0 = CTX if l == DEPTH - 1 else 0
                B0, G0 = P[("head", l)]
                B = B0 + b
                o = l * DNH + b - 1
                for v in range(1, 7):
                    for d in range(2):
                        x = 22 * o + (4 * (v - 1) + 2 * d if v < 6 else 20 + d)
                        act.wait_ge(E["x_sum"], x + 1)
                        act.activation(X[:, d, :], bank[6 + d][:, :], ACT.Copy).then_inc(E["x_ready"], 1)
                        if v < 6:
                            act.wait_ge(E["x_sum"], x + 2)
                            act.activation(XT[:, d, :], bank[4 + d][:, :], ACT.Copy).then_inc(E["xt_ready"], 1)
                        if (v, d) == (1, 0):
                            split(B, 3)
                        if (v, d) == (3, 0):
                            split(B + 1, 0)
                        if (v, d) == (5, 0):
                            split(B + 1, 1)
                        if follow and (v, d) == (1, 1):
                            prep_in(l, b, 0)
                            prep_in(l, b, 1)
                        if (v, d) == (2, 1):
                            have(act, pair_done[1], G0 + b)
                            act.activation(gate[:, c0:T], gate[:, c0:T], ACT.Silu)
                        if follow and (v, d) == (3, 1):
                            prep_silu(l, b, 0)
                        if follow and (v, d) == (4, 1):
                            prep_silu(l, b, 1)
                        if follow and (v, d) == (5, 1):
                            prep_in(l, b, 2)
                for d in range(2):
                    act.wait_ge(E["p_sum"], 18 * o + 12 + 2 * d + 1)
                    act.activation(XT[:, d, :], bank[4 + d][:, :], ACT.Copy).then_inc(E["xt_ready"], 1)
                    act.wait_ge(E["p_sum"], 18 * o + 12 + 2 * d + 2)
                    act.activation(Pm[:, d, :], bank[6 + d][:, :], ACT.Copy).then_inc(E["pm_ready"], 1)
                if follow:
                    prep_silu(l, b, 2)
                split(B + 1, 2)
                log_exp()
                if follow:
                    prep_rsqrt(l, b, 0)
                    prep_rsqrt(l, b, 1)
                output_and_front(l, b, True, follow)

            def heads(l):
                B0 = P[("head", l)][0]
                act.wait_ge(panel_done, 4 * B0)
                act.wait_ge(tab_ready, l + 1)
                for n in range(3):
                    prep_in(l, 0, n)
                for n in range(3):
                    prep_silu(l, 0, n)
                split(B0 + 1, 0)
                split(B0 + 1, 1)
                log_exp()
                for n in range(2):
                    prep_rsqrt(l, 0, n)
                output_and_front(l, 0, False, True)
                split(B0 + 1, 2)
                with steps.loop(1, DNH - 1, 3) as b:
                    head(l, b, True)
                head(l, DNH - 1, True)
                head(l, DNH, False)
                split(B0 + DNH + 1, 3)

            def branch(l, r):
                B0, G0 = P[("br", l, r)]
                c0 = CTX if l == DEPTH - 1 else 0
                n0 = (3 * l + r) * 8

                def step(i):
                    for k in range(2):
                        if r == 0 and isinstance(i, int):
                            norm_k(l, k)
                        split(B0 + i + 1, 2 * k)
                        act.wait_ge(panel_done, 4 * (B0 + i) + 2 * k + 1)
                        have(act, pair_done[k], G0 + i)
                        act.activation(sil[:, k, c0:T], bank[2 * k][:, c0:T], ACT.Sigmoid,
                                       bias=vec[:, ds(l * NVL + V_GZ + 8 * r + 2 * i + k, 1)]).then_inc(C["br_gate"], 1)
                        split(B0 + i + 1, 2 * k + 1)

                if r == 0:
                    step(0)
                with act.Fori(1 if r == 0 else 0, 4) as i:
                    step(i)

            def bias_in(j, bcol, dst, c0):
                act.activation(dst[:, c0:T], bank[j][:, c0:T], ACT.Identity, bias=vec[:, bcol:bcol + 1]).then_inc(A["a_x"], 1)

            def norm_k(l, k):
                wait(act, A["a_done"], 10 * l + k)
                qk_norm(10 * l + k, kT[:, k, :], 0)

            def qk_norm(na, x, c0):
                act.wait_ge(A["a_x"], na + 1)
                act.activation(asq[:, c0:T], x[:, c0:T], ACT.Square).then_inc(A["a_sq"], 1)
                log_exp()
                act.wait_ge(A["a_var"], na + 1)
                rsqrt(ars[:, c0:T], ars[:, c0:T], A["a_rstd"])

            def attention_kv(l):
                B0, _ = P[("kv", l)]
                L = l * NVL
                have(act, E["head_ready"], DNH * (l + 1))
                act.wait_ge(panel_done, 4 * B0 + 4)
                for j in range(2):
                    bias_in(j, L + V_KV + j, kT[:, j, :], 0)
                act.wait_ge(A["a_x"], 10 * l + 2)
                act.sem_inc(pair_done[0], 1)
                for j in range(2):
                    act.activation(qx[:, j, :], bank[2 + j][:, :], ACT.Identity,
                                   bias=vec[:, L + V_KV + 2 + j:L + V_KV + 3 + j]).then_inc(A["a_vx"], 1)
                act.wait_ge(A["a_vx"], 2 * l + 2)
                act.sem_inc(pair_done[1], 1)

            def attention(l):
                c0 = CTX if l == DEPTH - 1 else 0
                L = l * NVL
                na = 10 * l + 2
                nu = att_units_before(l, 0)
                for p in range(2):
                    B, G = P[("q", l)][0] + p, P[("q", l)][1] + p
                    for j in range(4):
                        split(B + 1, j)
                        wait(act, A["a_done"], na)
                        bias_in(j, L + V_Q + 4 * p + j, ax, c0)
                        qk_norm(na, ax, c0)
                        na += 1
                    act.wait_ge(A["a_done"], na)
                    units = att_units(l)

                    def evac_pt(u):
                        act.wait_ge(A["s_turned"], nu + u + 1)
                        act.activation(PT[:, u % 2, :], bank[6 + u % 2][:, :], ACT.Copy).then_inc(A["s_pt"], 1)

                    for u, (j, a, lat) in enumerate(units):
                        act.wait_ge(A["s_max"], nu + u + 1)
                        if u >= 2:
                            act.wait_ge(A["s_turned"], nu + u - 1)
                        for q in range(1 if lat else 2):
                            w = 512 if lat else 256
                            st = 8 * (u % 2) + q
                            last = act.activation(Pb[:, u % 2, q * w:(q + 1) * w], bank[4 + u % 2][:, q * w:(q + 1) * w], ACT.Exp,
                                                  scale=HD ** -0.5, bias=stat[:, st + 2:st + 3], accum_out=stat[:, st + 4:st + 5])
                        last.then_inc(A["s_exp"], 1)
                        if u:
                            evac_pt(u - 1)
                    evac_pt(len(units) - 1)
                    nu += len(units)
                    for j in range(4):
                        act.wait_ge(A["s_pv"], nu)
                        act.activation(bh[:, 4 * p + j, c0:T], bank[j][:, c0:T], ACT.Copy).then_inc(A["att_hi"], 1)

            def conv(l):
                B0, G0 = P[("conv", l)]
                c0 = CTX if l == DEPTH - 1 else 0
                with steps.loop(0, 2, 0) as i:
                    B = B0 + 3 * i
                    n0 = 8 * l + 4 * i
                    for t in range(4):
                        q = 3 * t
                        split(B + q // 4 + 1, q % 4)
                        act.wait_ge(panel_done, 4 * B + q + 1)
                        act.wait_ge(C["c_vec"], 2 * l + i + 1)
                        have(act, C["c_out"], n0 + t)
                        act.activation(c4[:, c0:T], bank[q % 4][:, c0:T], ACT.Identity,
                                       bias=cvec[:, t * CV:t * CV + 1]).then_inc(C["c_p4"], 1)
                        split(B + (q + 1) // 4 + 1, (q + 1) % 4)
                        split(B + (q + 2) // 4 + 1, (q + 2) % 4)
                        have(act, C["c_out"], n0 + t + 1)
                        act.activation(bh[:, ds(4 * i + t, 1), c0:T].rearrange("p a t -> p (a t)"), cz[:, t % 2, c0:T],
                                       ACT.Copy).then_inc(C["c_hi"], 1)

            def project_out(l):
                B0, G0 = P[("out", l)]
                c0 = CTX if l == DEPTH - 1 else 0
                act.wait_ge(panel_done, 4 * B0)
                have(act, pair_done[1], G0)
                for t in range(KT):
                    act.activation(uh[:, t, c0:T], m3[:, t, c0:T], ACT.Copy).then_inc(C["mh_ready"], 1)
                last_residual(B0, G0, 3 * l + 2)

            act.wait_ge(h_loaded, 16)
            for t in range(KT):
                square(0, t)
            norm_rstd(0)
            ada_only(("ada", 0))
            for l in range(DEPTH):
                norm(3 * l, l, 0)
                ffn(l, 0)
                norm_rstd(3 * l + 1)
                ada_only(("ada1", l))
                norm(3 * l + 1, l, 1)
                ab(l)
                heads(l)
                attention_kv(l)
                branch(l, 0)
                attention(l)
                branch(l, 1)
                conv(l)
                branch(l, 2)
                project_out(l)
                norm_rstd(3 * l + 2)
                norm(3 * l + 2, l, 2)
                ffn(l, 1)
                norm_rstd(3 * l + 3)
                if l == 0:
                    ada_only(("ada2", 0))

        @block.vector
        def _(dve):
            steps = Steps(dve, dve_step)
            stt = dve.scalar_tensor_tensor

            def split(B, j):
                if isinstance(B, int) and B >= NB:
                    return
                dve.wait_ge(hi_ready, 4 * B + j + 1)
                dve.tensor_tensor(wlo[:, j, :], raw[:, j, :], whi[:, j, :].bitcast(f32), ALU.subtract).then_inc(lo_ready, 1)

            for s in (*pair_done, mod_ready, E["head_ready"], C["c_out"]):
                dve.sem_inc(s, 1)
            dve.memset(cstat[:, :, :].bitcast(f32), 0.0).then_inc(setup_dve, 1)
            dve.wait_ge(setup_act, 2)
            dve.wait_ge(setup_dve, 1)
            dve.tensor_tensor(cstat[:, :, 2:4], csil[:, :, :], cstat[:, :, 0:2].bitcast(f32), ALU.subtract).then_inc(setup_dve, 1)
            for j in range(4):
                split(0, j)

            def ada_panels(B):
                for j in range(4):
                    split(B + 1, j)

            def ada_mod(g, l, local):
                have(dve, ada_turned, g + 1)
                b0 = l * NVL + V_ADA + 4 * local
                bias = vec[:, ds(b0, 4)].rearrange("p (a b) -> p a b", b=1).broadcast_to([128, 4, 2])
                dve.tensor_tensor(mod[:, ds(4 * g, 4), :], bank[5][:, 0:8].rearrange("p (a b) -> p a b", b=2), bias,
                                  ALU.add).then_inc(mod_ready, 1)

            def ada_only(key):
                B0, _ = P[key]
                g0, n = P["groups"][key]
                with dve.Fori(0, n) as i:
                    ada_panels(B0 + i)
                    ada_mod(g0 + i, g0 // ADA_GROUPS, (g0 % ADA_GROUPS) + i)

            def norm_var(n):
                c0 = norm_conds(n)
                dve.wait_ge(sq_used, 8 * n + 8)
                dve.tensor_scalar(nvar[:, c0:T], bank[6][:, c0:T], 1.0 / D, EPS, ALU.mult, ALU.add).then_inc(var_ready, 1)

            def norm(n, l, j):
                c0 = norm_conds(n)
                if j is not None:
                    have(dve, mod_ready, ADA_GROUPS * l + 6 * (j + 1))
                    sc = modc(l, 3 * j + 1)
                    g = vec[:, l * NVL + V_NG + 8 * j:l * NVL + V_NG + 8 * j + 8]
                    g = g.rearrange("p (a b) -> p a b", b=1).broadcast_to([128, KT, 2])
                    stt(out=normA[:, :, :], in0=mod[:, sc:sc + 8, :], scalar=1.0, in1=g, op0=ALU.add,
                        op1=ALU.mult).then_inc(norm_gain, 1)
                    gt = modc(l, 3 * j + 2)
                    steps.do(dve.tensor_scalar(hgate[:, :, :], mod[:, gt:gt + 8, :], 1.0 if j == 1 else 0.5, None, ALU.mult))
                    steps.sync()
                    B = first_split(l, j)
                dve.wait_ge(rstd_ready, n + 1)

                def low(t):
                    dve.wait_ge(uh_ready, 8 * n + t + 1)
                    dve.tensor_tensor(ul[:, t, c0:T], nut[:, t % 2, c0:T], uh[:, t, c0:T].bitcast(f32), ALU.subtract).then_inc(u_ready, 1)

                for t in range(KT):
                    if j is None:
                        f = vec[:, V_FG + t:V_FG + t + 1]
                        stt(out=m3[:, t, 0:SEQ], in0=h[:, t, CTX:T], scalar=f, in1=nrs[:, CTX:T],
                            op0=ALU.mult, op1=ALU.mult).then_inc(out_ready, 1)
                        continue
                    if B is not None and t in (0, 4):
                        split(B, t // 2)
                        split(B, t // 2 + 1)
                    wait(dve, u_ready, 8 * n + t - 1)
                    dve.tensor_tensor(nut[:, t % 2, c0:T], h[:, t, c0:T], nrs[:, c0:T], ALU.mult).then_inc(ut_ready, 1)
                    if t:
                        low(t - 1)
                if j is not None:
                    low(KT - 1)

            def last_residual(B0, G0, c0):
                for i in range(2):
                    for j in range(4):
                        t = 4 * i + j
                        dve.wait_ge(panel_done, 4 * (B0 + i) + j + 1)
                        for k, a, b in conds(c0):
                            last = stt(out=h[:, t, a:b], in0=bank[j][:, a:b], scalar=hgate[:, t, k:k + 1],
                                       in1=h[:, t, a:b], op0=ALU.mult, op1=ALU.add)
                        last.then_inc(pair_done[j // 2] if j % 2 else res_ready, 1)
                        split(B0 + i + 1, j)

            def residual(B, G, t0, c0):
                for j in range(4):
                    split(B + 1, j)
                    dve.wait_ge(panel_done, 4 * B + j + 1)
                    for k, a, b in conds(c0):
                        t = t0 + j
                        hh = h[:, ds(t, 1), a:b].rearrange("p a t -> p (a t)")
                        last = stt(out=hh, in0=bank[j][:, a:b], scalar=hgate[:, ds(t, 1), k:k + 1].rearrange("p a t -> p (a t)"),
                                   in1=hh, op0=ALU.mult, op1=ALU.add)
                    if j % 2:
                        last.then_inc(pair_done[j // 2], 1)

            def ffn(l, f):
                c0 = CTX if l == DEPTH - 1 and f == 1 else 0
                tile0 = (2 * l + f) * FT
                for p, tiles in enumerate(PIECES):
                    B0, G0 = P[("up", l, f, p)]
                    g0, rides = P[("rides", l, f, p)]
                    per = 2 if rides else 1
                    dve.wait_ge(panel_done, 4 * B0)

                    def step(i, first):
                        B, G, n0 = B0 + per * i, G0 + i, tile0 + 2 * i
                        if rides:
                            if not first:
                                ada_panels(B)
                            B = B + 1
                        for k in range(2):
                            split(B + 1, 2 * k)
                            if rides and k == 0:
                                ada_mod(g0 + i, g0 // ADA_GROUPS, (g0 % ADA_GROUPS) + i)
                            dve.wait_ge(sil_ready, n0 + k + 1)
                            dve.wait_ge(panel_done, 4 * B + 2 * k + 2)
                            dve.tensor_tensor(hbuf[:, k, c0:T], sil[:, k, c0:T], bank[2 * k + 1][:, c0:T],
                                              ALU.mult).then_inc(pair_done[k], 1)
                            split(B + 1, 2 * k + 1)
                            dve.wait_ge(hid_hi, n0 + k + 1)
                            dve.tensor_tensor(bl[:, ds(2 * i + k, 1), c0:T].rearrange("p a t -> p (a t)"), hbuf[:, k, c0:T],
                                              bh[:, ds(2 * i + k, 1), c0:T].rearrange("p a t -> p (a t)").bitcast(f32),
                                              ALU.subtract).then_inc(hid_ready, 1)

                    if p == 0:
                        step(0, True)
                    with dve.Fori(1 if p == 0 else 0, tiles // 2) as i:
                        step(i, False)
                    tile0 += tiles
                    B0, G0 = P[("down", l, f, p)]
                    have(dve, pair_done[1], G0)
                    if p == len(PIECES) - 1:
                        last_residual(B0, G0, c0)
                    else:
                        with dve.Fori(0, 2) as i:
                            residual(B0 + i, G0 + i, 4 * i, c0)
                    have(dve, pair_done[0], G0 + 2)
                    have(dve, pair_done[1], G0 + 2)

            def ab(l):
                q = lambda a: SM[:, a:a + 64]
                q3 = lambda a: q(a).rearrange("p (c n) -> p c n", c=TC)
                row = lambda a, n: rows[:, l, a:a + n].rearrange("p (c n) -> p c n", c=1).broadcast_to([128, TC, n])
                dve.wait_ge(wab_hi, l + 1)
                dve.tensor_tensor(wabl, wab, wabh.bitcast(f32), ALU.subtract).then_inc(wab_lo, 1)
                dve.wait_ge(ab_sum, l + 1)
                ps = bank[7][:, 0:128].rearrange("p (c n) -> p c n", c=TC)
                dve.tensor_tensor(q3(0), ps[:, :, 0:16], row(R_AB, 16), ALU.add)
                steps.do(dve.tensor_tensor(q3(960), ps[:, :, 16:32], row(R_AB + 16, 16), ALU.add))
                steps.sync()
                steps.do(dve.tensor_tensor(q3(0), q3(0), row(R_DT, 16), ALU.add))
                steps.sync()
                stt(out=q(64), in0=q(0), scalar=-1.0, in1=q(0), op0=ALU.mult, op1=ALU.min).then_inc(ab_z, 1)
                dve.wait_ge(ab_exp, 2 * l + 1)
                steps.do(stt(out=q(384), in0=q(0), scalar=0.0, in1=q(320), op0=ALU.max, op1=ALU.add))
                steps.do(dve.tensor_scalar(q(832), q(192), 1.0, None, ALU.add))
                steps.sync()
                al = SM[:, 256:272].rearrange("p (c n) -> p c n", c=1).broadcast_to([128, TC, 16])
                stt(out=q3(384), in0=q3(384), scalar=-1.0, in1=al, op0=ALU.mult, op1=ALU.mult).then_inc(g_ready, 1)
                steps.do(dve.reciprocal(q(832), q(832)))
                dve.wait_ge(gc_sum, l + 1)
                dve.tensor_copy(q(448), bank[7][:, 128:192])
                steps.do(dve.tensor_copy(q(512), bank[7][:, 192:256]))
                steps.sync()
                dve.tensor_tensor(q(576), q(512), q(448), ALU.subtract).then_inc(ab_z, 1)
                dve.wait_ge(ab_exp, 2 * l + 2)
                dve.wait_ge(ab_z, 2 * l + 2)
                steps.do(dve.tensor_scalar(q(640), q(640), -1.0, None, ALU.mult))
                steps.do(dve.tensor_tensor(q(768), q(768), q(832), ALU.mult))
                steps.sync()
                for kind, src in ((HB_G, 384), (HB_GC, 448), (HB_NEG, 640), (HB_BETA, 832), (HB_KD, 768), (HB_TOT, 704)):
                    for d in range(2):
                        dst = tab[:, :, (kind * 2 + d) * 4:(kind * 2 + d) * 4 + 4]
                        s = q(src).rearrange("p (c d h) -> p h d c", c=TC, d=2)[:, :, d, :]
                        last = dve.tensor_copy(dst, s)
                last.then_inc(tab_ready, 1)

            def prep_vec(l, b):
                G0 = P[("head", l)][1]
                v0 = V_HEAD + l * NVL + HV * b
                have(dve, pair_done[1], G0 + b)
                dve.tensor_copy(hv[:, :], vec[:, ds(v0, HV)]).then_inc(E["hv_ready"], 1)
                for j in range(3):
                    steps.do(dve.memset(pre[:, j, :, 0:1], 0.0))
                    steps.do(dve.memset(pre[:, j, :, 257:258], 0.0))
                steps.sync()

            def prep_conv(l, b, n):
                c0 = CTX if l == DEPTH - 1 else 0
                s0 = c0 // CTX
                o = l * DNH + b
                j = (1, 0, 2)[n]
                a = s0 if j == 0 else 0
                dve.wait_ge(E["hv_ready"], o + 1)
                dve.wait_ge(E["pre_ready"], 3 * o + n + 1)
                x = kraw[:, :] if j == 1 else qkv[:, j, :]
                y = x.rearrange("p (s t) -> p s t", s=2)[:, a:2, :]
                tap = lambda i: hv[:, 4 + 3 * j + i:5 + 3 * j + i]
                steps.do(dve.tensor_scalar(y, pre[:, j, a:2, 0:256], tap(0), None, ALU.mult))
                steps.sync()
                steps.do(stt(out=y, in0=pre[:, j, a:2, 1:257], scalar=tap(1), in1=y, op0=ALU.mult, op1=ALU.add))
                steps.sync()
                stt(out=y, in0=pre[:, j, a:2, 2:258], scalar=tap(2), in1=y, op0=ALU.mult, op1=ALU.add).then_inc(E["conv_ready"], 1)

            def prep_var(l, b):
                c0 = CTX if l == DEPTH - 1 else 0
                o = l * DNH + b
                dve.wait_ge(E["conv_ready"], 3 * o + 3)
                for n in range(2):
                    a = c0 if n else 0
                    dve.wait_ge(E["l2_sum"], 2 * o + n + 1)
                    dve.tensor_scalar(hrs[:, n, a:T], bank[n][:, a:T], EPS, None, ALU.add).then_inc(E["l2_var"], 1)
                dve.wait_ge(E["l2_var"], 2 * o + 2)
                dve.sem_inc(pair_done[0], 1)

            def k_norm(l, b):
                o = l * DNH + b
                dve.wait_ge(E["l2_rstd"], 2 * o + 1)
                dve.tensor_tensor(qkv[:, 1, :], kraw[:, :], hrs[:, 0, :], ALU.mult).then_inc(E["kn_ready"], 1)

            def q_norm(l, b):
                c0 = CTX if l == DEPTH - 1 else 0
                o = l * DNH + b
                dve.wait_ge(E["l2_rstd"], 2 * o + 2)
                stt(out=qkv[:, 0, c0:T], in0=qkv[:, 0, c0:T], scalar=128 ** -0.5, in1=hrs[:, 1, c0:T],
                    op0=ALU.mult, op1=ALU.mult).then_inc(E["qn_ready"], 1)

            def output_and_front(l, b, output, front):
                c0 = CTX if l == DEPTH - 1 else 0
                o, f = l * DNH + b - 1, l * DNH + b

                def decay(d):
                    dve.wait_ge(E["gc_row"], 2 * f + d + 1)
                    for c in range(TC):
                        last = stt(out=DT[:, d, 128 * c:128 * c + 128], in0=bank[4 + d][:, 128 * c:128 * c + 128],
                                   scalar=hb[:, hcol(HB_GC, d, c)], in1=cst[:, C_NM + 128 * d:C_NM + 128 * d + 128],
                                   op0=ALU.subtract, op1=ALU.add)
                    last.then_inc(E["dm_ready"], 1)

                def low_a(d):
                    dve.wait_ge(E["dt_ready"], 2 * f + d + 1)
                    for c in range(TC):
                        s = slice(128 * c, 128 * c + 128)
                        last = stt(out=AT[:, d, s], in0=Gs[:, s], scalar=hb[:, hcol(HB_BETA, d, c)], in1=DT[:, d, s],
                                   op0=ALU.mult, op1=ALU.mult)
                    last.then_inc(E["at_ready"], 1)
                    dve.wait_ge(E["at_ready"], 2 * f + d + 1)
                    steps.do(dve.tensor_tensor(c4d(IT[:, d, :]), c4d(AT[:, d, :]), bc(cst[:, C_LV:C_LV + 128], TC, 128), ALU.mult))
                    steps.sync()
                    dve.tensor_tensor(c4d(XT[:, d, :]), c4d(IT[:, d, :]), bc(ident, TC, 128), ALU.add).then_inc(E["xt0_ready"], 1)

                if front:
                    if output:
                        dve.wait_ge(E["vn_ready"], 8 * o + 8)
                    dve.tensor_copy(hb[:, :], tab[:, ds(b, 1), :].rearrange("p a n -> p (a n)")).then_inc(E["hb_ready"], 1)
                    k_norm(l, b)
                    dve.wait_ge(E["hb_ready"], f + 1)
                    decay(0)
                if output:
                    dve.wait_ge(E["on_sum"], o + 1)
                    dve.tensor_scalar(eo[:, 1, c0:T], bank[7][:, c0:T], 1.0 / 128, EPS, ALU.mult, ALU.add).then_inc(E["on_var"], 1)
                if front:
                    decay(1)
                    q_norm(l, b)
                if output:
                    dve.wait_ge(E["on_rstd"], o + 1)
                    steps.do(stt(out=eo[:, 0, c0:T], in0=bank[6][:, c0:T], scalar=vec[:, l * NVL + V_DNG:l * NVL + V_DNG + 1],
                                 in1=eo[:, 1, c0:T], op0=ALU.mult, op1=ALU.mult))
                    steps.sync()
                    dve.tensor_tensor(gate[:, c0:T], gate[:, c0:T], eo[:, 0, c0:T], ALU.mult).then_inc(E["on_ready"], 1)
                if front:
                    dve.wait_ge(E["gram"], 2 * f + 1)
                    dve.tensor_tensor(c4d(Gs), c4d(bank[7][:, :]), bc(cst[:, C_OFF:C_OFF + 128], TC, 128), ALU.mult).then_inc(E["gs_ready"], 1)
                    dve.wait_ge(E["kv_turned"], 2 * f + 1)
                    dve.tensor_copy(vtok, bank[2][:, :]).then_inc(E["vtok_ready"], 1)
                    dve.wait_ge(E["gs_ready"], f + 1)
                    low_a(0)
                if output:
                    dve.wait_ge(E["bh_ready"], o + 1)
                    dve.tensor_tensor(bl[:, ds(b - 1, 1), c0:T].rearrange("p a t -> p (a t)"), gate[:, c0:T],
                                      bh[:, ds(b - 1, 1), c0:T].rearrange("p a t -> p (a t)").bitcast(f32),
                                      ALU.subtract).then_inc(E["head_ready"], 1)
                if front:
                    low_a(1)

            def head(l, b, follow):
                c0 = CTX if l == DEPTH - 1 else 0
                B = P[("head", l)][0] + b
                o = l * DNH + b - 1
                for v in range(1, 7):
                    mask = bc(cst[:, C_LV + 128 * v:C_LV + 128 * v + 128], TC, 128)
                    for d in range(2):
                        dve.wait_ge(E["p_sum"], 18 * o + 2 * (v - 1) + d + 1)
                        dve.tensor_tensor(c4d(Pm[:, d, :]), c4d(bank[3][:, :]), mask, ALU.mult).then_inc(E["pm_ready"], 1)
                        if v == 1:
                            dve.wait_ge(E["eg_ready"], 2 * o + d + 1)
                            dve.wait_ge(E["qn_ready"], o + 1)
                            dve.tensor_tensor(Qt[:, d, c0:T], qkv[:, 0, c0:T], eg[:, d, c0:T], ALU.mult).then_inc(E["qt_ready"], 1)
                            dve.wait_ge(E["kq_ready"], o + 1)
                            dve.wait_ge(E["xt0_ready"], 4 * o + d + 1)
                            dve.tensor_tensor(IT[:, d, c0:T], KQs[:, c0:T], DT[:, d, c0:T], ALU.mult).then_inc(E["it_ready"], 1)
                        if follow and (v, d) == (1, 1):
                            dve.wait_ge(E["qt_ready"], 2 * o + 2)
                            prep_vec(l, b)
                        if (v, d) == (2, 0):
                            split(B, 3)
                        if follow and (v, d) == (2, 1):
                            prep_conv(l, b, 0)
                        if follow and (v, d) == (3, 1):
                            prep_conv(l, b, 1)
                        if (v, d) == (4, 0):
                            split(B + 1, 0)
                        if (v, d) == (5, 1):
                            split(B + 1, 1)
                if follow:
                    prep_conv(l, b, 2)
                for d in range(2):
                    dve.wait_ge(E["p_sum"], 18 * o + 16 + d + 1)
                    dve.wait_ge(E["it_ready"], 2 * o + d + 1)
                    last = dve.tensor_tensor(XTf[:, d, :], XT[:, d, :].bitcast(f32), bank[4 + d][:, :], ALU.subtract)
                    last.then_inc(E["xt0_ready"], 1)
                if follow:
                    prep_var(l, b)
                for s in range(TC):
                    for d in range(2):
                        c = chunk(d, s)
                        if s:
                            dve.wait_ge(E["ks_sum"], 6 * o + 2 * (s - 1) + d + 1)
                            stt(out=Rr[:, d, :], in0=bank[4 + d][:, 0:128], scalar=hb[:, hcol(HB_NEG, d, c)],
                                in1=vtok[:, 128 * c:128 * c + 128], op0=ALU.mult, op1=ALU.add).then_inc(E["r_ready"], 1)
                    for d in range(2):
                        c = chunk(d, s)
                        dve.wait_ge(E["y_sum"], 8 * o + 2 * s + d + 1)
                        if s < TC - 1:
                            dve.tensor_scalar(vd[:, d, :], bank[4 + d][:, 128:256], hb[:, hcol(HB_KD, d, c)], None,
                                              ALU.mult).then_inc(E["vd_ready"], 1)
                    for d in range(2):
                        c = chunk(d, s)
                        dve.tensor_scalar(vn[:, d, :], bank[4 + d][:, 128:256], hb[:, hcol(HB_BETA, d, c)], None,
                                          ALU.mult).then_inc(E["vn_ready"], 1)
                    if s < TC - 1:
                        for d in range(2):
                            c = chunk(d, s)
                            dve.wait_ge(E["ds_sum"], 6 * o + 2 * s + d + 1)
                            if s == 0:
                                dve.tensor_copy(St[:, 0, d, :], state_bank(d, follow)).then_inc(E["s_ready"], 1)
                            else:
                                dve.wait_ge(E["s_ready"], 6 * o + 2 * (s - 1) + d + 1)
                                stt(out=St[:, s % 2, d, :], in0=St[:, (s - 1) % 2, d, :], scalar=hb[:, hcol(HB_TOT, d, c)],
                                    in1=state_bank(d, follow), op0=ALU.mult, op1=ALU.add).then_inc(E["s_ready"], 1)
                    if s == 1:
                        split(B + 1, 2)
                output_and_front(l, b, True, follow)

            HSTEPS = 6 + 2 + 6 + 1
            def heads(l):
                B0 = P[("head", l)][0]
                dve.wait_ge(panel_done, 4 * B0)
                prep_vec(l, 0)
                for n in range(3):
                    prep_conv(l, 0, n)
                split(B0 + 1, 0)
                split(B0 + 1, 1)
                prep_var(l, 0)
                output_and_front(l, 0, False, True)
                split(B0 + 1, 2)
                with steps.loop(1, DNH - 1, HSTEPS) as b:
                    head(l, b, True)
                head(l, DNH - 1, True)
                head(l, DNH, False)
                split(B0 + DNH + 1, 3)

            def branch(l, r):
                B0, G0 = P[("br", l, r)]
                c0 = CTX if l == DEPTH - 1 else 0
                n0 = (3 * l + r) * 8

                def step(i):
                    for k in range(2):
                        if r == 0 and isinstance(i, int):
                            if k == 0:
                                for j in range(2):
                                    dve.wait_ge(A["a_vturn"], 2 * l + j + 1)
                                    dve.tensor_copy(vt[:, j, :, :].rearrange("p c f -> p (c f)"),
                                                    bank[6 + j][:, :]).then_inc(A["a_vtok"], 1)
                            qk_norm(10 * l + k, l * NVL + V_KG, kT[:, k, :], kT[:, k, :], 0)
                        split(B0 + i + 1, 2 * k)
                        dve.wait_ge(panel_done, 4 * (B0 + i) + 2 * k + 2)
                        dve.wait_ge(C["br_gate"], n0 + 2 * i + k + 1)
                        mt = m3[:, ds(2 * i + k, 1), c0:T].rearrange("p a t -> p (a t)")
                        if r == 0:
                            dve.tensor_tensor(mt, sil[:, k, c0:T], bank[2 * k + 1][:, c0:T], ALU.mult).then_inc(pair_done[k], 1)
                        else:
                            steps.do(dve.tensor_tensor(hbuf[:, k, c0:T], sil[:, k, c0:T], bank[2 * k + 1][:, c0:T], ALU.mult))
                            steps.sync()
                            dve.tensor_tensor(mt, mt, hbuf[:, k, c0:T], ALU.add).then_inc(pair_done[k], 1)
                        split(B0 + i + 1, 2 * k + 1)

                if r == 0:
                    step(0)
                with steps.loop(1 if r == 0 else 0, 4, 0 if r == 0 else 2) as i:
                    step(i)
                for k in range(2):
                    have(dve, pair_done[k], G0 + 4)

            def qk_norm(na, gcol, x, dst, c0):
                dve.wait_ge(A["a_sum"], na + 1)
                dve.tensor_scalar(ars[:, c0:T], bank[4][:, c0:T], 1.0 / HD, EPS, ALU.mult, ALU.add).then_inc(A["a_var"], 1)
                dve.wait_ge(A["a_rstd"], na + 1)
                stt(out=dst[:, c0:T], in0=x[:, c0:T], scalar=vec[:, gcol:gcol + 1], in1=ars[:, c0:T],
                    op0=ALU.mult, op1=ALU.mult).then_inc(A["a_norm"], 1)
                dve.wait_ge(A["a_swap"], na + 1)
                steps.do(dve.tensor_tensor(asw[:, 0:256], bank[5][:, 0:256], cst[:, C_SIN:C_SIN + 256], ALU.mult))
                steps.do(dve.tensor_tensor(asw[:, 256:512], dst[:, CTX:T], cst[:, C_COS:C_COS + 256], ALU.mult))
                steps.sync()
                dve.tensor_tensor(dst[:, CTX:T], asw[:, 0:256], asw[:, 256:512], ALU.add).then_inc(A["a_done"], 1)

            def attention(l):
                c0 = CTX if l == DEPTH - 1 else 0
                L = l * NVL
                na = 10 * l + 2
                nu = att_units_before(l, 0)
                for p in range(2):
                    B, G = P[("q", l)][0] + p, P[("q", l)][1] + p
                    for j in range(4):
                        split(B + 1, j)
                        qk_norm(na, L + V_QG, ax, qx[:, j, :], c0)
                        na += 1
                    dve.wait_ge(A["a_done"], na)
                    units = att_units(l)

                    def scale_p(u):
                        lat = units[u][2]
                        n = 1 if lat else 2
                        dve.wait_ge(A["s_exp"], nu + u + 1)
                        st = 8 * (u % 2)
                        steps.do(dve.reciprocal(stat[:, st + 6:st + 6 + n], stat[:, st + 4:st + 4 + n]))
                        steps.sync()
                        for q in range(n):
                            w = 512 // n
                            last = dve.tensor_scalar(Pb[:, u % 2, q * w:(q + 1) * w], Pb[:, u % 2, q * w:(q + 1) * w],
                                                     stat[:, st + 6 + q:st + 7 + q], None, ALU.mult)
                        last.then_inc(A["s_scaled"], 1)

                    for u, (j, a, lat) in enumerate(units):
                        n = 1 if lat else 2
                        st = 8 * (u % 2)
                        dve.wait_ge(A["s_sum"], nu + u + 1)
                        steps.do(dve.reduce_max(stat[:, st:st + n], bank[4 + u % 2][:, :].rearrange("p (n k) -> p n k", n=n), AX.X))
                        steps.sync()
                        dve.tensor_scalar(stat[:, st + 2:st + 2 + n], stat[:, st:st + n], -HD ** -0.5, None,
                                          ALU.mult).then_inc(A["s_max"], 1)
                        if u:
                            scale_p(u - 1)
                    scale_p(len(units) - 1)
                    nu += len(units)
                    for j in range(4):
                        dve.wait_ge(A["att_hi"], 8 * l + 4 * p + j + 1)
                        last = dve.tensor_tensor(bl[:, 4 * p + j, c0:T], bank[j][:, c0:T], bh[:, 4 * p + j, c0:T].bitcast(f32), ALU.subtract)
                        if j % 2:
                            last.then_inc(pair_done[j // 2], 1)
                        else:
                            last.then_inc(A["att_ready"], 1)

            def conv(l):
                B0, G0 = P[("conv", l)]
                c0 = CTX if l == DEPTH - 1 else 0
                s0 = c0 // CTX
                two = lambda ap: ap.rearrange("p (s t) -> p s t", s=2)[:, s0:2, :]
                for k in (0, 257):
                    steps.do(dve.memset(cpr[:, :, k:k + 1], 0.0))
                steps.sync()
                with steps.loop(0, 2, 4 * 4 - 2) as i:
                    B = B0 + 3 * i
                    n0 = 8 * l + 4 * i
                    dve.tensor_copy(cvec, vec[:, ds(l * NVL + V_CONV + 4 * CV * i, 4 * CV)]).then_inc(C["c_vec"], 1)
                    dve.wait_ge(C["c_vec"], 2 * l + i + 1)
                    for t in range(4):
                        q = 3 * t
                        v = lambda n: cvec[:, t * CV + n:t * CV + n + 1]
                        split(B + q // 4 + 1, q % 4)
                        split(B + (q + 1) // 4 + 1, (q + 1) % 4)
                        dve.wait_ge(C["c_p4"], n0 + t + 1)
                        dve.wait_ge(panel_done, 4 * B + q + 2)
                        ins = stt(out=cpr[:, s0:2, 1:257], in0=two(bank[(q + 1) % 4][:, :]), scalar=v(1), in1=two(c4[:, :]),
                                  op0=ALU.add, op1=ALU.mult)
                        if t in (0, 2):
                            ins.then_inc(pair_done[0 if t == 0 else 1], 1)
                            have(dve, pair_done[0 if t == 0 else 1], (G0 + 3 * i + (0 if t == 0 else 1)) + 1)
                        else:
                            steps.do(ins)
                            steps.sync()
                        y = two(cy[:, :])
                        ins = dve.tensor_scalar(y, cpr[:, s0:2, 0:256], v(3), None, ALU.mult)
                        if t in (1, 3):
                            k = 1 if t == 1 else 0
                            ins.then_inc(pair_done[k], 1)
                            have(dve, pair_done[k], G0 + 3 * i + (1 if t == 1 else 3))
                        else:
                            steps.do(ins)
                            steps.sync()
                        steps.do(stt(out=y, in0=cpr[:, s0:2, 1:257], scalar=v(4), in1=y, op0=ALU.mult, op1=ALU.add))
                        steps.sync()
                        steps.do(stt(out=y, in0=cpr[:, s0:2, 2:258], scalar=v(5), in1=y, op0=ALU.mult, op1=ALU.add))
                        steps.sync()
                        split(B + (q + 2) // 4 + 1, (q + 2) % 4)
                        dve.wait_ge(panel_done, 4 * B + q + 3)
                        z = cz[:, t % 2, :]
                        stt(out=z[:, c0:T], in0=bank[(q + 2) % 4][:, c0:T], scalar=v(2), in1=cy[:, c0:T],
                            op0=ALU.add, op1=ALU.mult).then_inc(C["c_out"], 1)
                        dve.wait_ge(C["c_hi"], n0 + t + 1)
                        ins = dve.tensor_tensor(bl[:, ds(4 * i + t, 1), c0:T].rearrange("p a t -> p (a t)"), z[:, c0:T],
                                                bh[:, ds(4 * i + t, 1), c0:T].rearrange("p a t -> p (a t)").bitcast(f32), ALU.subtract)
                        if t == 1:
                            ins.then_inc(pair_done[0], 1)
                        elif t == 3:
                            ins.then_inc(pair_done[1], 1)
                        else:
                            steps.do(ins)

            def project_out(l):
                B0, G0 = P[("out", l)]
                c0 = CTX if l == DEPTH - 1 else 0
                for t in range(KT):
                    dve.wait_ge(C["mh_ready"], 8 * l + t + 1)
                    dve.tensor_tensor(ul[:, t, c0:T], m3[:, t, c0:T], uh[:, t, c0:T].bitcast(f32), ALU.subtract).then_inc(C["mx_ready"], 1)
                last_residual(B0, G0, c0)
                have(dve, pair_done[0], G0 + 2)
                have(dve, pair_done[1], G0 + 2)

            norm_var(0)
            ada_only(("ada", 0))
            for l in range(DEPTH):
                norm(3 * l, l, 0)
                ffn(l, 0)
                norm_var(3 * l + 1)
                ada_only(("ada1", l))
                norm(3 * l + 1, l, 1)
                ab(l)
                heads(l)
                branch(l, 0)
                attention(l)
                branch(l, 1)
                conv(l)
                branch(l, 2)
                project_out(l)
                norm_var(3 * l + 2)
                norm(3 * l + 2, l, 2)
                ffn(l, 1)
                norm_var(3 * l + 3)
                if l == 0:
                    ada_only(("ada2", 0))
            norm(3 * DEPTH, None, None)

        @block.tensor
        def _(pe):
            mm = pe.matmul

            def panel(B, j, xh, xl, c0, kts=KT, ready=None, lo=0, hi=None):
                hi = 3 * kts if hi is None else hi
                if lo == 0:
                    pe.wait_ge(lo_ready, 4 * B + j + 1)
                w = lambda t, a: a[:, j, 128 * t:128 * t + 128]
                for n in range(lo, hi):
                    t, r = n // 3, n % 3
                    if ready is not None and r == 0:
                        pe.wait_ge(ready[0], ready[1] + t + 1)
                    a, x = ((whi, xh), (whi, xl), (wlo, xh))[r]
                    last = mm(bank[j][:, c0:T], w(t, a), x[:, t, c0:T], start=n == 0, stop=n == 3 * kts - 1)
                if hi == 3 * kts:
                    last.then_inc(panel_done, 1)

            def pair_free(G, j):
                if j % 2 == 0:
                    have(pe, pair_done[j // 2], G)

            def ada_panels(B, g):
                have(pe, ada_row, g)
                for j in range(4):
                    pe.wait_ge(lo_ready, 4 * B + j + 1)
                    for t in range(2):
                        for w in (whi, wlo):
                            last = mm(bank[4][:, :], cstat[:, 2 * j + t, :], w[:, j, 512 * t:512 * t + 512],
                                      start=(j, t) == (0, 0) and w is whi, stop=(j, t) == (3, 1) and w is wlo)
                    last.then_inc(panel_done, 1)

            def ada_turn(g):
                have(pe, ada_row, g + 1)
                have(pe, mod_ready, g)
                for t in range(4):
                    last = mm(bank[5][:, 2 * t:2 * t + 2], arow[:, 128 * t:128 * t + 128], cst[0:4, C_SEL:C_SEL + 2],
                              start=True, stop=True)
                last.then_inc(ada_turned, 1)

            def ada_only(key):
                B0, _ = P[key]
                g0, n = P["groups"][key]
                with pe.Fori(0, n) as i:
                    ada_panels(B0 + i, g0 + i)
                    ada_turn(g0 + i)

            def tile_sum(n, t):
                c0 = norm_conds(n)
                pe.wait_ge(sq_ready, 8 * n + t + 1)
                if t == 0:
                    wait(pe, var_ready, n)
                mm(bank[6][:, c0:T], ones, nsq[:, t % 2, c0:T], start=t == 0, stop=t == KT - 1).then_inc(sq_used, 1)

            def last_products(B0, G0, n, xh, xl, c0, kts=KT, ready=None):
                for i in range(2):
                    for j in range(4):
                        pair_free(G0 + i, j)
                        panel(B0 + i, j, xh, xl, c0, kts=kts, ready=ready if (i, j) == (0, 0) else None)
                        if i or j:
                            tile_sum(n, 4 * i + j - 1)
                tile_sum(n, KT - 1)

            def first_panels(B, G, c0, n):
                pair_free(G, 0)
                for t in range(KT):
                    for j in range(2):
                        panel(B, j, uh, ul, c0, ready=(u_ready, 8 * n) if j == 0 else None, lo=3 * t, hi=3 * t + 3)

            def ffn(l, f, n):
                c0 = CTX if l == DEPTH - 1 and f == 1 else 0
                tile0 = (2 * l + f) * FT
                for p, tiles in enumerate(PIECES):
                    B0, G0 = P[("up", l, f, p)]
                    g0, rides = P[("rides", l, f, p)]
                    per = 2 if rides else 1


                    def step(i, first):
                        B, G = B0 + per * i, G0 + i
                        if rides:
                            ada_panels(B, g0 + i)
                            B = B + 1
                        if first:
                            first_panels(B, G, c0, n)
                            if rides:
                                ada_turn(g0 + i)
                        for j in range(2 if first else 0, 4):
                            pair_free(G, j)
                            panel(B, j, uh, ul, c0)
                            if rides and j == 0:
                                ada_turn(g0 + i)

                    if p == 0:
                        step(0, True)
                    with pe.Fori(1 if p == 0 else 0, tiles // 2) as i:
                        step(i, False)
                    tile0 += tiles
                    B0, G0 = P[("down", l, f, p)]
                    pe.wait_ge(hid_ready, tile0)
                    if p == len(PIECES) - 1:
                        last_products(B0, G0, 3 * l + 1 + 2 * f, bh, bl, c0, kts=tiles)
                        continue
                    with pe.Fori(0, 2) as i:
                        for j in range(4):
                            pair_free(G0 + i, j)
                            panel(B0 + i, j, bh, bl, c0, kts=tiles)

            def ab_products(l):
                pe.wait_ge(wab_lo, l + 1)
                for c in range(TC):
                    s = slice(128 * c, 128 * c + 128)
                    for t in range(KT):
                        for r, (x, w) in enumerate(((uh, wabh), (ul, wabh), (uh, wabl))):
                            last = mm(bank[7][:, 32 * c:32 * c + 32], x[:, t, s], w[:, 32 * t:32 * t + 32],
                                      start=t == 0 and r == 0, stop=t == KT - 1 and r == 2)
                last.then_inc(ab_sum, 1)

            def ab_sums(l):
                pe.wait_ge(g_ready, l + 1)
                g = SM[:, 384:448].rearrange("p (c n) -> p c n", c=TC)
                for c in range(TC):
                    for d in range(2):
                        mm(bank[7][:, 128 + 16 * c + 8 * d:136 + 16 * c + 8 * d], cst[:, C_CUM + 128 * d:C_CUM + 128 * d + 128],
                           g[:, c, 8 * d:8 * d + 8], start=True, stop=True)
                    last = mm(bank[7][:, 192 + 16 * c:208 + 16 * c], ones, g[:, c, :], start=True, stop=True)
                last.then_inc(gc_sum, 1)

            def projections(l, b, issued, follow):
                B0, G0 = P[("head", l)]
                c0 = CTX if l == DEPTH - 1 else 0
                B, G = B0 + b, G0 + b
                at_ = [issued]

                def project(n):
                    while n:
                        k_, at = at_[0] // 24, at_[0] % 24
                        k = min(n, 24 - at)
                        j, nxt = k_ % 4, k_ // 4
                        if at == 0:
                            pair_free(G + nxt, j)
                        all_tokens = j in (1, 2) or (not follow if nxt == 0 else isinstance(b, int) and b == DNH - 1)
                        panel(B + nxt, j, uh, ul, 0 if all_tokens else c0, lo=at, hi=at + k)
                        at_[0] += k
                        n -= k

                return project

            def output_and_front(l, b, output, front, project):
                c0 = CTX if l == DEPTH - 1 else 0
                cs = [c for c in range(TC) if 128 * c >= c0]
                sl = lambda c: slice(128 * c, 128 * c + 128)
                o, f = l * DNH + b - 1, l * DNH + b
                if front:
                    pe.wait_ge(E["silu_ready"], 3 * f + 3)
                    for c in range(TC):
                        last = pe.transpose(bank[2][:, sl(c)], qkv[:, 2, sl(c)], ident)
                    last.then_inc(E["kv_turned"], 1)
                    pe.wait_ge(E["hb_ready"], f + 1)
                    for d in range(2):
                        for c in range(TC):
                            last = mm(bank[4 + d][:, sl(c)], hb[:, hcol(HB_G, d, c)].broadcast_to([128, 128]),
                                      cst[:, C_CUM + 128 * d:C_CUM + 128 * d + 128], start=True, stop=True)
                        last.then_inc(E["gc_row"], 1)
                if output:
                    pe.wait_ge(E["osq_ready"], o + 1)
                    mm(bank[7][:, c0:T], ones, eo[:, 0, c0:T], start=True, stop=True).then_inc(E["on_sum"], 1)
                if not front:
                    return
                pe.wait_ge(E["kn_ready"], f + 1)
                for c in range(TC):
                    last = pe.transpose(bank[1][:, sl(c)], qkv[:, 1, sl(c)], ident)
                last.then_inc(E["kv_turned"], 1)
                project(6)
                if output:
                    pe.wait_ge(E["on_var"], o + 1)
                for c in range(TC):
                    last = mm(bank[7][:, sl(c)], qkv[:, 1, sl(c)], qkv[:, 1, sl(c)], start=True, stop=True)
                last.then_inc(E["gram"], 1)
                project(18)
                pe.wait_ge(E["vtok_ready"], f + 1)
                pe.wait_ge(E["qn_ready"], f + 1)
                for c in cs:
                    last = mm(bank[2][:, sl(c)], qkv[:, 1, sl(c)], qkv[:, 0, sl(c)], start=True, stop=True)
                last.then_inc(E["gram"], 1)
                pe.wait_ge(E["ktok_ready"], f + 1)
                project(8)
                for d in range(2):
                    pe.wait_ge(E["xt0_ready"], 4 * f + d + 1)
                    if d == 0 and output:
                        pe.wait_ge(E["on_ready"], o + 1)
                    if d == 1:
                        pe.wait_ge(E["gs_ready"], f + 1)
                    for c in range(TC):
                        mm(bank[6 + d][:, sl(c)], XT[:, d, sl(c)], idr[:, :], start=c == 0, stop=False, skip_group_check=True)
                    pe.wait_ge(E["eg_ready"], 2 * f + d + 1)
                    mm(bank[4 + d][:, :], idr[:, :], XT[:, d, :], start=True, stop=False,
                       skip_group_check=True).then_inc(E["xt0_turned"], 1)
                    project(8)

            def head(l, b, follow):
                B0, G0 = P[("head", l)]
                c0 = CTX if l == DEPTH - 1 else 0
                project = projections(l, b, 48, follow)
                o = l * DNH + b - 1
                cs = [c for c in range(TC) if 128 * c >= c0]
                sl = lambda c: slice(128 * c, 128 * c + 128)

                def product(v, d):
                    if v == 1:
                        pe.wait_ge(E["atr_ready"], 2 * o + d + 1)
                    pe.wait_ge(E["x_ready"], 14 * o + 2 * (v - 1) + d + 1)
                    if (v, d) != (1, 0):
                        pe.wait_ge(E["pm_ready"], 14 * o + 2 * (v - 1) + d)
                    for c in range(TC):
                        last = mm(bank[3][:, sl(c)], ATr[:, d, sl(c)], X[:, d, sl(c)], start=True, stop=True)
                    last.then_inc(E["p_sum"], 1)

                def add(v, d):
                    pe.wait_ge(E["pm_ready"], 14 * o + 2 * (v - 1) + d + 1)
                    if v > 1:
                        pe.wait_ge(E["xt_ready"], 12 * o + 2 * (v - 2) + d + 1)
                    for c in range(TC):
                        last = mm(bank[6 + d][:, sl(c)], XT[:, d, sl(c)], Pm[:, d, sl(c)], start=False, stop=False, skip_group_check=True)
                    last.then_inc(E["x_sum"], 1)
                    if v < 6:
                        for c in range(TC):
                            last = mm(bank[4 + d][:, sl(c)], Pm[:, d, sl(c)], XT[:, d, sl(c)], start=False, stop=False, skip_group_check=True)
                        last.then_inc(E["x_sum"], 1)

                pair_free(G0 + b, 2)
                pe.wait_ge(E["kq_ready"], o + 1)
                product(1, 0)
                for v in range(1, 7):
                    fill = 3 if v < 5 else 0
                    add(v, 0)
                    product(v, 1)
                    project(fill)
                    if v < 6:
                        product(v + 1, 0)
                    project(fill)
                    add(v, 1)
                    if follow and v in (5, 6):
                        square_sum(l, b, v - 5)
                for d in range(2):
                    pe.wait_ge(E["x_ready"], 14 * o + 12 + d + 1)
                    for c in range(TC):
                        last = pe.transpose(bank[4 + d][:, sl(c)], X[:, d, sl(c)].bitcast(f32), ident)
                    last.then_inc(E["p_sum"], 1)
                    mm(bank[6 + d][:, :], idr[:, :], X[:, d, :], start=True, stop=False, skip_group_check=True)
                    mm(bank[6 + d][:, :], nidr[:, :], bc(idr[:, :], TC, 128), start=False, stop=False, skip_group_check=True)
                    for c in range(TC):
                        last = mm(bank[6 + d][:, sl(c)], AT[:, d, sl(c)], X[:, d, sl(c)].bitcast(f32), start=False, stop=False,
                                  skip_group_check=True)
                    last.then_inc(E["p_sum"], 1)
                project(2)
                for d in range(2):
                    pe.wait_ge(E["xt_ready"], 12 * o + 10 + d + 1)
                    pe.wait_ge(E["pm_ready"], 14 * o + 12 + d + 1)
                    for c in range(TC):
                        last = mm(bank[4 + d][:, sl(c)], Pm[:, d, sl(c)], XT[:, d, sl(c)], start=True, stop=True)
                    last.then_inc(E["p_sum"], 1)
                project(4)
                first = [True]
                for s in range(TC):
                    if s:
                        for d in range(2):
                            c = chunk(d, s)
                            pe.wait_ge(E["s_ready"], 6 * o + 2 * (s - 1) + d + 1)
                            mm(bank[4 + d][:, 0:128], qkv[:, 1, sl(c)], St[:, (s - 1) % 2, d, :], start=True, stop=True).then_inc(E["ks_sum"], 1)
                        project(1)
                    for d in range(2):
                        c = chunk(d, s)
                        if s == 0:
                            pe.wait_ge(E["xt0_ready"], 4 * o + 2 + d + 1)
                            r = vtok[:, sl(c)]
                        else:
                            pe.wait_ge(E["r_ready"], 6 * o + 2 * (s - 1) + d + 1)
                            r = Rr[:, d, :]
                        mm(bank[4 + d][:, 128:256], XTf[:, d, sl(c)], r, start=True, stop=True).then_inc(E["y_sum"], 1)
                    project(2)
                    for d in range(2):
                        c = chunk(d, s)
                        if s < TC - 1:
                            pe.wait_ge(E["vd_ready"], 6 * o + 2 * s + d + 1)
                            if not follow and d == 1:
                                pe.wait_ge(E["vn_ready"], 8 * o + 2 * s + d + 1)
                            mm(state_bank(d, follow), ktok[:, sl(c)], vd[:, d, :], start=True, stop=True).then_inc(E["ds_sum"], 1)
                    for d in range(2):
                        c = chunk(d, s)
                        pe.wait_ge(E["vn_ready"], 8 * o + 2 * s + d + 1)
                        if first[0]:
                            pe.wait_ge(E["qt_ready"], 2 * o + 2)
                            pe.wait_ge(E["it_ready"], 2 * o + 2)
                        if c not in cs:
                            continue
                        if s:
                            mm(bank[6][:, sl(c)], St[:, (s - 1) % 2, d, :], Qt[:, d, sl(c)], start=first[0], stop=False, skip_group_check=True)
                            first[0] = False
                        last = mm(bank[6][:, sl(c)], vn[:, d, :], IT[:, d, sl(c)], start=first[0],
                                  stop=False, skip_group_check=True)
                        first[0] = False
                    project(1)
                last.then_inc(E["o_sum"], 1)
                project(3)
                output_and_front(l, b, True, follow, project)

            def square_sum(l, b, n):
                a = (CTX if l == DEPTH - 1 else 0) if n else 0
                pe.wait_ge(E["hsq_ready"], 2 * (l * DNH + b) + n + 1)
                mm(bank[n][:, a:T], ones, hsq[:, n, a:T], start=True, stop=True).then_inc(E["l2_sum"], 1)

            def heads(l, n):
                B0, G0 = P[("head", l)]
                c0 = CTX if l == DEPTH - 1 else 0
                pair_free(G0, 0)
                for t in range(KT):
                    for j in range(2):
                        panel(B0, j, uh, ul, c0 if j == 0 else 0, ready=(u_ready, 8 * n) if j == 0 else None,
                              lo=3 * t, hi=3 * t + 3)
                ab_products(l)
                for j in range(2, 4):
                    pair_free(G0, j)
                    panel(B0, j, uh, ul, c0 if j == 3 else 0)
                    if j == 2:
                        ab_sums(l)
                for n in range(2):
                    square_sum(l, 0, n)
                output_and_front(l, 0, False, True, projections(l, 0, 96, True))
                with pe.Fori(1, DNH - 1) as b:
                    head(l, b, True)
                head(l, DNH - 1, True)
                head(l, DNH, False)

            def branch(l, r, ready):
                B0, G0 = P[("br", l, r)]
                c0 = CTX if l == DEPTH - 1 else 0
                for s, n in ready:
                    have(pe, s, n)
                if r == 0:
                    for j in range(4):
                        pair_free(G0, j)
                        panel(B0, j, *((uh, ul) if j % 2 == 0 else (bh, bl)), c0)
                        if j == 0:
                            v_turn(l)
                        if j % 2 == 0:
                            qk_sum(10 * l + j // 2, 0)
                        else:
                            qk_swap(10 * l + j // 2, kT[:, j // 2, :])
                with pe.Fori(1 if r == 0 else 0, 4) as i:
                    for j in range(4):
                        pair_free(G0 + i, j)
                        panel(B0 + i, j, *((uh, ul) if j % 2 == 0 else (bh, bl)), c0)

            def qk_sum(na, c0):
                pe.wait_ge(A["a_sq"], na + 1)
                mm(bank[4][:, c0:T], cst[:, C_BLK:C_BLK + 128], asq[:, c0:T], start=True, stop=True).then_inc(A["a_sum"], 1)

            def qk_swap(na, dst):
                pe.wait_ge(A["a_norm"], na + 1)
                mm(bank[5][:, 0:256], cst[:, C_PERM:C_PERM + 128], dst[:, CTX:T], start=True, stop=True).then_inc(A["a_swap"], 1)

            def v_turn(l):
                for j in range(2):
                    pe.wait_ge(A["a_vx"], 2 * l + j + 1)
                    for c in range(TC):
                        last = pe.transpose(bank[6 + j][:, 128 * c:128 * c + 128], qx[:, j, 128 * c:128 * c + 128], ident)
                    last.then_inc(A["a_vturn"], 1)

            def attention(l):
                c0 = CTX if l == DEPTH - 1 else 0
                pe.wait_ge(A["a_vtok"], 2 * l + 2)
                na = 10 * l + 2
                nu = att_units_before(l, 0)
                for p in range(2):
                    B, G = P[("q", l)][0] + p, P[("q", l)][1] + p
                    for j in range(5):
                        if j < 4:
                            pair_free(G, j)
                            panel(B, j, uh, ul, c0, hi=12)
                        if j:
                            qk_sum(na, c0)
                        if j < 4:
                            panel(B, j, uh, ul, c0, lo=12)
                        if j:
                            qk_swap(na, qx[:, j - 1, :])
                            na += 1
                    pe.wait_ge(A["a_done"], na)
                    units = att_units(l)

                    def turn(u):
                        pe.wait_ge(A["s_scaled"], nu + u + 1)
                        for k in range(4):
                            last = pe.transpose(bank[6 + u % 2][:, 128 * k:128 * k + 128], Pb[:, u % 2, 128 * k:128 * k + 128], ident)
                        last.then_inc(A["s_turned"], 1)

                    def pv(u):
                        j, a, kind = units[u]
                        pe.wait_ge(A["s_pt"], nu + u + 1)
                        rows_ = slice(64 * a, 64 * a + 64)
                        v = lambda kt: vt[:, p, kt, 64 * a:64 * a + 64]
                        pt = lambda k: PT[:, u % 2, 128 * k:128 * k + 128]
                        if kind:
                            for kt in range(4):
                                last = mm(bank[j][rows_, 128 * kind:128 * kind + 128], v(kt), pt(kt), start=kt == 0, stop=kt == 3)
                        else:
                            for q in range(2):
                                for kt in range(2):
                                    last = mm(bank[j][rows_, 128 * q:128 * q + 128], v(kt), pt(2 * q + kt), start=kt == 0, stop=kt == 1)
                        last.then_inc(A["s_pv"], 1)

                    def scores(u):
                        j, a, kind = units[u]
                        if u >= 2:
                            pe.wait_ge(A["s_exp"], nu + u - 1)
                        r = slice(64 * a, 64 * a + 64)
                        if kind:
                            last = mm(bank[4 + u % 2][:, :], qx[r, j, 128 * kind:128 * kind + 128], kT[r, p, :], start=True, stop=True)
                        else:
                            for q in range(2):
                                last = mm(bank[4 + u % 2][:, 256 * q:256 * q + 256], qx[r, j, 128 * q:128 * q + 128], kT[r, p, 0:CTX],
                                          start=True, stop=True)
                        last.then_inc(A["s_sum"], 1)

                    n = len(units)
                    scores(0)
                    for u in range(n + 2):
                        if u + 1 < n:
                            scores(u + 1)
                        if u >= 2:
                            pv(u - 2)
                        if 1 <= u <= n:
                            turn(u - 1)
                    nu += n

            def conv(l):
                B0, G0 = P[("conv", l)]
                c0 = CTX if l == DEPTH - 1 else 0
                with pe.Fori(0, 2) as i:
                    for q in range(12):
                        pair_free(G0 + 3 * i + q // 4, q % 4)
                        panel(B0 + 3 * i + q // 4, q % 4, uh, ul, c0)

            def project_out(l):
                B0, G0 = P[("out", l)]
                c0 = CTX if l == DEPTH - 1 else 0
                last_products(B0, G0, 3 * l + 2, uh, ul, c0, ready=(C["mx_ready"], 8 * l))

            pe.sem_inc(ada_turned, 1)
            pe.wait_ge(setup_act, 2)
            pe.wait_ge(setup_dve, 2)
            pe.wait_ge(consts_loaded, 16)
            for t in range(KT):
                tile_sum(0, t)
            ada_only(("ada", 0))
            for l in range(DEPTH):
                ffn(l, 0, 3 * l)
                ada_only(("ada1", l))
                heads(l, 3 * l + 1)
                branch(l, 0, [(pair_done[1], P[("kv", l)][1] + 1)])
                attention(l)
                branch(l, 1, [(pair_done[0], P[("q", l)][1] + 2), (pair_done[1], P[("q", l)][1] + 2)])
                conv(l)
                branch(l, 2, [(pair_done[1], P[("conv", l)][1] + 6)])
                project_out(l)
                ffn(l, 1, 3 * l + 2)
                if l == 0:
                    ada_only(("ada2", 0))


def _tables():
    c = np.zeros((128, NC), np.float32)
    i = np.arange(128)
    c[:, C_ID:C_ID + 128] = np.eye(128)
    c[:, C_OFF:C_OFF + 128] = 1 - np.eye(128)
    c[:, C_ONE:C_ONE + 128] = 1
    c[:, C_BLK:C_BLK + 128] = (i[:, None] // 64) == (i[None, :] // 64)
    c[:, C_PERM:C_PERM + 128] = (i[:, None] ^ 32) == i[None, :]
    for v in range(7):
        s = 1 << v
        c[:, C_LV + 128 * v:C_LV + 128 * v + 128] = -1.0 * (
            (i[:, None] // (2 * s) == i[None, :] // (2 * s)) & (i[:, None] // s != i[None, :] // s))
    for d in range(2):
        ok = (i[None, :] >= i[:, None]) if d == 0 else (i[None, :] <= i[:, None])
        c[:, C_NM + 128 * d:C_NM + 128 * d + 128] = np.where(ok, 0.0, NEG)
        c[:, C_CUM + 128 * d:C_CUM + 128 * d + 128] = ok
    GW = 64
    t = np.arange(SEQ)
    inv = (10000.0 ** (-np.arange(16, dtype=np.float32) / 16)).astype(np.float32)
    ang = np.concatenate([(t // GW).astype(np.float32)[:, None] * inv, (t % GW).astype(np.float32)[:, None] * inv], 1)
    cos, sin = np.cos(ang).T, np.sin(ang).T
    c[:, C_COS:C_COS + 256] = np.tile(cos, (4, 1))
    c[:, C_SIN:C_SIN + 256] = np.tile(np.concatenate([-sin, sin]), (2, 1))
    c[0, C_SEL] = c[2, C_SEL] = c[1, C_SEL + 1] = c[3, C_SEL + 1] = 1
    return c


def _q_order():
    heads = [(2 * p + a) * 4 + i for p in range(2) for i in range(4) for a in range(2)]
    return np.concatenate([np.arange(64 * x, 64 * x + 64) for x in heads])


def _panels(w):
    k, mm = w.shape
    p = w.reshape(k // 128, 128, mm // 128, 128).transpose(2, 1, 0, 3)
    if k < 1024:
        p = np.concatenate([p, np.zeros((p.shape[0], 128, 8 - k // 128, 128), np.float32)], 2)
    return p.reshape(-1, 128, 1024)


def _stream(w_ada, ffn_w1, ffn_w3, ffn_w2, w_in, w_br, w_out):
    P = plan()
    s = np.zeros((4 * P["blocks"], 128, 1024), np.float32)

    def put(key, panels):
        b = P[key][0]
        s[4 * b:4 * b + len(panels)] = panels

    def ada(g):
        l, n = g // ADA_GROUPS, g % ADA_GROUPS
        w = w_ada[l][:, 512 * n:512 * n + 512]
        return w.reshape(4, 2, 128, 512).transpose(0, 2, 1, 3).reshape(4, 128, 1024)

    def ada_run(key, n):
        b, (g0, _) = P[key][0], P["groups"][key]
        for i in range(n):
            s[4 * (b + i):4 * (b + i) + 4] = ada(g0 + i)

    qo = _q_order()
    for l in range(DEPTH):
        wi = w_in[l]
        if l == 0:
            ada_run(("ada", 0), 6)
        for f in range(2):
            at = 0
            for p, tiles in enumerate(PIECES):
                b = P[("up", l, f, p)][0]
                g0, rides = P[("rides", l, f, p)]
                cols = slice(128 * at, 128 * (at + tiles))
                w1, w3 = _panels(ffn_w1[l, f][:, cols]), _panels(ffn_w3[l, f][:, cols])
                for i in range(tiles // 2):
                    if rides:
                        s[4 * b:4 * b + 4] = ada(g0 + i)
                        b += 1
                    for k in range(2):
                        s[4 * b + 2 * k], s[4 * b + 2 * k + 1] = w1[2 * i + k], w3[2 * i + k]
                    b += 1
                put(("down", l, f, p), _panels(ffn_w2[l, f][cols]))
                at += tiles
            if f == 0:
                ada_run(("ada1", l), 1)
                parts = [_panels(wi[:, o:o + 1024]) for o in (ODN, ODN + 1024, ODN + 2048, OG)]
                put(("head", l), np.stack(parts, 1).reshape(-1, 128, 1024))
                for r, br in enumerate((2, 0, 1)):
                    wb = w_br[l, br]
                    if br == 0:
                        wb = wb[qo]
                    pr = np.stack([_panels(wi[:, OGZ + 1024 * br:OGZ + 1024 * br + 1024]), _panels(wb)], 1)
                    put(("br", l, r), pr.reshape(-1, 128, 1024))
                put(("kv", l), _panels(wi[:, OK:OK + 512]))
                put(("q", l), _panels(wi[:, OQ:OQ + 1024][:, qo]))
                parts = [_panels(wi[:, o:o + 1024]) for o in (O4, O5, O3)]
                put(("conv", l), np.stack(parts, 1).reshape(-1, 128, 1024))
                put(("out", l), _panels(w_out[l]))
            elif l == 0:
                ada_run(("ada2", 0), 2)
    return s


def _fm(v):
    return v.reshape(-1, 128).T


def _vectors(c, c_ctx, b_ada, norm_g, b_in, q_norm_g, k_norm_g, sc_conv, dn_conv, dn_norm_g, final_norm_g):
    v = np.zeros((128, NV), np.float32)
    for l in range(DEPTH):
        L, b = l * NVL, b_in[l]

        def put(at, x):
            v[:, L + at:L + at + x.shape[1]] = x

        put(V_KV, _fm(b[OK:OK + 512]))
        put(V_Q, _fm(b[OQ:OQ + 1024][_q_order()]))
        put(V_QG, np.concatenate([q_norm_g[l], q_norm_g[l]])[:, None])
        put(V_KG, np.concatenate([k_norm_g[l], k_norm_g[l]])[:, None])
        for n in range(DNH):
            at = V_HEAD + HV * n
            for j, o in enumerate((ODN, ODN + 1024, ODN + 2048, OG)):
                put(at + j, b[o + 128 * n:o + 128 * n + 128][:, None])
            for j in range(3):
                put(at + 4 + 3 * j, dn_conv[l][:, 1024 * j + 128 * n:1024 * j + 128 * n + 128].T)
        for n in range(KT):
            at = V_CONV + CV * n
            for j, o in enumerate((O4, O5, O3)):
                put(at + j, b[o + 128 * n:o + 128 * n + 128][:, None])
            put(at + 3, sc_conv[l][:, 128 * n:128 * n + 128].T)
        for r, br in enumerate((2, 0, 1)):
            put(V_GZ + 8 * r, _fm(b[OGZ + 1024 * br:OGZ + 1024 * br + 1024]))
        put(V_NG, _fm(norm_g[l].reshape(-1)))
        put(V_DNG, dn_norm_g[l][:, None])
        put(V_ADA, _fm(b_ada[l]))
    v[:, V_FG:V_FG + KT] = _fm(final_norm_g)
    v[:, V_C:V_C + 2 * KT:2] = _fm(c_ctx)
    v[:, V_C + 1:V_C + 2 * KT:2] = _fm(c[0])
    return v


def _rows(b_in, dn_dt_bias, dn_a_log):
    r = np.zeros((DEPTH, NR), np.float32)
    for l in range(DEPTH):
        r[l, R_AB:R_AB + 32] = b_in[l, OAB:OAB + 32]
        r[l, R_DT:R_DT + 16] = dn_dt_bias[l].reshape(-1)
        r[l, R_AL:R_AL + 16] = dn_a_log[l].reshape(-1)
    return np.ascontiguousarray(np.broadcast_to(r.reshape(1, -1), (128, DEPTH * NR)))


def kernel(**inputs):
    import concourse.bacc as bacc
    from concourse.bass_utils import run_bass_kernel_spmd

    a = {k: np.asarray(v) for k, v in inputs.items()}
    arrays = {
        "stream": _stream(*(a[k] for k in ("w_ada", "ffn_w1", "ffn_w3", "ffn_w2", "w_in", "w_br", "w_out"))),
        "h_in": np.ascontiguousarray(np.concatenate([a["ctx"][0], a["x"][0]]).T),
        "vecs": _vectors(*(a[k] for k in ("c", "c_ctx", "b_ada", "norm_g", "b_in", "q_norm_g", "k_norm_g", "sc_conv",
                                          "dn_conv", "dn_norm_g", "final_norm_g"))),
        "rows": _rows(a["b_in"], a["dn_dt_bias"], a["dn_a_log"]),
        "wab": np.ascontiguousarray(a["w_in"][:, :, OAB:OAB + 32].reshape(DEPTH, KT, 128, 32).transpose(2, 0, 1, 3)).reshape(128, -1),
        "consts": _tables(),
    }
    nc = bacc.Bacc("TRN2", target_bir_lowering=False, num_devices=1)
    aps = [nc.dram_tensor(k, v.shape, mybir.dt.float32, kind="ExternalInput").ap() for k, v in arrays.items()]
    out = nc.dram_tensor("out", (D, SEQ), mybir.dt.float32, kind="ExternalOutput").ap()
    build(nc, *aps, out)
    r = run_bass_kernel_spmd(nc, [arrays], core_ids=[0])
    return np.ascontiguousarray(np.asarray(r.results[0]["out"]).T)[None]
```
